# Optimizing a Trainium2 kernel written in Bass

```python
import jax, jax.numpy as jnp
from jax import lax
import numpy as np
import math
import jax
import jax.numpy as jnp

D_MODEL = 1024
BATCH = 1
SEQ = 1024
DEPTH = 1

CTX_LEN = 256
GRID_W = 64
D_F = D_MODEL // 2
N_FG = 4
FG = D_F // N_FG
D_M = D_MODEL // 2
N_H = 4
DH = D_M // N_H
CHUNK = 64
CONV_K = 3
N_GATE_KINDS = 4
FORGET_BIAS_LO = 3.0
FORGET_BIAS_HI = 6.0
N_BRANCH = 2
N_EXPERTS = 16
CAP_FACTOR = 2
D_FF_E = D_MODEL
EPS = 1e-6
OFF_F = 0
OFF_QK = OFF_F + D_F
OFF_V = OFF_QK + 2 * D_M
OFF_O = OFF_V + D_M
OFF_G = OFF_O + D_M
OFF_BR = OFF_G + N_GATE_KINDS * N_H
IN_COLS = OFF_BR + N_BRANCH * D_MODEL


def rmsnorm(x, g):
    xf = x.astype(jnp.float32)
    y = xf * lax.rsqrt(jnp.mean(xf * xf, axis=-1, keepdims=True) + EPS)
    return (y * g.astype(jnp.float32)).astype(x.dtype)

def modulate(h, shift, scale):
    return h * (1 + scale) + shift

def grid_conv(u, w, rows):
    b, l, ch = u.shape
    ug = u.reshape(b, rows, l // rows, ch)
    out = lax.conv_general_dilated(ug, w[:, :, None, :].astype(u.dtype), (1, 1), 'SAME',
                                   dimension_numbers=('NHWC', 'HWIO', 'NHWC'),
                                   feature_group_count=ch)
    return out.reshape(b, l, ch)

def mlstm_inputs(p, rows, w_conv, b_gates):
    b, l, _ = p.shape
    qk = jax.nn.silu(grid_conv(p[..., OFF_QK:OFF_V], w_conv, rows))
    to_heads = lambda a: a.reshape(b, l, N_H, DH).transpose(0, 2, 1, 3).astype(jnp.float32)
    q = to_heads(qk[..., :D_M])
    k = to_heads(qk[..., D_M:]) * (DH ** -0.5)
    v = to_heads(p[..., OFF_V:OFF_O])
    g = (p[..., OFF_G:OFF_BR].astype(jnp.float32).reshape(b, l, N_GATE_KINDS, N_H).transpose(2, 0, 3, 1)
         + b_gates.astype(jnp.float32)[:, None, :, None])
    return q, k, v, g

def zero_state(b):
    return (jnp.zeros((b, N_H, DH, DH), jnp.float32), jnp.zeros((b, N_H, DH), jnp.float32),
            jnp.zeros((b, N_H), jnp.float32))

def mlstm_scan(q, k, v, ig, fl, state):
    b, h, l, dh = q.shape
    nc = l // CHUNK

    def chunks(a):
        return jnp.moveaxis(a.reshape((b, h, nc, CHUNK) + a.shape[3:]), 2, 0)

    tril = jnp.tril(jnp.ones((CHUNK, CHUNK), dtype=bool))

    def step(carry, inp):
        c0, n0, m0 = carry
        qc, kc, vc, ic, fc = inp
        cum = jnp.cumsum(fc, axis=-1)
        logw = jnp.where(tril, cum[..., :, None] - cum[..., None, :] + ic[..., None, :], -jnp.inf)
        inter = cum + m0[..., None]
        m = jnp.maximum(inter, logw.max(-1))
        s = jnp.einsum('bhjd,bhsd->bhjs', qc, kc) * jnp.exp(logw - m[..., None])
        dec = jnp.exp(inter - m)
        num = jnp.einsum('bhjs,bhsd->bhjd', s, vc) + dec[..., None] * jnp.einsum('bhjk,bhkv->bhjv', qc, c0)
        den = s.sum(-1) + dec * jnp.einsum('bhjk,bhk->bhj', qc, n0)
        hc = num / jnp.maximum(jnp.abs(den), jnp.exp(-m))[..., None]
        tot = cum[..., -1]
        a = tot[..., None] - cum + ic
        m_new = jnp.maximum(tot + m0, a.max(-1))
        wa = jnp.exp(a - m_new[..., None])
        dn = jnp.exp(tot + m0 - m_new)
        c_new = dn[..., None, None] * c0 + jnp.einsum('bhs,bhsk,bhsv->bhkv', wa, kc, vc)
        n_new = dn[..., None] * n0 + jnp.einsum('bhs,bhsk->bhk', wa, kc)
        return (c_new, n_new, m_new), hc

    final, hs = lax.scan(step, state, (chunks(q), chunks(k), chunks(v), chunks(ig), chunks(fl)))
    return jnp.moveaxis(hs, 0, 2).reshape(b, h, l, dh), final

def bidir_mlstm(q, k, v, g, init):
    flip = lambda a: jnp.flip(a, axis=2)
    h_f, s_f = mlstm_scan(q, k, v, g[0], jax.nn.log_sigmoid(g[1]), init[0])
    h_b, s_b = mlstm_scan(flip(q), flip(k), flip(v), flip(g[2]), flip(jax.nn.log_sigmoid(g[3])), init[1])
    return h_f + flip(h_b), (s_f, s_b)

def branch_merge(p, h_m, w_fourier, w_mlstm, w_out):
    b, l, _ = p.shape
    u = p[..., OFF_F:OFF_QK].astype(jnp.float32).reshape(b, l, N_FG, FG)
    fu = jnp.fft.fft2(u, axes=(1, 3), norm='ortho').real.astype(p.dtype).reshape(b, l, D_F)
    y_f = fu @ w_fourier
    hm = h_m.transpose(0, 2, 1, 3).reshape(b, l, D_M).astype(p.dtype)
    y_m = (jax.nn.sigmoid(p[..., OFF_O:OFF_G]) * hm) @ w_mlstm
    gates = jax.nn.sigmoid(p[..., OFF_BR:])
    merged = gates[..., :D_MODEL] * y_f + gates[..., D_MODEL:] * y_m
    return merged @ w_out

def expert_choice(h, w_router, w_gate, w_up, w_down):
    b, l, _ = h.shape
    cap = CAP_FACTOR * l // N_EXPERTS
    aff = jax.nn.softmax(jnp.einsum('bld,de->ble', h, w_router).astype(jnp.float32), axis=-1)
    vals, idx = lax.top_k(jnp.swapaxes(aff, 1, 2), cap)
    bidx = jnp.arange(b)[:, None, None]
    xs = h[bidx, idx]
    hid = jax.nn.silu(jnp.einsum('becd,edf->becf', xs, w_gate)) * jnp.einsum('becd,edf->becf', xs, w_up)
    y = jnp.einsum('becf,efd->becd', hid, w_down) * vals[..., None].astype(h.dtype)
    return jnp.zeros_like(h).at[bidx, idx].add(y)

def first_inputs(seed: int = 0) -> dict:
    key = jax.random.key(seed)
    ks = jax.random.split(key, 20)
    nrm = jax.random.normal
    forget = jnp.linspace(FORGET_BIAS_LO, FORGET_BIAS_HI, N_H)
    zeros_h = jnp.zeros((N_H,))
    gate_base = jnp.stack([zeros_h, forget, zeros_h, forget])
    return {
        'x': nrm(ks[0], (BATCH, SEQ, D_MODEL), jnp.float32),
        'c': nrm(ks[1], (BATCH, D_MODEL), jnp.float32),
        'ctx': nrm(ks[2], (BATCH, CTX_LEN, D_MODEL), jnp.float32),
        'c_ctx': nrm(ks[3], (D_MODEL,), jnp.float32),
        'w_ada': nrm(ks[4], (DEPTH, D_MODEL, 6 * D_MODEL), jnp.float32) * (0.5 * D_MODEL ** -0.5),
        'b_ada': nrm(ks[5], (DEPTH, 6 * D_MODEL), jnp.float32) * 0.02,
        'g_norm1': 1.0 + 0.02 * nrm(ks[6], (DEPTH, D_MODEL), jnp.float32),
        'w_in': nrm(ks[7], (DEPTH, D_MODEL, IN_COLS), jnp.float32) * D_MODEL ** -0.5,
        'b_gates': gate_base[None] + 0.1 * nrm(ks[8], (DEPTH, N_GATE_KINDS, N_H), jnp.float32),
        'w_conv': nrm(ks[9], (DEPTH, CONV_K, CONV_K, 2 * D_M), jnp.float32) * (1.0 / CONV_K),
        'w_fourier': nrm(ks[10], (DEPTH, D_F, D_MODEL), jnp.float32) * D_F ** -0.5,
        'w_mlstm': nrm(ks[11], (DEPTH, D_M, D_MODEL), jnp.float32) * D_M ** -0.5,
        'w_out': nrm(ks[12], (DEPTH, D_MODEL, D_MODEL), jnp.float32) * D_MODEL ** -0.5,
        'g_norm2': 1.0 + 0.02 * nrm(ks[13], (DEPTH, D_MODEL), jnp.float32),
        'w_router': nrm(ks[14], (DEPTH, D_MODEL, N_EXPERTS), jnp.float32) * D_MODEL ** -0.5,
        'w_gate_e': nrm(ks[15], (DEPTH, N_EXPERTS, D_MODEL, D_FF_E), jnp.float32) * D_MODEL ** -0.5,
        'w_up_e': nrm(ks[16], (DEPTH, N_EXPERTS, D_MODEL, D_FF_E), jnp.float32) * D_MODEL ** -0.5,
        'w_down_e': nrm(ks[17], (DEPTH, N_EXPERTS, D_FF_E, D_MODEL), jnp.float32) * D_FF_E ** -0.5,
        'g_final': 1.0 + 0.02 * nrm(ks[18], (D_MODEL,), jnp.float32),
    }

def first_block(x, c, ctx, c_ctx, w_ada, b_ada, g_norm1, w_in, b_gates, w_conv, w_fourier, w_mlstm,
              w_out, g_norm2, w_router, w_gate_e, w_up_e, w_down_e, g_final):
    b, seq, _ = x.shape
    rows = seq // GRID_W
    for l in range(DEPTH):
        last = l == DEPTH - 1
        mx = (jax.nn.silu(c) @ w_ada[l] + b_ada[l])[:, None, :]
        sh1, sc1, ga1, sh2, sc2, ga2 = jnp.split(mx, 6, axis=-1)
        mc = jax.nn.silu(c_ctx) @ w_ada[l] + b_ada[l]
        csh1, csc1, cga1, csh2, csc2, cga2 = jnp.split(mc, 6, axis=-1)
        pc = modulate(rmsnorm(ctx, g_norm1[l]), csh1, csc1) @ w_in[l]
        qc, kc, vc, gc = mlstm_inputs(pc, 1, w_conv[l], b_gates[l])
        h_mc, ctx_states = bidir_mlstm(qc, kc, vc, gc, (zero_state(b), zero_state(b)))
        px = modulate(rmsnorm(x, g_norm1[l]), sh1, sc1) @ w_in[l]
        qx, kx, vx, gx = mlstm_inputs(px, rows, w_conv[l], b_gates[l])
        h_mx, _ = bidir_mlstm(qx, kx, vx, gx, ctx_states)
        x = x + ga1 * branch_merge(px, h_mx, w_fourier[l], w_mlstm[l], w_out[l])
        hx2 = modulate(rmsnorm(x, g_norm2[l]), sh2, sc2)
        x = x + ga2 * expert_choice(hx2, w_router[l], w_gate_e[l], w_up_e[l], w_down_e[l])
        if not last:
            ctx = ctx + cga1 * branch_merge(pc, h_mc, w_fourier[l], w_mlstm[l], w_out[l])
            hc2 = modulate(rmsnorm(ctx, g_norm2[l]), csh2, csc2)
            ctx = ctx + cga2 * expert_choice(hc2, w_router[l], w_gate_e[l], w_up_e[l], w_down_e[l])
    return rmsnorm(x, g_final)


DEPTH_2 = 2

QBLK = 128
HEAD_DIM = 64
NORM_EPS = 1e-6

A_HEADS = 4
A_QK_WIDTH = A_HEADS * 2 * HEAD_DIM
A_VDIM = 2 * HEAD_DIM
A_WIDTH = A_HEADS * A_VDIM

B_HEADS = 8
B_WIDTH = B_HEADS * HEAD_DIM

C_HEADS = 8
C_KV_HEADS = 2
C_GROUP = C_HEADS // C_KV_HEADS
C_WIDTH = C_HEADS * HEAD_DIM
C_KV_WIDTH = C_KV_HEADS * HEAD_DIM
WINDOW = 128
WIN_CHUNKS = WINDOW // CHUNK

D_HEADS = 8
D_WIDTH = D_HEADS * HEAD_DIM
D_LEFT_CHUNKS = 8
D_BAND = (D_LEFT_CHUNKS + 1) * CHUNK
REL_MAX = 256
REL_SIZE = REL_MAX + CHUNK

EVEN_SPLITS = (A_QK_WIDTH, A_QK_WIDTH, A_WIDTH, A_WIDTH, B_WIDTH, B_WIDTH, B_WIDTH, B_WIDTH, B_HEADS)
ODD_SPLITS = (C_WIDTH, C_KV_WIDTH, C_KV_WIDTH, C_WIDTH, D_WIDTH, D_WIDTH, D_WIDTH, D_WIDTH)
P_EVEN = sum(EVEN_SPLITS)
P_ODD = sum(ODD_SPLITS)
MIX_EVEN = A_WIDTH + B_WIDTH
MIX_ODD = C_WIDTH + D_WIDTH


def rms_norm(x, g):
    xf = x.astype(jnp.float32)
    y = xf * lax.rsqrt(jnp.mean(xf * xf, axis=-1, keepdims=True) + NORM_EPS)
    return (y * g.astype(jnp.float32)).astype(x.dtype)

def split_cols(z, sizes):
    idx = np.cumsum(np.array(sizes))[:-1].tolist()
    return jnp.split(z, idx, axis=-1)

def alibi_slopes(n_heads):
    return 2.0 ** (-8.0 * jnp.arange(1, n_heads + 1, dtype=jnp.float32) / n_heads)

def sweep_query_blocks(fn, n_blocks):
    out = lax.map(fn, jnp.arange(n_blocks))
    out = jnp.moveaxis(out, 0, 1)
    return out.reshape((out.shape[0], -1) + out.shape[3:])

def diff_attention(q, k, v, lam, lam_init, subln_g):
    bsz, seq = q.shape[:2]
    scale = HEAD_DIM ** -0.5
    slopes = alibi_slopes(A_HEADS)
    tk = jnp.arange(seq)

    def block(b):
        start = b * QBLK
        tq = start + jnp.arange(QBLK)
        qb = lax.dynamic_slice_in_dim(q, start, QBLK, axis=1)
        s = jnp.einsum("bqhcd,bkhcd->bhcqk", qb, k).astype(jnp.float32) * scale
        dist = jnp.abs(tq[:, None] - tk[None, :]).astype(jnp.float32)
        s = s - (slopes[:, None, None] * dist)[None, :, None]
        allowed = (tk[None, :] // CHUNK) <= (tq[:, None] // CHUNK)
        s = jnp.where(allowed, s, -jnp.inf)
        p = jax.nn.softmax(s, axis=-1)
        w = p[:, :, 0] - lam * p[:, :, 1]
        return jnp.einsum("bhqk,bkhe->bqhe", w.astype(v.dtype), v)

    o = sweep_query_blocks(block, seq // QBLK)
    o = rms_norm(o, subln_g) * (1.0 - lam_init)
    return o.reshape(bsz, seq, A_WIDTH)

def forgetting_attention(q, k, v, log_f):
    bsz, seq = q.shape[:2]
    scale = HEAD_DIM ** -0.5
    cum = jnp.transpose(jnp.cumsum(log_f, axis=1), (0, 2, 1))
    tk = jnp.arange(seq)

    def block(b):
        start = b * QBLK
        tq = start + jnp.arange(QBLK)
        qb = lax.dynamic_slice_in_dim(q, start, QBLK, axis=1)
        cq = lax.dynamic_slice_in_dim(cum, start, QBLK, axis=2)
        s = jnp.einsum("bqhd,bkhd->bhqk", qb, k).astype(jnp.float32) * scale
        s = s + cq[..., :, None] - cum[:, :, None, :]
        s = jnp.where(tk[None, :] <= tq[:, None], s, -jnp.inf)
        p = jax.nn.softmax(s, axis=-1)
        return jnp.einsum("bhqk,bkhd->bqhd", p.astype(v.dtype), v)

    o = sweep_query_blocks(block, seq // QBLK)
    return o.reshape(bsz, seq, B_WIDTH)

def sliding_window_sink_attention(q, k, v, sinks):
    bsz, seq = q.shape[:2]
    nb = seq // QBLK
    scale = HEAD_DIM ** -0.5

    def band(t):
        tp = jnp.pad(t, ((0, 0), (QBLK, 0), (0, 0), (0, 0)))
        tb = tp.reshape(bsz, nb + 1, QBLK, C_KV_HEADS, HEAD_DIM)
        return jnp.concatenate([tb[:, :-1], tb[:, 1:]], axis=2)

    kb, vb = band(k), band(v)
    qb = q.reshape(bsz, nb, QBLK, C_KV_HEADS, C_GROUP, HEAD_DIM)
    s = jnp.einsum("bnqkgd,bnskd->bnkgqs", qb, kb).astype(jnp.float32) * scale
    iq = jnp.arange(QBLK)
    ik = jnp.arange(2 * QBLK) - QBLK
    dist = jnp.abs(iq[:, None] - ik[None, :]).astype(jnp.float32)
    slopes = alibi_slopes(C_HEADS).reshape(C_KV_HEADS, C_GROUP, 1, 1)
    s = s - (slopes * dist)[None, None]
    chunk_diff = (iq[:, None] // CHUNK + QBLK // CHUNK) - ((ik[None, :] + QBLK) // CHUNK)
    in_window = (chunk_diff >= 0) & (chunk_diff <= WIN_CHUNKS)
    valid = (jnp.arange(nb)[:, None] * QBLK + ik[None, :]) >= 0
    mask = in_window[None] & valid[:, None, :]
    s = jnp.where(mask[None, :, None, None], s, -jnp.inf)
    sink = jnp.broadcast_to(sinks.astype(jnp.float32).reshape(1, 1, C_KV_HEADS, C_GROUP, 1, 1),
                            s.shape[:-1] + (1,))
    p = jax.nn.softmax(jnp.concatenate([s, sink], axis=-1), axis=-1)[..., :-1]
    o = jnp.einsum("bnkgqs,bnskd->bnqkgd", p.astype(v.dtype), vb)
    return o.reshape(bsz, seq, C_WIDTH)

def chunk_relpos_attention(q, k, v, rel_table):
    bsz, seq = q.shape[:2]
    nc = seq // CHUNK
    scale = HEAD_DIM ** -0.5
    idx = jnp.arange(nc)[:, None] + jnp.arange(D_LEFT_CHUNKS + 1)[None, :]

    def band(t):
        tp = jnp.pad(t, ((0, 0), (D_LEFT_CHUNKS * CHUNK, 0), (0, 0), (0, 0)))
        tp = tp.reshape(bsz, nc + D_LEFT_CHUNKS, CHUNK, D_HEADS, HEAD_DIM)
        return tp[:, idx].reshape(bsz, nc, D_BAND, D_HEADS, HEAD_DIM)

    kb, vb = band(k), band(v)
    qc = q.reshape(bsz, nc, CHUNK, D_HEADS, HEAD_DIM)
    s = jnp.einsum("bnqhd,bnkhd->bnhqk", qc, kb).astype(jnp.float32) * scale
    iq = jnp.arange(CHUNK)
    ik = jnp.arange(D_BAND) - D_LEFT_CHUNKS * CHUNK
    rel = iq[:, None] - ik[None, :]
    ridx = jnp.clip(rel, -(CHUNK - 1), REL_MAX) + (CHUNK - 1)
    bias = rel_table[:, ridx].astype(jnp.float32)
    s = s + bias[None, None]
    valid = (jnp.arange(nc)[:, None] * CHUNK + ik[None, :]) >= 0
    s = jnp.where(valid[None, :, None, None, :], s, -jnp.inf)
    p = jax.nn.softmax(s, axis=-1)
    o = jnp.einsum("bnhqk,bnkhd->bnqhd", p.astype(v.dtype), vb)
    return o.reshape(bsz, seq, D_WIDTH)

def even_layer(x, ln_g, w_in, w_out, a_qn_g, a_kn_g, a_lq1, a_lk1, a_lq2, a_lk2, a_subln_g,
               b_qn_g, b_kn_g, b_f_bias, layer_idx):
    bsz, seq, _ = x.shape
    z = rms_norm(x, ln_g) @ w_in
    aq, ak, av, ag, bq, bk, bv, bg, bf = split_cols(z, EVEN_SPLITS)
    aq = rms_norm(aq.reshape(bsz, seq, A_HEADS, 2, HEAD_DIM), a_qn_g)
    ak = rms_norm(ak.reshape(bsz, seq, A_HEADS, 2, HEAD_DIM), a_kn_g)
    av = av.reshape(bsz, seq, A_HEADS, A_VDIM)
    lam_init = 0.8 - 0.6 * math.exp(-0.3 * layer_idx)
    f32 = jnp.float32
    lam = (jnp.exp(jnp.sum(a_lq1.astype(f32) * a_lk1.astype(f32)))
           - jnp.exp(jnp.sum(a_lq2.astype(f32) * a_lk2.astype(f32))) + lam_init)
    a_out = diff_attention(aq, ak, av, lam, lam_init, a_subln_g)
    bq = rms_norm(bq.reshape(bsz, seq, B_HEADS, HEAD_DIM), b_qn_g)
    bk = rms_norm(bk.reshape(bsz, seq, B_HEADS, HEAD_DIM), b_kn_g)
    bv = bv.reshape(bsz, seq, B_HEADS, HEAD_DIM)
    log_f = jax.nn.log_sigmoid(bf.astype(f32) + b_f_bias.astype(f32))
    b_out = forgetting_attention(bq, bk, bv, log_f)
    mixed = jnp.concatenate([a_out * jax.nn.silu(ag), b_out * jax.nn.silu(bg)], axis=-1)
    return x + mixed @ w_out

def odd_layer(x, ln_g, w_in, w_out, c_qn_g, c_kn_g, c_sinks, d_qn_g, d_kn_g, d_rel_bias):
    bsz, seq, _ = x.shape
    z = rms_norm(x, ln_g) @ w_in
    cq, ck, cv, cg, dq, dk, dv, dg = split_cols(z, ODD_SPLITS)
    cq = rms_norm(cq.reshape(bsz, seq, C_HEADS, HEAD_DIM), c_qn_g)
    ck = rms_norm(ck.reshape(bsz, seq, C_KV_HEADS, HEAD_DIM), c_kn_g)
    cv = cv.reshape(bsz, seq, C_KV_HEADS, HEAD_DIM)
    c_out = sliding_window_sink_attention(cq, ck, cv, c_sinks)
    dq = rms_norm(dq.reshape(bsz, seq, D_HEADS, HEAD_DIM), d_qn_g)
    dk = rms_norm(dk.reshape(bsz, seq, D_HEADS, HEAD_DIM), d_kn_g)
    dv = dv.reshape(bsz, seq, D_HEADS, HEAD_DIM)
    d_out = chunk_relpos_attention(dq, dk, dv, d_rel_bias)
    mixed = jnp.concatenate([c_out * jax.nn.silu(cg), d_out * jax.nn.silu(dg)], axis=-1)
    return x + mixed @ w_out

def second_inputs(seed: int = 0) -> dict:
    key = jax.random.key(seed)
    ne = (DEPTH_2 + 1) // 2
    no = DEPTH_2 // 2
    ks = jax.random.split(key, 23)

    def nrm(k, shape, s):
        return s * jax.random.normal(k, shape, jnp.float32)

    def gain(k, shape):
        return 1.0 + 0.1 * jax.random.normal(k, shape, jnp.float32)

    return {
        "x": jax.random.normal(ks[0], (BATCH, SEQ, D_MODEL), jnp.float32),
        "even_ln_g": gain(ks[1], (ne, D_MODEL)),
        "even_w_in": nrm(ks[2], (ne, D_MODEL, P_EVEN), D_MODEL ** -0.5),
        "even_w_out": nrm(ks[3], (ne, MIX_EVEN, D_MODEL), MIX_EVEN ** -0.5),
        "a_q_norm_g": gain(ks[4], (ne, HEAD_DIM)),
        "a_k_norm_g": gain(ks[5], (ne, HEAD_DIM)),
        "a_lambda_q1": nrm(ks[6], (ne, HEAD_DIM), 0.1),
        "a_lambda_k1": nrm(ks[7], (ne, HEAD_DIM), 0.1),
        "a_lambda_q2": nrm(ks[8], (ne, HEAD_DIM), 0.1),
        "a_lambda_k2": nrm(ks[9], (ne, HEAD_DIM), 0.1),
        "a_subln_g": gain(ks[10], (ne, A_VDIM)),
        "b_q_norm_g": gain(ks[11], (ne, HEAD_DIM)),
        "b_k_norm_g": gain(ks[12], (ne, HEAD_DIM)),
        "b_forget_bias": 3.0 + nrm(ks[13], (ne, B_HEADS), 0.5),
        "odd_ln_g": gain(ks[14], (no, D_MODEL)),
        "odd_w_in": nrm(ks[15], (no, D_MODEL, P_ODD), D_MODEL ** -0.5),
        "odd_w_out": nrm(ks[16], (no, MIX_ODD, D_MODEL), MIX_ODD ** -0.5),
        "c_q_norm_g": gain(ks[17], (no, HEAD_DIM)),
        "c_k_norm_g": gain(ks[18], (no, HEAD_DIM)),
        "c_sinks": nrm(ks[19], (no, C_HEADS), 0.5),
        "d_q_norm_g": gain(ks[20], (no, HEAD_DIM)),
        "d_k_norm_g": gain(ks[21], (no, HEAD_DIM)),
        "d_rel_bias": nrm(ks[22], (no, D_HEADS, REL_SIZE), 0.5),
    }

def second_block(x, even_ln_g, even_w_in, even_w_out, a_q_norm_g, a_k_norm_g, a_lambda_q1,
              a_lambda_k1, a_lambda_q2, a_lambda_k2, a_subln_g, b_q_norm_g, b_k_norm_g,
              b_forget_bias, odd_ln_g, odd_w_in, odd_w_out, c_q_norm_g, c_k_norm_g, c_sinks,
              d_q_norm_g, d_k_norm_g, d_rel_bias):
    for i in range(DEPTH_2):
        j = i // 2
        if i % 2 == 0:
            x = even_layer(x, even_ln_g[j], even_w_in[j], even_w_out[j], a_q_norm_g[j],
                           a_k_norm_g[j], a_lambda_q1[j], a_lambda_k1[j], a_lambda_q2[j],
                           a_lambda_k2[j], a_subln_g[j], b_q_norm_g[j], b_k_norm_g[j],
                           b_forget_bias[j], i)
        else:
            x = odd_layer(x, odd_ln_g[j], odd_w_in[j], odd_w_out[j], c_q_norm_g[j],
                          c_k_norm_g[j], c_sinks[j], d_q_norm_g[j], d_k_norm_g[j],
                          d_rel_bias[j])
    return x


def setup_inputs(seed=0):
    out = dict(first_inputs(seed))
    for name, value in second_inputs(seed + 1).items():
        if name != "x":
            out[name + "_2"] = value
    return out


def reference(
    x, c, ctx, c_ctx, w_ada, b_ada, g_norm1, w_in, b_gates, w_conv, w_fourier, w_mlstm, w_out,
    g_norm2, w_router, w_gate_e, w_up_e, w_down_e, g_final, even_ln_g_2, even_w_in_2,
    even_w_out_2, a_q_norm_g_2, a_k_norm_g_2, a_lambda_q1_2, a_lambda_k1_2, a_lambda_q2_2,
    a_lambda_k2_2, a_subln_g_2, b_q_norm_g_2, b_k_norm_g_2, b_forget_bias_2, odd_ln_g_2,
    odd_w_in_2, odd_w_out_2, c_q_norm_g_2, c_k_norm_g_2, c_sinks_2, d_q_norm_g_2, d_k_norm_g_2,
    d_rel_bias_2,
):
    x = first_block(
        x, c, ctx, c_ctx, w_ada, b_ada, g_norm1, w_in, b_gates, w_conv, w_fourier, w_mlstm,
        w_out, g_norm2, w_router, w_gate_e, w_up_e, w_down_e, g_final,
    )
    return second_block(
        x, even_ln_g_2, even_w_in_2, even_w_out_2, a_q_norm_g_2, a_k_norm_g_2, a_lambda_q1_2,
        a_lambda_k1_2, a_lambda_q2_2, a_lambda_k2_2, a_subln_g_2, b_q_norm_g_2, b_k_norm_g_2,
        b_forget_bias_2, odd_ln_g_2, odd_w_in_2, odd_w_out_2, c_q_norm_g_2, c_k_norm_g_2,
        c_sinks_2, d_q_norm_g_2, d_k_norm_g_2, d_rel_bias_2,
    )


_drawn_inputs = setup_inputs


def setup_inputs(seed=0):
    import zlib

    import numpy as np

    out = dict(_drawn_inputs(seed))
    spreads = {}
    factors = {'ctx': 5.778,
     'c_ctx': 4.495,
     'b_ada': 2.874,
     'g_norm1': 8.0,
     'g_norm2': 7.236,
     'a_lambda_q1_2': 3.851,
     'a_lambda_k1_2': 2.797,
     'b_q_norm_g_2': 5.262,
     'b_k_norm_g_2': 5.312,
     'odd_ln_g_2': 2.811,
     'c_q_norm_g_2': 6.927,
     'c_k_norm_g_2': 5.995,
     'c_sinks_2': 8.0,
     'd_q_norm_g_2': 8.0,
     'd_k_norm_g_2': 8.0,
     'd_rel_bias_2': 3.056}
    for name, (base, spread) in spreads.items():
        noise = np.random.default_rng([zlib.crc32(name.encode()), seed]).standard_normal(out[name].shape)
        drawn = base * np.exp(spread * noise) if base else spread * noise
        out[name] = jnp.asarray(drawn.astype(out[name].dtype))
    for name, factor in factors.items():
        out[name] = (out[name] * factor).astype(out[name].dtype)
    return out
```

```python
import math
from contextlib import ExitStack

import numpy as np
import concourse.bass as bass
from concourse import mybir

F32 = mybir.dt.float32
BF16 = mybir.dt.bfloat16
I32 = mybir.dt.int32
U32 = mybir.dt.uint32
ALU = mybir.AluOpType
ACT = mybir.ActivationFunctionType
AX = mybir.AxisListType

P = 128
D = 1024
SEQ = 1024
CTX = 256
KT = D // P
TT = SEQ // P
CT = CTX // P
HALF = 512
EPS = 1e-6
NH, DH = 4, 128
GRID_W = 64
GRID_H = SEQ // GRID_W
NCH = CT + TT
KSC = DH ** -0.5
NEXP, CAP = 16, 128
RING = 3
BWD = 32
NG = BWD + NH
NEG = -1e30


HD = 64
LAM0 = 0.8 - 0.6 * math.exp(0.0)


class Attn:

    def __init__(self, p, layer, mix0, comps, span, dv, kv_shared=False):
        self.p, self.layer, self.mix0, self.comps, self.dv = p, layer, mix0, comps, dv
        self.units, self.groups = [], []
        for c in range(4):
            order = [(b, h) for b in range(TT) for h in range(2)] if comps == 2 else [(b, h) for h in range(2) for b in range(TT)]
            for b, h in order:
                k0 = max(0, b - span)
                head = 2 * c + h
                qc, row = (head % 4, HD * (head // 4)) if kv_shared else (c, HD * h)
                self.units.append((c, h, b, qc, row, 0 if kv_shared else c, k0, b - k0 + 1))
        for i in range(0, len(self.units), comps):
            self.groups.append(self.units[i:i + comps])
        G = len(self.groups)
        self.G = G
        self.big = [sum(1 for g in self.groups[:u] if g[0][7] > 4) for u in range(G + 1)]
        self.last = {}
        for u, g in enumerate(self.groups):
            self.last[g[0][0]] = u
        self.per_bias = G // 4 if comps == 2 else G // 8
        self.nbias = G // self.per_bias
        self.lag = 1 if comps == 2 else 2

    def steps(self):
        n = self.G
        for i in range(n + self.lag + 3):
            pick = lambda j: j if 0 <= j < n else None
            yield (pick(i), pick(i - self.lag), pick(i - self.lag - 1),
                   [c for c, u in self.last.items() if i == u + self.lag + 2])


def build(nc, a, out, scratch, stop=99):
    ctx = ExitStack()
    sems, shared = {}, {}

    def S(name):
        name = shared[name][0] if name in shared else name
        if name not in sems:
            sems[name] = ctx.enter_context(nc.semaphore(name))
        return sems[name]

    class Chain:

        def __init__(self, eng, name):
            self.eng, self.sem, self.n, self.loop = eng, S(name), 0, 0

        def __call__(self, ins):
            self.n += 1
            ins.then_inc(self.sem, 1)
            self.eng.wait_ge(self.sem, self.loop + self.n)

    with ctx:
        ATT = {"A": Attn("A", 0, 0, 2, TT, 2 * HD), "B": Attn("B", 0, 4, 1, TT, HD),
               "C": Attn("C", 1, 0, 1, 1, HD, kv_shared=True), "D": Attn("D", 1, 4, 1, 4, HD)}

        def share(kind, stages):
            total = {}
            for prefix, signals in stages:
                for sig, n in signals.items():
                    shared[prefix + sig] = (kind + sig, total.get(sig, 0))
                    total[sig] = total.get(sig, 0) + n

        def before(name):
            return shared[name][1] if name in shared else 0

        share("norm", [(p, {"_sq": t, "_rt": 1, "_xn": t, "_tr": 2 * t, "_evA": t, "_evD": t})
                       for p, t in (("n1", TT), ("nc", CT), ("n2", TT), ("n3", TT), ("n4", TT))])
        share("plain", [(p, {"_mm": j, "_evA": (j + 1) // 2, "_evD": j // 2})
                        for p, j in (("ada", 12), ("u", TT), ("dft", 16), ("fu", 8), ("v", NCH), ("av", TT), ("bv", TT), ("dv", TT))])
        share("proj", [(p, {q: TT for q in ("_z", "_sq", "_ss", "_rt", "_zn", "_tr", "_evA")})
                       for p in ("aq", "ak", "bq", "bk", "cq", "ck", "dq", "dk")])
        share("sigate", [(p, {"_mm": 8, "_sg": 8, "_mul": 8}) for p in ("ag", "bg", "cg", "dg")])
        share("wout", [(p, {"_mm": 2 * TT, "_ev": 2 * TT}) for p in ("wo", "wo0", "wo1")])
        share("res", [(p, {"_out": 16, "_in": 16}) for p in ("res0", "res1")])
        share("attn", [(n, {"_qk": len(at.units), "_s": len(at.units), "_e": len(at.units), "_w": at.G if n == "A" else 0, "_tr": at.G,
                            "_wevA": at.G, "_wevD": at.big[at.G], "_pv": at.G, "_o": at.G, "_on": 4 if n == "A" else 0, "_otr": 8, "_mix": 8,
                            **({} if n == "D" else {"_bias0": 64, "_bias1": 0 if n == "A" else 64})})
                       for n, at in ATT.items()])

        def sb(name, cols, dt=F32, parts=P):
            return ctx.enter_context(nc.sbuf_tensor(name, [parts, cols], dt))

        ring = sb("ring", RING * KT * HALF)
        hidden = sb("hidden", KT * SEQ)
        ctx_hidden = sb("ctx_hidden", KT * CTX)
        pair = sb("pair", 8192)
        wide = sb("wide", 9256)
        small = sb("small", 6500)
        kctx = sb("kctx", NH * CTX)
        cols = sb("cols", NCH * 4 * NG)
        ident = sb("ident", P)
        identb = sb("identb", P, BF16)
        maskb = sb("maskb", 2 * NH * P, BF16)
        sel_wT = sb("sel_wT", 8 * P)
        sel = sel_wT[0:NG, :]
        dftc = sb("dftc", 2 * P)
        cT = sb("cT", KT * 2)
        csil = sb("csil", KT * 2)
        adaT = sb("adaT", 2 * 48)
        badaT = sb("badaT", 48)
        gT = sb("gT", 5 * KT)
        mod = sb("mod", 3 * KT)
        wconv = sb("wconv", 8 * 9)
        wgate = sb("wgate", KT * 2 * NG)
        bgate = sb("bgate", 2)
        epsc = sb("epsc", 1)
        onec = sb("onec", 1)
        wrt = sb("wrt", KT * NEXP)
        extra = sb("extra", SEQ)
        att = sb("att", 64)
        qst = sb("qst", 48)
        gcol = sb("gcol", 16)
        wbf = wgate[:, 384:448]
        bbf = sb("bbf", 1)
        stat = sb("stat", 64)
        psum = ctx.enter_context(nc.psum_tensor("psum", [P, 8 * HALF], F32))

        def bank(b):
            return psum[:, b * HALF:(b + 1) * HALF]

        def ringv(s):
            return ring[:, s * KT * HALF:(s + 1) * KT * HALF].rearrange("p (k n) -> p k n", k=KT)

        hT = hidden[:].rearrange("p (k n) -> p k n", k=KT)
        hcT = ctx_hidden[:].rearrange("p (k n) -> p k n", k=KT)
        x_sb = wide[:, 0:TT * D].rearrange("p (t n) -> p t n", t=TT)
        xn_buf = small[:, 0:2 * D].rearrange("p (b n) -> p b n", b=2)
        sq_buf = small[:, 2 * D:3 * D]
        cx_sb = small[:, 3 * D:5 * D].rearrange("p (t n) -> p t n", t=CT)
        mask_in = ctx_hidden[:, 0:2 * NH * P]
        adarow = pair[0:2, 0:6 * D]
        u_sb = small[:, 0:4 * D].rearrange("p (t n) -> p t n", t=TT)
        pq = pair[:].rearrange("p (a c n) -> p a c n", a=2, c=4)
        fuT = wide[:, 0:4 * D].rearrange("p (c n) -> p c n", c=4)

        tiles, place, last_read = [], {}, []

        def kview(w, c0, n=HALF, r0=0, rows=D):
            return w[r0:r0 + rows, c0:c0 + n].rearrange("(k p) n -> p k n", p=P)

        def add_tile(key, read, w, c0, n=HALF):
            place[key] = len(tiles)
            last_read.append(read)
            tiles.append([(0, 4, n, kview(w, c0, n, 0, 512)), (4, 4, n, kview(w, c0, n, 512, 512))])

        OFF_QK, OFF_V, OFF_O, OFF_G, OFF_BR = 512, 1536, 2048, 2560, 2576
        for j in range(12):
            add_tile(("ada", j), ("ada_mm", j + 1), a["w_ada"], j * HALF)
        add_tile("f", ("u_mm", TT), a["w_in"], 0)
        for n in range(2):
            add_tile(("cos", n), ("dft_mm", 8 * n + 4), a["dft_cos"], n * HALF)
            add_tile(("sin", n), ("dft_mm", 8 * n + 8), a["dft_sin"], n * HALF)
        add_tile("q", ("qk_mm", NH), a["w_in"], OFF_QK)
        add_tile("k", ("qk_mm", 2 * NH), a["w_in"], OFF_QK + 512)
        add_tile("v", ("v_mm", NCH), a["w_in"], OFF_V)
        add_tile("o", ("o_mm", 8), a["w_in"], OFF_O)
        for m in range(2):
            place["fm", m] = len(tiles)
            last_read.append(("mg_y", 8 * (m + 1)))
            tiles.append([(0, 4, HALF, kview(a["w_fourier"], m * HALF, rows=512)),
                          (4, 4, HALF, kview(a["w_mlstm"], m * HALF, rows=512))])
            add_tile(("br1", m), ("mg_y", 8 * (m + 1)), a["w_in"], OFF_BR + m * HALF)
            add_tile(("br2", m), ("mg_y", 8 * (m + 1)), a["w_in"], OFF_BR + D + m * HALF)
        for m in range(2):
            add_tile(("wo", m), ("wo_mm", TT * (m + 1)), a["w_out"], m * HALF)

        n_moe = len(tiles)
        for e in range(NEXP + 1):
            if e < NEXP:
                for key, sig in (("gate", "moe_g"), ("up", "moe_u")):
                    for m in range(2):
                        add_tile((key, e, m), (sig, 2 * e + m + 1), a["w_" + key][e], m * HALF)
            if e >= 1:
                for m in range(2):
                    add_tile(("down", e - 1, m), ("moe_d", 2 * (e - 1) + m + 1), a["w_down"][e - 1], m * HALF)
        assert n_moe % RING == 2
        for layer, w, plan in ((0, a["even_w_in"], (("aq", 0), ("ak", 512), ("av", 1024), ("bq", 2048), ("bk", 2560), ("bv", 3072),
                                                    ("ag", 1536), ("bg", 3584))),
                               (1, a["odd_w_in"], (("cq", 0), ("ck", 512), ("dq", 1280), ("dk", 1792), ("dv", 2304),
                                                   ("cg", 768), ("dg", 2816)))):
            for key, c0 in plan:
                sig = {"v": ("_mm", TT), "g": ("_mm", 8)}.get(key[1], ("_z", TT))
                add_tile(key, (key + sig[0], sig[1]), w, c0, 256 if key == "ck" else HALF)
            for m in range(2):
                add_tile(("out", layer, m), (f"wo{layer}_mm", TT * (m + 1)), a[("even_w_out", "odd_w_out")[layer]], m * HALF)
        LOOPED = (place["gate", 2, 0], place["down", 15, 0])

        def load_tile(sp, n):
            if n >= RING:
                name, value = last_read[n - RING]
                sp.wait_ge(S(name), before(name) + value)
            for k0, kn, w, src in tiles[n]:
                sp.dma_start(ringv(n % RING)[:, k0:k0 + kn, 0:w], src).then_inc(S(f"ring_full{n % RING}"), 16)

        def tile_ready(pe, key):
            n = place[key]
            pe.wait_ge(S(f"ring_full{n % RING}"), 32 * (n // RING + 1))
            return ringv(n % RING)

        def group(pe, outp, pairs):
            for i, (l, r) in enumerate(pairs):
                mm = pe.matmul(outp, l, r, start=(i == 0), stop=(i == len(pairs) - 1))
            return mm

        def jobs_mm(pe, p, j, nb, outp, pairs):
            if j >= nb:
                pe.wait_ge(S(p + "_ev" + "AD"[j % 2]), before(p + "_ev" + "AD"[j % 2]) + (j - nb) // 2 + 1)
            mm = group(pe, outp, pairs)
            mm.then_inc(S(p + "_mm"), 1)
            return mm

        def emptied(eng, p, jobs):
            eng.wait_ge(S(p + "_evA"), before(p + "_evA") + (jobs + 1) // 2)
            if jobs > 1:
                eng.wait_ge(S(p + "_evD"), before(p + "_evD") + jobs // 2)

        def evac(eng, p, jobs, f):
            side = 0 if hasattr(eng, "activation") else 1
            for j in range(side, jobs, 2):
                eng.wait_ge(S(p + "_mm"), before(p + "_mm") + j + 1)
                f(j).then_inc(S(p + "_ev" + "AD"[side]), 1)

        def copy(eng, o, i):
            return eng.activation(o, i, ACT.Copy) if hasattr(eng, "activation") else eng.tensor_copy(o, i)

        def norm_act(act, link, p, T, src, ready, col, dst, A, B):
            for t in range(T):
                ready(act, t)
                if t:
                    act.wait_ge(S(p + "_sq"), before(p + "_sq") + t)
                ins = act.activation(sq_buf, src(t), ACT.Square, accum_out=stat[:, col + t:col + t + 1])
                ins.then_inc(S(p + "_sq"), 1)
            act.wait_ge(S(p + "_sq"), before(p + "_sq") + T)
            act.activation(stat[:, col + 16:col + 16 + T], stat[:, col:col + T], ACT.Sqrt,
                           bias=epsc[:, 0:1], scale=1.0 / D).then_inc(S(p + "_rt"), 1)
            for t in range(T):
                act.wait_ge(S(p + "_tr"), before(p + "_tr") + 2 * t + 1)
                for k in range(4):
                    ins = act.activation(dst(t, k), bank(2 * (t % 2))[:, k * P:(k + 1) * P], ACT.Identity,
                                         bias=(B(k) if B else 0.0), scale=A(k))
                ins.then_inc(S(p + "_evA"), 1)

        def norm_dve(dve, link, p, T, src, ready, col, dst, A, B, stored=None):
            dve.wait_ge(S(p + "_rt"), before(p + "_rt") + 1)
            for t in range(T):
                ready(dve, t)
            link(dve.reciprocal(stat[:, col + 32:col + 32 + T], stat[:, col + 16:col + 16 + T]))
            for t in range(T + 1):
                if t < T:
                    if t >= 2:
                        dve.wait_ge(S(p + "_tr"), before(p + "_tr") + 2 * (t - 1))
                        if stored:
                            stored(dve, t - 2)
                    dve.tensor_scalar(xn_buf[:, t % 2, :], src(t), stat[:, col + 32 + t:col + 33 + t], None,
                                      ALU.mult).then_inc(S(p + "_xn"), 1)
                if t >= 1:
                    dve.wait_ge(S(p + "_tr"), before(p + "_tr") + 2 * t)
                    for k in range(4, 8):
                        i = bank(2 * ((t - 1) % 2) + 1)[:, (k - 4) * P:(k - 3) * P]
                        if B:
                            ins = dve.tensor_scalar(dst(t - 1, k), i, A(k), B(k), ALU.mult, ALU.add)
                        else:
                            ins = dve.tensor_scalar(dst(t - 1, k), i, A(k), None, ALU.mult)
                    ins.then_inc(S(p + "_evD"), 1)

        def norm_pe(pe, p, T):
            for t in range(T):
                pe.wait_ge(S(p + "_xn"), before(p + "_xn") + t + 1)
                if t >= 2:
                    pe.wait_ge(S(p + "_evA"), before(p + "_evA") + t - 1)
                    pe.wait_ge(S(p + "_evD"), before(p + "_evD") + t - 1)
                for h in range(2):
                    for k in range(4):
                        mm = pe.transpose(bank(2 * (t % 2) + h)[:, k * P:(k + 1) * P],
                                          xn_buf[:, t % 2, (4 * h + k) * P:(4 * h + k + 1) * P], ident[:])
                    mm.then_inc(S(p + "_tr"), 1)

        def normed(eng, p, T):
            eng.wait_ge(S(p + "_evA"), before(p + "_evA") + T)
            eng.wait_ge(S(p + "_evD"), before(p + "_evD") + T)

        PADW, PADH = GRID_W + 2, GRID_H + 2
        pads = [small[:, i * 1280:i * 1280 + PADH * PADW] for i in range(2)]
        cpads = [small[:, 2560 + i * 320:2560 + i * 320 + CTX + 2] for i in range(2)]
        accs = [small[:, 3200 + i * 1280:3200 + i * 1280 + SEQ] for i in range(2)]
        caccs = [small[:, 3200 + i * 1280 + SEQ:3200 + (i + 1) * 1280] for i in range(2)]
        qT = pair[:, 0:4 * D].rearrange("p (h n) -> p h n", h=NH)
        kT = pair[:, 4 * D:8 * D].rearrange("p (h n) -> p h n", h=NH)
        kcT = kctx[:].rearrange("p (h n) -> p h n", h=NH)
        VW = DH + 1
        vex = wide[:, 0:NCH * NH * VW].rearrange("p (c h n) -> p c h n", c=NCH, h=NH)
        hsum = wide[:, NCH * NH * VW:NCH * NH * VW + 4 * D].rearrange("p (c n) -> p c n", c=TT)
        mT = wide[:, 0:KT * D].rearrange("p (k n) -> p k n", k=KT)
        TTOT = CTX + SEQ
        rowv = small[0:NG, 0:6400].rearrange("p (a n) -> p a n", n=1280)
        rF, rI, rC, rM, rR = (rowv[:, i, :] for i in (1, 2, 3, 4, 0))
        ones_row = cols[0:NG, 0:P]
        colv = cols[:].rearrange("p (c a g) -> p c a g", c=NCH, a=4)
        Cst = small[:, 1280:1280 + 8 * VW].rearrange("p (c n) -> p c n", c=8)
        kw = small[:, 2312:2312 + 1024].rearrange("p (b h n) -> p b h n", b=2, h=NH)
        se = small[:, 3336:3336 + 1024].rearrange("p (b h n) -> p b h n", b=2, h=NH)
        ee = small[:, 4360:4360 + 1024].rearrange("p (b h n) -> p b h n", b=2, h=NH)
        ob = small[:, 5384:5384 + NH * VW].rearrange("p (h n) -> p h n", h=NH)
        dnb = small[:, 5900:5900 + 8 * NCH].rearrange("p (c n) -> p c n", c=8)
        rec = small[:, 5980:5984]
        tmpn = small[:, 5984:6496].rearrange("p (h n) -> p h n", h=NH)
        oT = pair[:, 0:4 * D].rearrange("p (h n) -> p h n", h=NH)
        hmT = pair[:, 4 * D:8 * D].rearrange("p (h n) -> p h n", h=NH)
        fuR = small[:, 0:4 * D].rearrange("p (c n) -> p c n", c=4)
        sg = small[:, 4 * D:4 * D + 2048].rearrange("p (b a n) -> p b a n", b=2, a=2)
        sgd = ctx_hidden[:].rearrange("p (b a n) -> p b a n", b=2, a=2)

        x2nd = pair[:].rearrange("p (t n) -> p t n", t=TT)
        x1 = hidden[:].rearrange("p (t n) -> p t n", t=TT)
        h2T = pair[:].rearrange("p (k n) -> p k n", k=KT)
        ga1b, ga2b = small[:, 3072:4096], small[:, 4096:5120]
        gfb = small[:, 5120:6144]
        affT = ctx_hidden[0:NEXP, 0:SEQ]
        aff = ctx_hidden[:, SEQ:SEQ + P].rearrange("p (t e) -> p t e", e=NEXP)
        route = kctx[:, 0:512]
        vals, idx, idxf = route[0:NEXP, 0:P], route[0:NEXP, P:2 * P].bitcast(U32), route[0:NEXP, 2 * P:3 * P]
        valc, idxc = route[:, 384:400], route[:, 400:416].bitcast(I32)
        idx1 = route[:, 416:420].bitcast(I32)
        lmax, lsum = route[:, 420:428], route[:, 428:436]
        xg, xs, sgate, hid, hd, yb = (wide[:, i * D:(i + 1) * D] for i in range(6))
        xsT, hidT = xs.rearrange("p (k n) -> p k n", k=KT), hd.rearrange("p (k n) -> p k n", k=KT)

        qT2 = wide[:, 0:4 * D].rearrange("p (c n) -> p c n", c=4)
        kT2 = wide[:, 4 * D:8 * D].rearrange("p (c n) -> p c n", c=4)
        v2 = small[:, 0:4 * D].rearrange("p (t n) -> p t n", t=TT)
        obuf = [small[:, (4 + i) * D:(5 + i) * D].rearrange("p (b n) -> p b n", b=TT) for i in range(2)]
        xlay = [pair[:].rearrange("p (k n) -> p k n", k=KT), hidden[:].rearrange("p (k n) -> p k n", k=KT)]
        H2 = xlay
        M2 = xlay[::-1]
        R2 = xlay
        x3 = wide[:, 0:TT * D].rearrange("p (t n) -> p t n", t=TT)
        wT = [w[:].rearrange("p (k n) -> p k n", k=KT) for w in (kctx, sel_wT)]
        sA = [ctx_hidden[:, 0:D], ctx_hidden[:, D:2 * D], wide[:, 8 * D:9 * D], extra[:]]
        SBUFS = {"A": sA, "B": sA[:3], "C": sA, "D": sA}
        BIAS = {"A": [cols[:, 0:D]], "B": [cols[:, 0:D], extra[:]],
                "C": [cols[:, 0:256], cols[:, 256:512]], "D": [cols[:, 0:640], cols[:, 640:1280]]}
        nmx, esum, rinv, esk = (att[:, 8 * i:8 * i + 8] for i in range(4))
        sinkb, nsink, nlam, lsums = att[:, 32:40], att[:, 40:48], att[:, 48:49], att[:, 50:52]
        lamb = wgate[:, 0:256].rearrange("p (a n) -> p a n", a=4)
        lamx = wgate[:, 256:384].rearrange("p (a n) -> p a n", a=2)
        sqz = [extra[:, 0:HALF], extra[:, HALF:D]]
        zn = [ctx_hidden[:, 0:HALF], ctx_hidden[:, HALF:D]]
        frow = [ctx_hidden[0:8, 0:D], ctx_hidden[0:8, D:2 * D], wide[0:8, 8 * D:9 * D]]
        xsq = cols[:, D:D + P]
        sgt = [extra[:, 0:HALF], extra[:, HALF:D]]
        QK = {"aq": (0, 8, HALF, qT2), "ak": (0, 1, HALF, kT2), "bq": (0, 9, HALF, qT2), "bk": (0, 3, HALF, kT2),
              "cq": (1, 10, HALF, qT2), "ck": (1, 5, P, kT2), "dq": (1, 11, HALF, qT2), "dk": (1, 7, HALF, kT2)}

        steps = []
        for i in range(NCH):
            f = i
            b = (CT - 1 - i) if i < CT else NCH - 1 - (i - CT)
            steps += [(0, f, i >= CT), (1, b, i >= CT)]
        outs_before = [sum(1 for s in steps[:i] if s[2]) for i in range(len(steps) + 1)]

        def span(c):
            return slice(c * P, (c + 1) * P)

        def chain_row(d, h):
            return (BWD if d else 0) + h

        def ksrc(h, c):
            return kcT[:, h, c * P:(c + 1) * P] if c < CT else kT[:, h, (c - CT) * P:(c - CT + 1) * P]

        block = ctx.enter_context(nc.Block())

        @block.sync
        def _(sp):
            for n in range(2):
                load_tile(sp, n)
            sp.dma_start(x_sb, a["x"].rearrange("(t p) n -> p t n", p=P)).then_inc(S("x_in"), 16)
            sp.dma_start(cx_sb, a["ctx"].rearrange("(t p) n -> p t n", p=P)).then_inc(S("cx_in"), 16)
            for n in range(2, len(tiles)):
                if n == LOOPED[0]:
                    with sp.Fori(2, NEXP) as e:
                        for j in range(6):
                            name, value = (("moe_u", e * 2), ("moe_d", e * 2 - 3), ("moe_d", e * 2 - 2),
                                           ("moe_g", e * 2 + 1), ("moe_g", e * 2 + 2), ("moe_u", e * 2 + 1))[j]
                            sp.wait_ge(S(name), before(name) + value)
                            w = a[("w_gate", "w_up", "w_down")[j // 2]]
                            w = w[bass.ds(e - j // 4, 1), :, (j % 2) * HALF:(j % 2 + 1) * HALF].rearrange("e (k p) n -> p (e k) n", p=P)
                            for k0 in (0, 4):
                                sp.dma_start(ringv(j % RING)[:, k0:k0 + 4, :], w[:, k0:k0 + 4, :]).then_inc(S(f"ring_full{j % RING}"), 16)
                if LOOPED[0] <= n < LOOPED[1]:
                    continue
                if stop < 8 and n == place["aq"]:
                    tiles[:] = tiles[:n]
                    break
                load_tile(sp, n)
                if n == place["wo", 1]:
                    sp.wait_ge(S("mg_add"), 16)
                    sp.dma_start(x2nd, a["x"].rearrange("(t p) n -> p t n", p=P)).then_inc(S("x_again"), 16)
                    if stop < 7:
                        return
                if n == place["o"] and stop < 4:
                    for q in range(RING):
                        sp.wait_ge(S(f"ring_full{q}"), 32 * sum(1 for z in range(n + 1) if z % RING == q))
                    return
                if n == place["k"]:
                    emptied(sp, "fu", 8)
                    sp.dma_start(scratch["fu"], fuT).then_inc(S("fu_out"), 16)
                if n == place["br1", 0]:
                    sp.wait_ge(S("scan_out"), TT * 2)
                    sp.wait_ge(S("fu_out"), 16)
                    sp.dma_start(fuR, scratch["fu"]).then_inc(S("fu_in"), 16)

            if stop < 8:
                for t in range(TT):
                    sp.wait_ge(S("xb"), t + 1)
                    sp.dma_start(out.rearrange("(t p) n -> p t n", p=P)[:, t, :], x1[:, t, :]).then_inc(S("out"), 16)
                sp.wait_ge(S("out"), 16 * TT)
            for q in range(RING):
                sp.wait_ge(S(f"ring_full{q}"), 32 * len(range(q, len(tiles), RING)))

        @block.gpsimd
        def _(pool):
            for o, i in ((cT[:], a["cT"]), (badaT[:], a["b_adaT"]), (gT[:], a["gT"]), (ident[:], a["ident"]),
                         (mask_in, a["masks"]), (sel, a["sel"]),
                         (dftc[:], a["dftc"]), (wconv[:], a["w_convT"]), (wgate[:], a["w_mgate"]),
                         (bgate[0:NG, :], a["b_gate"]), (wrt[:], a["w_routerT"])):
                pool.dma_start(o, i).then_inc(S("const"), 16)
            pool.memset(epsc[:], EPS).then_inc(S("epsc"), 1)
            pool.memset(onec[:], 1.0).then_inc(S("epsc"), 1)

            pool.wait_ge(S("mod"), 1)
            pool.dma_start(scratch["ada"].rearrange("(c p) -> p c", p=P), adaT[:, 0:48], allow_slow_non_contiguous=True).then_inc(S("ada_out"), 16)
            pool.wait_ge(S("ada_out"), 16)
            pool.wait_ge(S("mg_add"), 16)
            pool.dma_start(ga1b, scratch["ada"][2 * D:3 * D].partition_broadcast(P)).then_inc(S("ga1"), 16)
            pool.dma_start(ga2b, scratch["ada"][5 * D:6 * D].partition_broadcast(P)).then_inc(S("ga2"), 16)
            pool.dma_start(gfb, a["g_final"].partition_broadcast(P)).then_inc(S("gf"), 16)
            if stop < 7:
                pool.wait_ge(S("ga1"), 16); pool.wait_ge(S("ga2"), 16); pool.wait_ge(S("gf"), 16)
                return
            for t in range(TT):
                pool.wait_ge(S("wo_ev"), before("wo_ev") + TT + t + 1)
                pool.dma_start(scratch["acc"].rearrange("(t p) n -> p t n", p=P)[:, t, :], x1[:, t, :]).then_inc(S("acc_out"), 16)
            for t in range(TT):
                pool.wait_ge(S("n2_xn"), before("n2_xn") + t + 1)
                pool.dma_start(scratch["xn"].rearrange("(t p) n -> p t n", p=P)[:, t, :], xn_buf[:, t % 2, :]).then_inc(S(f"xn_out{t % 2}"), 16)
            pool.wait_ge(S("acc_out"), 16 * TT)
            for q in range(2):
                pool.wait_ge(S(f"xn_out{q}"), 16 * TT // 2)

            pool.wait_ge(S("route"), 1)
            pool.tensor_copy(idx1[:, 0:1], idxc[:, 0:1]).then_inc(S("moe_first"), 1)
            pool.wait_ge(S("moe_first"), 1)
            pool.indirect_dma_start(xg, None, scratch["xn"], bass.IndirectOffsetOnAxis(idx1[:, 0:1].bitcast(U32), 0)).then_inc(S("moe_gat"), 16)
            pool.wait_ge(S("moe_gat"), 16)
            pool.wait_ge(S("moe_xtr"), 2)
            pool.tensor_copy(idx1[:, 0:1], idxc[:, 1:2]).then_inc(S("moe_ix0"), 1)
            pool.wait_ge(S("moe_ix0"), 1)
            pool.indirect_dma_start(xg, None, scratch["xn"], bass.IndirectOffsetOnAxis(idx1[:, 0:1].bitcast(U32), 0)).then_inc(S("moe_gat"), 16)

            def one(e, more):
                if more:
                    pool.wait_ge(S("moe_xtr"), e * 2 + 2)
                    pool.wait_ge(S("moe_gat"), e * 16 + 16)
                    pool.tensor_copy(idx1[:, 0:1], idxc[:, bass.ds(e + 1, 1)])
                    pool.drain()
                    pool.indirect_dma_start(xg, None, scratch["xn"], bass.IndirectOffsetOnAxis(idx1[:, 0:1].bitcast(U32), 0)).then_inc(S("moe_gat"), 16)
                pool.wait_ge(S("moe_y"), e * 2)
                pool.tensor_copy(idx1[:, 1:2], idxc[:, bass.ds(e - 1, 1)])
                pool.drain()
                pool.indirect_dma_start(scratch["acc"], bass.IndirectOffsetOnAxis(idx1[:, 1:2].bitcast(U32), 0), yb, None,
                                        compute_op=ALU.add).then_inc(S("moe_sct"), 16)
                pool.wait_ge(S("moe_sct"), e * 16)

            with pool.Fori(1, NEXP - 1) as e:
                one(e, True)
            one(NEXP - 1, False)
            one(NEXP, False)
            pool.dma_start(x1, scratch["acc"].rearrange("(t p) n -> p t n", p=P)).then_inc(S("x2_in"), 16)
            pool.wait_ge(S("rows"), 1)
            for o, i in ((lamb, a["lams"].partition_broadcast(P)), (sinkb, a["sinks"].partition_broadcast(P)),
                         (gcol[:, 0:8], a["qk_gains"]), (gcol[:, 12:13], a["sub_gain"]), (wbf, a["w_forget"]),
                         (bbf[0:8, :], a["b_forget"])):
                pool.dma_start(o, i).then_inc(S("const2"), 16)
            if stop < 8:
                pool.wait_ge(S("const2"), 16 * 6)
                return
            for layer in range(2):
                pool.wait_ge(S(("xb", "x3")[layer]), before(("xb", "x3")[layer]) + (TT, 2 * TT)[layer])
                rows = scratch[("xb", "x3")[layer]].rearrange("(t p) n -> p t n", p=P)
                pool.dma_start(rows, (x1, x3)[layer]).then_inc(S(f"res{layer}_out"), 16)
                for name in ("AB", "CD")[layer]:
                    att = ATT[name]
                    nb = len(BIAS[name])
                    if name == "B":
                        pool.wait_ge(S("forget"), 1)
                        pool.dma_start(scratch["ncum"], frow[0]).then_inc(S("ncum_out"), 16)
                        pool.wait_ge(S("ncum_out"), 16)
                    if name == "A":
                        pool.wait_ge(S("ak_evA"), before("ak_evA") + TT)
                    for i in range(att.nbias):
                        o = BIAS[name][i % nb]
                        if i >= nb:
                            pool.wait_ge(S(name + "_s"), before(name + "_s") + att.per_bias * att.comps * (i - nb + 1))
                        elif name in "BD":
                            pool.wait_ge(S(name.lower() + "k_evA"), before(name.lower() + "k_evA") + TT)
                        elif name == "C":
                            pool.wait_ge(S("ck_evA"), before("ck_evA") + TT)
                        src = {"A": lambda: a["strip_a"][i], "B": lambda: scratch["ncum"][i].partition_broadcast(P),
                               "C": lambda: a["strip_c"][i],
                               "D": lambda: bass.AP(tensor=a["rel"].tensor, offset=i * 768, ap=[[1, P], [1, 640]])}[name]()
                        if name != "D":
                            pool.dma_start(o, src).then_inc(S(name + f"_bias{i % nb}"), 16)
                        else:
                            pool.dma_start(o, src).then_inc(S(f"D_rel{i % nb}"), 16)
                            pool.wait_ge(S(f"D_rel{i % nb}"), 16 * (i // nb + 1))
                            pool.memset(o[HD:P, 640 - HD:640], NEG).then_inc(S(f"D_bias{i % nb}"), 8)
                            pool.memset(o[0:HD, 0:HD], NEG).then_inc(S(f"D_bias{i % nb}"), 8)
                pool.wait_ge(S(("bg", "dg")[layer] + "_mm"), before(("bg", "dg")[layer] + "_mm") + 8)
                pool.wait_ge(S(f"res{layer}_out"), before(f"res{layer}_out") + 16)
                pool.dma_start(R2[layer], rows).then_inc(S(f"res{layer}_in"), 16)
            for t in range(TT):
                pool.wait_ge(S("wo1_ev"), before("wo1_ev") + TT + t + 1)
                pool.dma_start(out.rearrange("(t p) n -> p t n", p=P)[:, t, :], x3[:, t, :]).then_inc(S("out"), 16)
            pool.wait_ge(S("out"), 16 * TT)

        def consts(eng):
            eng.wait_ge(S("const"), 16 * 11)
            eng.wait_ge(S("epsc"), 2)

        xr = lambda eng, t: eng.wait_ge(S("x_in"), 16)
        cr = lambda eng, t: eng.wait_ge(S("cx_in"), 16)
        NX = ("n1", TT, lambda t: x_sb[:, t, :], xr, 0, lambda t, k: hT[:, k, t * P:(t + 1) * P],
              lambda k: mod[:, k:k + 1], lambda k: adaT[:, k:k + 1])
        NC = ("nc", CT, lambda t: cx_sb[:, t, :], cr, 8, lambda t, k: hcT[:, k, t * P:(t + 1) * P],
              lambda k: mod[:, KT + k:KT + k + 1], lambda k: adaT[:, 48 + k:48 + k + 1])

        W1 = lambda eng, t: eng.wait_ge(S("wo_ev"), before("wo_ev") + TT + t + 1)
        N2 = ("n2", TT, lambda t: x1[:, t, :], W1, 0, lambda t, k: h2T[:, k, t * P:(t + 1) * P],
              lambda k: mod[:, 2 * KT + k:2 * KT + k + 1], lambda k: adaT[:, 3 * KT + k:3 * KT + k + 1])

        def bias_ready(eng, name, g):
            att = ATT[name]
            i, nb = g // att.per_bias, len(BIAS[name])
            eng.wait_ge(S(name + f"_bias{i % nb}"), before(name + f"_bias{i % nb}") + 16 * (i // nb + 1))
            return BIAS[name][i % nb]

        XB = lambda eng, t: eng.wait_ge(S("xb"), t + 1)
        X3 = lambda eng, t: eng.wait_ge(S("wo0_ev"), before("wo0_ev") + TT + t + 1)
        N3 = ("n3", TT, lambda t: x1[:, t, :], XB, 0, lambda t, k: H2[0][:, k, t * P:(t + 1) * P],
              lambda k: gT[:, 2 * KT + k:2 * KT + k + 1], None)
        N4 = ("n4", TT, lambda t: x3[:, t, :], X3, 0, lambda t, k: H2[1][:, k, t * P:(t + 1) * P],
              lambda k: gT[:, 3 * KT + k:3 * KT + k + 1], None)

        @block.tensor
        def _(pe):
            consts(pe)
            pe.wait_ge(S("csil"), 1)
            for j in range(12):
                w = tile_ready(pe, ("ada", j))
                jobs_mm(pe, "ada", j, 2, bank(j % 2)[0:2, :],
                        [(csil[:, 2 * k:2 * k + 2], w[:, k, :]) for k in range(KT)])
            emptied(pe, "ada", 12)
            for j in range(48):
                mm = pe.transpose(bank(2)[:, 2 * j:2 * j + 2], adarow[:, j * P:(j + 1) * P], ident[0:2, 0:2])
            mm.then_inc(S("adaT_mm"), 1)
            norm_pe(pe, "n1", TT)
            normed(pe, "n1", TT)
            norm_pe(pe, "nc", CT)
            normed(pe, "nc", CT)
            w = tile_ready(pe, "f")
            for t in range(TT):
                mm = jobs_mm(pe, "u", t, 4, bank(t % 4), [(hT[:, k, span(t)], w[:, k, :]) for k in range(KT)])
            emptied(pe, "u", 8)
            j = 0
            for n in range(2):
                for part, key in enumerate(("cos", "sin")):
                    w = tile_ready(pe, (key, n))
                    for c in range(4):
                        mm = jobs_mm(pe, "dft", j, 4, bank(j % 4),
                                     [(u_sb[:, k, span(c)], w[:, k, :]) for k in range(KT)])
                        j += 1
            emptied(pe, "dft", 16)
            for j in range(8):
                c, n = j // 2, slice((j % 2) * HALF, (j % 2 + 1) * HALF)
                jobs_mm(pe, "fu", j, 4, bank(j % 4), [(dftc[:, 0:P], pq[:, 0, c, n]), (dftc[:, P:2 * P], pq[:, 1, c, n])])
            emptied(pe, "fu", 8)
            for qk, key in enumerate("qk"):
                w = tile_ready(pe, key)
                for h in range(NH):
                    u = qk * NH + h
                    if u >= 2:
                        pe.wait_ge(S("qk_pad"), u - 1)
                    b = 3 * (u % 2)
                    for n in range(2):
                        mm = group(pe, bank(b + n), [(w[:, k, span(h)], hT[:, k, n * HALF:(n + 1) * HALF]) for k in range(KT)])
                    if qk:
                        mm = group(pe, bank(b + 2)[:, 0:CTX], [(w[:, k, span(h)], hcT[:, k, :]) for k in range(KT)])
                    mm.then_inc(S("qk_mm"), 1)
            pe.wait_ge(S("qk_pad"), 8)
            w = tile_ready(pe, "v")
            for c in range(NCH):
                src = hcT[:, :, span(c)] if c < CT else hT[:, :, span(c - CT)]
                mm = jobs_mm(pe, "v", c, 4, bank(c % 4), [(src[:, k, :], w[:, k, :]) for k in range(KT)])
            emptied(pe, "v", NCH)
            for i in range(2):
                lw = lambda k: wgate[:, (k * 2 + i) * NG:(k * 2 + i + 1) * NG]
                group(pe, bank(3 * i)[0:NG, 0:CTX], [(lw(k), hcT[:, k, :]) for k in range(KT)])
                for n in range(2):
                    mm = group(pe, bank(3 * i + 1 + n)[0:NG, :], [(lw(k), hT[:, k, n * HALF:(n + 1) * HALF]) for k in range(KT)])
            mm.then_inc(S("gate_mm"), 1)
            pe.wait_ge(S("rows"), 1)
            for c in range(NCH):
                if c >= 2:
                    pe.wait_ge(S("cols"), c - 1)
                for i, r in enumerate((rI, rF, rC, rM)):
                    mm = pe.transpose(bank(c % 2)[:, i * NG:(i + 1) * NG], r[:, span(c)], ident[0:NG, 0:NG])
                mm.then_inc(S("cols_mm"), 1)
            for d in range(2):
                for h in range(NH):
                    e = P - 1 if d == 0 else 0
                    mm = pe.matmul(bank(2)[:, (4 * d + h) * NCH:(4 * d + h + 1) * NCH],
                                   sel[:, (4 * d + h) * P:(4 * d + h + 1) * P], rC[:, e:TTOT:P], start=True, stop=True)
            mm.then_inc(S("dn_mm"), 1)
            pe.wait_ge(S("dn"), 1)
            pe.wait_ge(S("cols"), NCH)
            if stop < 4:
                return
            pe.wait_ge(S("c_zero"), 2)
            for i, (d, c, has) in enumerate(steps):
                no = outs_before[i]
                if has:
                    x0 = c - CT
                    if no >= 1:
                        pe.wait_ge(S("scan_se"), no)
                        pe.wait_ge(S("scan_e"), 4 * no)
                    for h in range(NH):
                        mm = pe.matmul(bank(0)[:, span(h)], ksrc(h, c), qT[:, h, span(x0)], start=True, stop=True)
                    mm.then_inc(S("scan_s"), 1)
                    pe.matmul(bank(1), identb[:], maskb[:, d * NH * P:(d + 1) * NH * P], start=True, stop=False, skip_group_check=True)
                    for h in range(NH):
                        mm = pe.matmul(bank(1)[:, span(h)], sel[:, (4 * d + h) * P:(4 * d + h + 1) * P], rR[:, span(c)],
                                       start=False, stop=(h == NH - 1), skip_group_check=True)
                    mm.then_inc(S("scan_r"), 1)
                if i >= 1:
                    pe.wait_ge(S("scan_c"), 4 * i)
                for h in range(NH):
                    mm = pe.transpose(bank(2)[:, span(h)], ksrc(h, c), ident[:])
                mm.then_inc(S("scan_kt"), 1)
                if has:
                    if no >= 1:
                        pe.wait_ge(S("scan_o"), 4 * no)
                    for h in range(NH):
                        mm = pe.matmul(bank(3 + h // 2)[:, (h % 2) * VW:(h % 2 + 1) * VW], qT[:, h, span(c - CT)],
                                       Cst[:, 4 * d + h, :], start=True, stop=True)
                    pe.wait_ge(S("scan_se"), no + 1)
                    for h in range(NH):
                        mm = pe.matmul(bank(5 + h // 2)[:, (h % 2) * VW:(h % 2 + 1) * VW], se[:, no % 2, h, :],
                                       vex[:, c, h, :], start=True, stop=True)
                    mm.then_inc(S("scan_u"), 1)
                pe.wait_ge(S("scan_kw"), 4 * (i + 1))
                for h in range(NH):
                    o = bank(7)[:, h * VW:(h + 1) * VW] if h < 3 else bank(2)[:, 0:VW]
                    mm = pe.matmul(o, kw[:, i % 2, h, :], vex[:, c, h, :], start=True, stop=True)
                mm.then_inc(S("scan_d"), 1)
            pe.wait_ge(S("scan_c"), 4 * len(steps))
            pe.wait_ge(S("scan_o"), 4 * 2 * TT)
            pe.wait_ge(S("scan_out"), 2 * TT)
            w = tile_ready(pe, "o")
            for j in range(8):
                h, n = j // 2, slice((j % 2) * HALF, (j % 2 + 1) * HALF)
                pe_w = [(w[:, k, span(h)], hT[:, k, n]) for k in range(KT)]
                if j >= 4:
                    pe.wait_ge(S("o_ev"), j - 3)
                mm = group(pe, bank(j % 4), pe_w)
                mm.then_inc(S("o_mm"), 1)
            for t in range(TT):
                if t >= 2:
                    pe.wait_ge(S("hm_ev"), t - 1)
                for h in range(NH):
                    mm = pe.transpose(bank(4 + t % 2)[:, span(h)], hsum[:, t, span(h)], ident[:])
                mm.then_inc(S("hm_mm"), 1)
            pe.wait_ge(S("hm_ev"), TT)
            pe.wait_ge(S("o_ev"), 8)
            pe.wait_ge(S("fu_in"), 16)
            j = 0
            for m in range(2):
                fm, b1, b2 = (tile_ready(pe, (n, m)) for n in ("fm", "br1", "br2"))
                for c in range(4):
                    for n in range(2):
                        b, ns = 4 * (j % 2), slice(n * HALF, (n + 1) * HALF)
                        if j >= 2:
                            pe.wait_ge(S("mg_sig"), 2 * (j - 1))
                            pe.wait_ge(S("mg_mul"), 2 * (j - 1))
                        group(pe, bank(b), [(b1[:, k, span(c)], hT[:, k, ns]) for k in range(KT)])
                        group(pe, bank(b + 1), [(b2[:, k, span(c)], hT[:, k, ns]) for k in range(KT)]).then_inc(S("mg_br"), 1)
                        group(pe, bank(b + 2), [(fm[:, k, span(c)], fuR[:, k, ns]) for k in range(4)])
                        mm = group(pe, bank(b + 3), [(fm[:, 4 + k, span(c)], hmT[:, k, ns]) for k in range(4)])
                        mm.then_inc(S("mg_y"), 1)
                        j += 1
            pe.wait_ge(S("mg_sig"), 32)
            pe.wait_ge(S("mg_mul"), 32)
            pe.wait_ge(S("mg_add"), 16)
            if stop < 7:
                return
            for m in range(2):
                w = tile_ready(pe, ("wo", m))
                for t in range(TT):
                    j = m * TT + t
                    if j >= 4:
                        pe.wait_ge(S("wo_ev"), before("wo_ev") + j - 3)
                    group(pe, bank(j % 4), [(mT[:, k, span(t)], w[:, k, :]) for k in range(KT)]).then_inc(S("wo_mm"), 1)
            pe.wait_ge(S("wo_ev"), before("wo_ev") + 2 * TT)
            norm_pe(pe, "n2", TT)
            normed(pe, "n2", TT)
            for t in range(TT):
                mm = group(pe, bank(0)[:, t * NEXP:(t + 1) * NEXP],
                           [(h2T[:, k, span(t)], wrt[:, k * NEXP:(k + 1) * NEXP]) for k in range(KT)])
            mm.then_inc(S("logits"), 1)
            pe.wait_ge(S("aff"), 1)
            for t in range(TT):
                mm = pe.transpose(bank(1 + t // 4)[0:NEXP, (t % 4) * P:(t % 4 + 1) * P], aff[:, t, :], ident[:])
            mm.then_inc(S("affT"), 1)
            pe.wait_ge(S("topk"), 1)
            pe.transpose(bank(3)[:, 0:NEXP], vals, ident[0:NEXP, 0:NEXP])
            pe.transpose(bank(3)[:, NEXP:2 * NEXP], idxf, ident[0:NEXP, 0:NEXP]).then_inc(S("picked"), 1)
            pe.wait_ge(S("route"), 1)

            def expert_tile(pe, e, j):
                pe.wait_ge(S(f"ring_full{j % RING}"), e * 64 + 32 * (10 + j // RING))
                return ringv(j % RING)

            def x_transposes(e):
                pe.wait_ge(S("moe_gat"), e * 16 + 16)
                for h in range(2):
                    for k in range(4):
                        mm = pe.transpose(bank(6 + h)[:, span(k)], xg[:, span(4 * h + k)], ident[:])
                    mm.then_inc(S("moe_xtr"), 1)

            def h_transposes(e):
                pe.wait_ge(S("moe_hid"), e * 2 + 2)
                for h in range(2):
                    for k in range(4):
                        mm = pe.transpose(bank(6 + h)[:, span(k)], hid[:, span(4 * h + k)], ident[:])
                    mm.then_inc(S("moe_htr"), 1)

            def gate_up(e, tiles_of):
                pe.wait_ge(S("moe_xevA"), e + 1)
                pe.wait_ge(S("moe_xevD"), e + 1)
                for i in range(4):
                    w = tiles_of(i)
                    group(pe, bank(i), [(xsT[:, k, :], w[:, k, :]) for k in range(KT)]).then_inc(S(("moe_g", "moe_u")[i // 2]), 1)

            def down(e, tiles_of):
                pe.wait_ge(S("moe_hevA"), e + 1)
                pe.wait_ge(S("moe_hevD"), e + 1)
                for i in range(2):
                    w = tiles_of(i)
                    group(pe, bank(4 + i), [(hidT[:, k, :], w[:, k, :]) for k in range(KT)]).then_inc(S("moe_d"), 1)

            def turn(e, more):
                pe.wait_ge(S("moe_sil"), e * 2)
                pe.wait_ge(S("moe_hid"), e * 2)
                gate_up(e, lambda i: expert_tile(pe, e, i))
                if not isinstance(e, int) or e >= 2:
                    pe.wait_ge(S("moe_y"), e * 2 - 2)
                down(e - 1, lambda i: expert_tile(pe, e, 4 + i))
                if more:
                    x_transposes(e + 1)
                    pe.wait_ge(S("moe_xevA"), e + 2)
                    pe.wait_ge(S("moe_xevD"), e + 2)
                h_transposes(e)

            x_transposes(0)
            gate_up(0, lambda i: tile_ready(pe, (("gate", "up")[i // 2], 0, i % 2)))
            x_transposes(1)
            pe.wait_ge(S("moe_xevA"), 2)
            pe.wait_ge(S("moe_xevD"), 2)
            h_transposes(0)
            turn(1, True)
            with pe.Fori(2, NEXP - 1) as e:
                turn(e, True)
            turn(NEXP - 1, False)
            pe.wait_ge(S("moe_y"), 2 * NEXP - 2)
            down(NEXP - 1, lambda i: tile_ready(pe, ("down", NEXP - 1, i)))
            if stop < 8:
                return

            def qk_pe(key):
                layer, _, ncol, _ = QK[key]
                w = tile_ready(pe, key)
                for t in range(TT + 1):
                    if t < TT:
                        if t >= 3:
                            pe.wait_ge(S(key + "_zn"), before(key + "_zn") + t - 2)
                            if key == "ck":
                                pe.wait_ge(S("cv_ev"), t - 2)
                        wd = 256 if key == "ck" else HALF
                        group(pe, bank(t % 3)[:, 0:wd], [(H2[layer][:, k, span(t)], w[:, k, 0:wd]) for k in range(KT)]).then_inc(S(key + "_z"), 1)
                    if t >= 1:
                        u = t - 1
                        pe.wait_ge(S(key + "_zn"), before(key + "_zn") + u + 1)
                        if u >= 2:
                            pe.wait_ge(S(key + "_evA"), before(key + "_evA") + u - 1)
                        for c in range(ncol // P):
                            mm = pe.transpose(bank(3 + u % 2)[:, span(c)], zn[u % 2][:, span(c)], ident[:])
                        mm.then_inc(S(key + "_tr"), 1)
                pe.wait_ge(S(key + "_evA"), before(key + "_evA") + TT)

            def v_pe(key, layer):
                w = tile_ready(pe, key)
                for t in range(TT):
                    jobs_mm(pe, key, t, 4, bank(t % 4), [(H2[layer][:, k, span(t)], w[:, k, :]) for k in range(KT)])
                emptied(pe, key, TT)

            def attn_pe(name):
                at = ATT[name]

                def scores(g):
                    for i, (c, h, b, qc, row, kc, k0, nk) in enumerate(at.groups[g]):
                        v = g * at.comps + i
                        if v >= 2:
                            pe.wait_ge(S(name + "_s"), before(name + "_s") + v - 1)
                        for m in range((nk + 3) // 4):
                            n = min(4, nk - 4 * m) * P
                            o = bank(2 * (v % 2) + m)[:, 0:n]
                            last = name == "B" and m == (nk - 1) // 4
                            mm = pe.matmul(o, qT2[row:row + HD, qc, span(b)], kT2[row:row + HD, kc, (k0 + 4 * m) * P:(k0 + 4 * m) * P + n],
                                           start=True, stop=not last, skip_group_check=last)
                            if last:
                                mm = pe.matmul(o[:, n - P:n], identb[:], maskb[:, NH * P:NH * P + P], start=False, stop=True,
                                               skip_group_check=True)
                        mm.then_inc(S(name + "_qk"), 1)

                def transposes(g):
                    nk, v = at.groups[g][0][7], g * at.comps
                    if name == "A":
                        pe.wait_ge(S("A_w"), before("A_w") + g + 1)
                    else:
                        pe.wait_ge(S(name + "_e"), before(name + "_e") + g + 1)
                    if g >= 1:
                        pe.wait_ge(S(name + "_wevA"), before(name + "_wevA") + g)
                        if at.big[g]:
                            pe.wait_ge(S(name + "_wevD"), before(name + "_wevD") + at.big[g])
                    sbuf = SBUFS[name][v % len(SBUFS[name])]
                    for i in range(nk):
                        mm = pe.transpose(bank(4 + i // 4)[:, span(i % 4)], sbuf[:, span(i)], ident[:])
                    mm.then_inc(S(name + "_tr"), 1)

                def outputs(g):
                    c, h, b, qc, row, kc, k0, nk = at.groups[g][0]
                    pe.wait_ge(S(name + "_wevA"), before(name + "_wevA") + g + 1)
                    if at.big[g + 1]:
                        pe.wait_ge(S(name + "_wevD"), before(name + "_wevD") + at.big[g + 1])
                    if g >= 1:
                        pe.wait_ge(S(name + "_o"), before(name + "_o") + g)
                    vc = {"A": c * P, "B": c * P + h * HD, "C": (2 * c + h) // 4 * HD, "D": c * P + h * HD}[name]
                    for i in range(nk):
                        mm = pe.matmul(bank(6)[:, 0:at.dv], wT[g % 2][:, i, :], v2[:, k0 + i, vc:vc + at.dv], start=(i == 0), stop=(i == nk - 1))
                    mm.then_inc(S(name + "_pv"), 1)

                def finish(c):
                    if name == "A":
                        pe.wait_ge(S("A_on"), before("A_on") + c + 1)
                    else:
                        pe.wait_ge(S(name + "_o"), before(name + "_o") + at.last[c] + 1)
                    for m in range(2):
                        if c or m:
                            pe.wait_ge(S(name + "_mix"), before(name + "_mix") + 2 * c + m)
                        for b in range(4):
                            mm = pe.transpose(bank(7)[:, span(b)], obuf[c % 2][:, 4 * m + b, :], ident[:])
                        mm.then_inc(S(name + "_otr"), 1)

                for a, b, c, done in at.steps():
                    if a is not None:
                        scores(a)
                    if b is not None:
                        transposes(b)
                    if c is not None:
                        outputs(c)
                    for chunk in done:
                        finish(chunk)
                pe.wait_ge(S(name + "_mix"), before(name + "_mix") + 8)

            def gates_pe(key, layer):
                w = tile_ready(pe, key)
                for j in range(8):
                    c, n = j // 2, slice((j % 2) * HALF, (j % 2 + 1) * HALF)
                    if j >= 4:
                        pe.wait_ge(S(key + "_sg"), before(key + "_sg") + j - 3)
                    group(pe, bank(j % 4), [(w[:, k, span(c)], H2[layer][:, k, n]) for k in range(KT)]).then_inc(S(key + "_mm"), 1)
                pe.wait_ge(S(key + "_sg"), before(key + "_sg") + 8)

            def out_pe(layer):
                pe.wait_ge(S(("bg", "dg")[layer] + "_mul"), before(("bg", "dg")[layer] + "_mul") + 8)
                pe.wait_ge(S(("ag", "cg")[layer] + "_mul"), before(("ag", "cg")[layer] + "_mul") + 8)
                for m in range(2):
                    w = tile_ready(pe, ("out", layer, m))
                    for t in range(TT):
                        j = m * TT + t
                        if j >= 4:
                            pe.wait_ge(S(f"wo{layer}_ev"), before(f"wo{layer}_ev") + j - 3)
                        group(pe, bank(j % 4), [(M2[layer][:, k, span(t)], w[:, k, :]) for k in range(KT)]).then_inc(S(f"wo{layer}_mm"), 1)
                pe.wait_ge(S(f"wo{layer}_ev"), before(f"wo{layer}_ev") + 2 * TT)

            pe.wait_ge(S("const2"), 16 * 6)
            norm_pe(pe, "n3", TT)
            normed(pe, "n3", TT)
            qk_pe("aq")
            qk_pe("ak")
            v_pe("av", 0)
            attn_pe("A")
            for n in range(2):
                mm = group(pe, bank(n)[0:8, :], [(wbf[:, 8 * k:8 * k + 8], H2[0][:, k, n * HALF:(n + 1) * HALF]) for k in range(KT)])
            mm.then_inc(S("forget_mm"), 1)
            pe.wait_ge(S("ncum_out"), 16)
            qk_pe("bq")
            qk_pe("bk")
            v_pe("bv", 0)
            attn_pe("B")
            gates_pe("ag", 0)
            gates_pe("bg", 0)
            out_pe(0)
            norm_pe(pe, "n4", TT)
            normed(pe, "n4", TT)
            qk_pe("cq")
            qk_pe("ck")
            attn_pe("C")
            qk_pe("dq")
            qk_pe("dk")
            v_pe("dv", 1)
            attn_pe("D")
            gates_pe("cg", 1)
            gates_pe("dg", 1)
            out_pe(1)

        @block.scalar
        def _(act):
            link = Chain(act, "act_own")
            consts(act)
            act.activation(csil[:], cT[:], ACT.Silu).then_inc(S("csil"), 1)
            evac(act, "ada", 12, lambda j: copy(act, adarow[:, j * HALF:(j + 1) * HALF], bank(j % 2)[0:2, :]))
            act.wait_ge(S("mod"), 1)
            norm_act(act, link, *NX)
            norm_act(act, link, *NC)
            evac(act, "u", 8, lambda j: copy(act, u_sb[:, j, :], bank(j % 4)))
            evac(act, "dft", 16, lambda j: copy(act, pq[:, (j // 4) % 2, j % 4, (j // 8) * HALF:(j // 8 + 1) * HALF], bank(j % 4)))
            evac(act, "fu", 8, lambda j: copy(act, fuT[:, j // 2, (j % 2) * HALF:(j % 2 + 1) * HALF], bank(j % 4)))
            act.wait_ge(S("pad_zero"), 4)
            for u in range(9):
                if u < 8:
                    act.wait_ge(S("qk_mm"), u + 1)
                    if u >= 2:
                        act.wait_ge(S("qk_conv"), u - 1)
                    grid = pads[u % 2].rearrange("p (y x) -> p y x", x=PADW)
                    for n in range(2):
                        ins = act.activation(grid[:, 1 + 8 * n:9 + 8 * n, 1:1 + GRID_W],
                                             bank(3 * (u % 2) + n).rearrange("p (y x) -> p y x", x=GRID_W), ACT.Copy)
                    if u >= 4:
                        ins = act.activation(cpads[u % 2][:, 1:1 + CTX], bank(3 * (u % 2) + 2)[:, 0:CTX], ACT.Copy)
                    ins.then_inc(S("qk_pad"), 1)
                if u >= 1:
                    v = u - 1
                    act.wait_ge(S("qk_conv"), v + 1)
                    if v == 0:
                        emptied(act, "fu", 8)
                    dst = (qT if v < 4 else kT)[:, v % 4, :]
                    ins = act.activation(dst, accs[v % 2], ACT.Silu)
                    if v >= 4:
                        ins = act.activation(kcT[:, v - 4, :], caccs[v % 2], ACT.Silu)
                    ins.then_inc(S("qk_silu"), 1)
            act.wait_ge(S("fu_out"), 16)
            evac(act, "v", NCH, lambda j: copy(act, vex[:, j, :, 0:DH], bank(j % 4).rearrange("p (h n) -> p h n", h=NH)))
            act.wait_ge(S("gate_mm"), 1)
            act.wait_ge(S("qk_silu"), 8)
            for i, r in enumerate((rI, rM)):
                link(act.activation(r[:, 0:CTX], bank(3 * i)[0:NG, 0:CTX], ACT.Identity, bias=bgate[0:NG, i:i + 1]))
                link(act.activation(r[:, CTX:TTOT], psum[0:NG, (3 * i + 1) * HALF:(3 * i + 3) * HALF], ACT.Identity,
                                    bias=bgate[0:NG, i:i + 1]))
            link(act.activation(rC, rM, ACT.Abs))
            link(act.activation(rC, rC, ACT.Exp, scale=-1.0))
            act.activation(rC, rC, ACT.Ln, bias=onec[0:NG, 0:1]).then_inc(S("gates"), 1)
            act.wait_ge(S("gate_rows"), 1)
            for c in range(NCH):
                act.activation(rF[:, span(c)], rI[:, span(c)], ACT.Exp, bias=stat[0:NG, 20 + c:21 + c])
                act.activation(rC[:, span(c)], rR[:, span(c)], ACT.Exp, bias=stat[0:NG, 40 + c:41 + c])
            act.activation(rM, rM, ACT.Exp, scale=-1.0).then_inc(S("rows"), 1)
            if stop < 4:
                return
            act.wait_ge(S("c_zero"), 2)
            for i, (d, c, has) in enumerate(steps):
                no = outs_before[i]
                act.wait_ge(S("scan_kt"), i + 1)
                if i >= 2:
                    act.wait_ge(S("scan_d"), i - 1)
                for h in range(NH):
                    g = chain_row(d, h)
                    act.activation(kw[:, i % 2, h, :], bank(2)[:, span(h)], ACT.Copy,
                                   scale=colv[:, c, 1, g:g + 1]).then_inc(S("scan_kw"), 1)
                if has:
                    act.wait_ge(S("scan_r"), no + 1)
                    if no >= 2:
                        act.wait_ge(S("scan_se"), no - 1)
                    for h in range(NH):
                        g = chain_row(d, h)
                        act.activation(ee[:, no % 2, h, :], bank(1)[:, span(h)], ACT.Exp,
                                       bias=colv[:, c, 0, g:g + 1]).then_inc(S("scan_e"), 1)
            act.wait_ge(S("scan_out"), 2 * TT)
            for j in range(8):
                act.wait_ge(S("o_mm"), j + 1)
                act.activation(oT[:, j // 2, (j % 2) * HALF:(j % 2 + 1) * HALF], bank(j % 4), ACT.Sigmoid).then_inc(S("o_ev"), 1)
            for j in range(16):
                act.wait_ge(S("mg_br"), j + 1)
                if j >= 2:
                    act.wait_ge(S("mg_mul"), 2 * (j - 1))
                for i in range(2):
                    act.activation(sg[:, j % 2, i, :], bank(4 * (j % 2) + i), ACT.Sigmoid).then_inc(S("mg_sig"), 1)
            if stop < 7:
                return
            act.wait_ge(S("mg_add"), 16)
            norm_act(act, link, *N2)
            act.wait_ge(S("lmax"), 1)
            for t in range(TT):
                act.activation(aff[:, t, :], bank(0)[:, t * NEXP:(t + 1) * NEXP], ACT.Exp, bias=lmax[:, t:t + 1],
                               accum_out=lsum[:, t:t + 1]).then_inc(S("lexp"), 1)

            def x_evac(e):
                act.wait_ge(S("moe_xtr"), e * 2 + 1)
                for k in range(4):
                    ins = act.activation(xsT[:, k, :], bank(6)[:, span(k)], ACT.Identity, bias=adaT[:, 3 * KT + k:3 * KT + k + 1],
                                         scale=mod[:, 2 * KT + k:2 * KT + k + 1])
                ins.then_inc(S("moe_xevA"), 1)

            def silu_gate(e):
                for m in range(2):
                    act.wait_ge(S("moe_g"), e * 2 + m + 1)
                    act.activation(sgate[:, m * HALF:(m + 1) * HALF], bank(m), ACT.Silu).then_inc(S("moe_sil"), 1)

            def h_evac(e):
                act.wait_ge(S("moe_htr"), e * 2 + 1)
                act.activation(hd[:, 0:HALF], bank(6), ACT.Copy).then_inc(S("moe_hevA"), 1)

            x_evac(0)
            silu_gate(0)
            x_evac(1)
            h_evac(0)
            with act.Fori(1, NEXP - 1) as e:
                act.wait_ge(S("moe_hid"), e * 2)
                silu_gate(e)
                x_evac(e + 1)
                h_evac(e)
            act.wait_ge(S("moe_hid"), 2 * NEXP - 2)
            silu_gate(NEXP - 1)
            h_evac(NEXP - 1)
            act.wait_ge(S("x2_in"), 16)
            for t in range(TT):
                if t:
                    act.wait_ge(S("nf_sq"), t)
                act.activation(sq_buf, x1[:, t, :], ACT.Square, accum_out=stat[:, t:t + 1]).then_inc(S("nf_sq"), 1)
            act.wait_ge(S("nf_sq"), TT)
            act.activation(stat[:, 16:16 + TT], stat[:, 0:TT], ACT.Sqrt, bias=epsc[:, 0:1], scale=1.0 / D).then_inc(S("nf_rt"), 1)
            if stop < 8:
                return

            def qk_act(key):
                _, g, ncol, dst = QK[key]
                nh = ncol // HD
                for t in range(TT + 2):
                    if t < TT:
                        act.wait_ge(S(key + "_z"), before(key + "_z") + t + 1)
                        if t >= 2:
                            act.wait_ge(S(key + "_ss"), before(key + "_ss") + t - 1)
                        act.activation(sqz[t % 2][:, 0:ncol], bank(t % 3)[:, 0:ncol], ACT.Square).then_inc(S(key + "_sq"), 1)
                    if 1 <= t <= TT:
                        u = t - 1
                        act.wait_ge(S(key + "_ss"), before(key + "_ss") + u + 1)
                        act.activation(qst[:, 24 * (u % 2) + 8:24 * (u % 2) + 8 + nh], qst[:, 24 * (u % 2):24 * (u % 2) + nh], ACT.Sqrt,
                                       bias=epsc[:, 0:1], scale=1.0 / HD).then_inc(S(key + "_rt"), 1)
                    if t >= 2:
                        u = t - 2
                        act.wait_ge(S(key + "_tr"), before(key + "_tr") + u + 1)
                        nc4 = ncol // P
                        act.activation(dst[:, 0:nc4, span(u)], bank(3 + u % 2)[:, 0:ncol].rearrange("p (c n) -> p c n", c=nc4), ACT.Copy,
                                       scale=gcol[:, g:g + 1]).then_inc(S(key + "_evA"), 1)

            def attn_act(name):
                at = ATT[name]
                nbuf = len(SBUFS[name])

                def weights(g):
                    for i, (c, h, b, qc, row, kc, k0, nk) in enumerate(at.groups[g]):
                        v = g * at.comps + i
                        act.wait_ge(S(name + "_s"), before(name + "_s") + v + 1)
                        sv = SBUFS[name][v % nbuf][:, 0:nk * P]
                        act.activation(sv, sv, ACT.Exp, bias=nmx[:, v % 8:v % 8 + 1], scale=-1.0,
                                       accum_out=esum[:, v % 8:v % 8 + 1]).then_inc(S(name + "_e"), 1)
                        if name == "C":
                            hd_ = 2 * c + h
                            act.activation(esk[:, v % 8:v % 8 + 1], sinkb[:, hd_:hd_ + 1], ACT.Exp,
                                           bias=nmx[:, v % 8:v % 8 + 1]).then_inc(S("C_sink"), 1)

                def empty(g):
                    nk = at.groups[g][0][7]
                    act.wait_ge(S(name + "_tr"), before(name + "_tr") + g + 1)
                    n = min(4, nk)
                    act.activation(wT[g % 2][:, 0:n, :], bank(4)[:, 0:n * P].rearrange("p (k n) -> p k n", k=n), ACT.Copy).then_inc(S(name + "_wevA"), 1)

                def squares(c):
                    act.wait_ge(S("A_o"), before("A_o") + at.last[c] + 1)
                    for b in range(TT):
                        if c or b:
                            act.wait_ge(S("A_osq"), TT * c + b)
                        act.activation(xsq, obuf[c % 2][:, b, :], ACT.Square,
                                       accum_out=qst[:, b:b + 1]).then_inc(S("A_osq"), 1)
                    act.wait_ge(S("A_osq"), TT * (c + 1))
                    act.activation(qst[:, 8:16], qst[:, 0:8], ACT.Sqrt, bias=epsc[:, 0:1], scale=1.0 / (2 * HD)).then_inc(S("A_ort"), 1)

                def mix(c):
                    for m in range(2):
                        act.wait_ge(S(name + "_otr"), before(name + "_otr") + 2 * c + m + 1)
                        act.activation(M2[at.layer][:, at.mix0 + c, m * HALF:(m + 1) * HALF], bank(7), ACT.Copy,
                                       scale=(gcol[:, 13:14] if name == "A" else 1.0)).then_inc(S(name + "_mix"), 1)

                for a, b, c, done in at.steps():
                    if a is not None:
                        weights(a)
                    if b is not None:
                        empty(b)
                    for chunk in done:
                        if name == "A":
                            squares(chunk)
                        mix(chunk)

            def gates_act(key, layer):
                for j in range(8):
                    act.wait_ge(S(key + "_mm"), before(key + "_mm") + j + 1)
                    if before(key + "_mul") + j >= 2:
                        act.wait_ge(S(key + "_mul"), before(key + "_mul") + j - 1)
                    act.activation(sgt[j % 2], bank(j % 4), ACT.Silu).then_inc(S(key + "_sg"), 1)

            def v_act(key):
                evac(act, key, TT, lambda j: copy(act, v2[:, j, :], bank(j % 4)))

            act.wait_ge(S("const2"), 16 * 6)
            act.wait_ge(S("lam_sum"), 2)
            act.activation(lsums, lsums, ACT.Exp).then_inc(S("lam_exp"), 1)
            act.wait_ge(S("n3_start"), before("n3_start") + 1)
            norm_act(act, link, *N3)
            qk_act("aq")
            qk_act("ak")
            v_act("av")
            attn_act("A")
            act.wait_ge(S("forget_mm"), 1)
            link(act.activation(frow[0], psum[0:8, 0:2 * HALF], ACT.Identity, bias=bbf[0:8, 0:1]))
            link(act.activation(frow[1], frow[0], ACT.Abs))
            link(act.activation(frow[1], frow[1], ACT.Exp, scale=-1.0))
            act.activation(frow[1], frow[1], ACT.Ln, bias=onec[0:8, 0:1]).then_inc(S("forget_ln"), 1)
            qk_act("bq")
            qk_act("bk")
            v_act("bv")
            attn_act("B")
            gates_act("ag", 0)
            gates_act("bg", 0)
            act.wait_ge(S("bg_mul"), before("bg_mul") + 8)
            norm_act(act, link, *N4)
            qk_act("cq")
            qk_act("ck")
            attn_act("C")
            qk_act("dq")
            qk_act("dk")
            v_act("dv")
            attn_act("D")
            gates_act("cg", 1)
            gates_act("dg", 1)

        @block.vector
        def _(dve):
            link = Chain(dve, "dve_own")
            consts(dve)
            link(dve.tensor_copy(identb[:], ident[:]))
            link(dve.tensor_copy(maskb[:], mask_in))
            evac(dve, "ada", 12, lambda j: copy(dve, adarow[:, j * HALF:(j + 1) * HALF], bank(j % 2)[0:2, :]))
            dve.wait_ge(S("adaT_mm"), 1)
            av = bank(2)[:, 0:96].rearrange("p (c b) -> p c b", b=2)
            for b in range(2):
                link(dve.tensor_tensor(adaT[:, b * 48:(b + 1) * 48], av[:, :, b], badaT[:], ALU.add))
            for i, (g, s) in enumerate(((0, KT), (0, 48 + KT), (1, 4 * KT))):
                link(dve.scalar_tensor_tensor(mod[:, i * KT:(i + 1) * KT], adaT[:, s:s + KT], 1.0,
                                              gT[:, g * KT:(g + 1) * KT], ALU.add, ALU.mult))
            dve.memset(stat[:, 63:64], 0.0).then_inc(S("mod"), 1)
            norm_dve(dve, link, *NX)
            norm_dve(dve, link, *NC)
            evac(dve, "u", 8, lambda j: copy(dve, u_sb[:, j, :], bank(j % 4)))
            evac(dve, "dft", 16, lambda j: copy(dve, pq[:, (j // 4) % 2, j % 4, (j // 8) * HALF:(j // 8 + 1) * HALF], bank(j % 4)))
            evac(dve, "fu", 8, lambda j: copy(dve, fuT[:, j // 2, (j % 2) * HALF:(j % 2 + 1) * HALF], bank(j % 4)))
            emptied(dve, "dft", 16)
            for i in range(2):
                dve.memset(pads[i], 0.0).then_inc(S("pad_zero"), 1)
                dve.memset(cpads[i], 0.0).then_inc(S("pad_zero"), 1)
            for u in range(8):
                dve.wait_ge(S("qk_pad"), u + 1)
                if u >= 2:
                    dve.wait_ge(S("qk_silu"), u - 1)
                grid = pads[u % 2].rearrange("p (y x) -> p y x", x=PADW)
                acc = accs[u % 2].rearrange("p (y x) -> p y x", x=GRID_W)
                wc = lambda t: wconv[:, u * 9 + t:u * 9 + t + 1]
                tap = lambda t: grid[:, t // 3:t // 3 + GRID_H, t % 3:t % 3 + GRID_W]
                link(dve.tensor_scalar(acc, tap(0), wc(0), None, ALU.mult))
                if u >= 4:
                    ca, cp = caccs[u % 2], cpads[u % 2]
                    link(dve.tensor_scalar(ca, cp[:, 0:CTX], wc(3), None, ALU.mult))
                    for t in (4, 5):
                        link(dve.scalar_tensor_tensor(ca, cp[:, t - 3:t - 3 + CTX], wc(t), ca, ALU.mult, ALU.add))
                for t in range(1, 8):
                    link(dve.scalar_tensor_tensor(acc, tap(t), wc(t), acc, ALU.mult, ALU.add))
                dve.scalar_tensor_tensor(acc, tap(8), wc(8), acc, ALU.mult, ALU.add).then_inc(S("qk_conv"), 1)
            dve.wait_ge(S("fu_out"), 16)
            dve.memset(vex[:, :, :, DH:VW], 1.0).then_inc(S("v_one"), 1)
            evac(dve, "v", NCH, lambda j: copy(dve, vex[:, j, :, 0:DH], bank(j % 4).rearrange("p (h n) -> p h n", h=NH)))
            link(dve.memset(ones_row, 1.0))
            dve.wait_ge(S("gates"), 1)
            link(dve.tensor_scalar(rM, rM, 0.0, None, ALU.min))
            link(dve.tensor_tensor(rF, rM, rC, ALU.subtract))
            for d in range(2):
                r = slice(0, NH) if d == 0 else slice(BWD, NG)
                sv = (lambda x: x) if d == 0 else (lambda x: x[:, ::-1])
                ends = (CTX - 1, TTOT - 1) if d == 0 else (0, CTX)
                if d == 0:
                    link(dve.memset(rM, 0.0))
                link(dve.tensor_tensor_scan(sv(rM[r, 0:CTX]), sv(rF[r, 0:CTX]), sv(rI[r, 0:CTX]), 0.0, ALU.add, ALU.max))
                link(dve.tensor_tensor_scan(sv(rM[r, CTX:TTOT]), sv(rF[r, CTX:TTOT]), sv(rI[r, CTX:TTOT]),
                                            rM[r, ends[0]:ends[0] + 1], ALU.add, ALU.max))
            link(dve.memset(rC, 0.0))
            for d in range(2):
                r = slice(0, NH) if d == 0 else slice(BWD, NG)
                sv = (lambda x: x) if d == 0 else (lambda x: x[:, ::-1])
                for c in range(NCH):
                    ins = dve.tensor_tensor_scan(sv(rC[r, span(c)]), sv(ones_row[r, :]), sv(rF[r, span(c)]), 0.0, ALU.mult, ALU.add)
                link(ins)
            link(dve.tensor_tensor(rI, rI, rC, ALU.subtract))
            link(dve.tensor_tensor(rR, rC, rM, ALU.subtract))
            link(dve.memset(stat[0:NG, 20:60], 0.0))
            for d in range(2):
                r = slice(0, NH) if d == 0 else slice(BWD, NG)
                e = P - 1 if d == 0 else 0
                link(dve.tensor_copy(stat[r, 20:20 + NCH], rR[r, e:TTOT:P]))
                if d == 0:
                    link(dve.tensor_copy(stat[r, 41:40 + NCH], rM[r, e:TTOT - P:P]))
                else:
                    link(dve.tensor_copy(stat[r, 40:41], rM[r, P:P + 1]))
                    link(dve.tensor_copy(stat[r, 42:42 + TT - 1], rM[r, CTX + P:TTOT:P]))
                    link(dve.tensor_copy(stat[r, 42 + TT - 1:42 + TT], rM[r, 0:1]))
            dve.memset(stat[:, 63:64], 0.0).then_inc(S("gate_rows"), 1)
            for c in range(NCH):
                dve.wait_ge(S("cols_mm"), c + 1)
                dve.tensor_copy(colv[:, c, :, :], bank(c % 2)[:, 0:4 * NG].rearrange("p (a g) -> p a g", a=4)).then_inc(S("cols"), 1)
            dve.wait_ge(S("dn_mm"), 1)
            dve.tensor_copy(dnb, bank(2)[:, 0:8 * NCH].rearrange("p (c n) -> p c n", c=8)).then_inc(S("dn"), 1)
            dve.wait_ge(S("cols"), NCH)
            dve.memset(Cst, 0.0).then_inc(S("c_zero"), 1)
            dve.wait_ge(S("dn"), 1)
            dve.wait_ge(S("c_zero"), 1)
            if stop < 4:
                return
            link(dve.tensor_scalar(colv[:, :, 1, :], colv[:, :, 1, :], KSC, None, ALU.mult))
            dve.memset(stat[:, 63:64], 0.0).then_inc(S("c_zero"), 1)
            for i, (d, c, has) in enumerate(steps):
                no = outs_before[i]
                if has:
                    dve.wait_ge(S("scan_s"), no + 1)
                    dve.wait_ge(S("scan_e"), 4 * (no + 1))
                    if no >= 2:
                        dve.wait_ge(S("scan_u"), no - 1)
                    dve.scalar_tensor_tensor(se[:, no % 2, :, :], bank(0).rearrange("p (h n) -> p h n", h=NH), KSC,
                                             ee[:, no % 2, :, :], ALU.mult, ALU.mult).then_inc(S("scan_se"), 1)
                    dve.wait_ge(S("scan_u"), no + 1)
                    for h in range(NH):
                        g = chain_row(d, h)
                        hs = slice((h % 2) * VW, (h % 2 + 1) * VW)
                        link(dve.tensor_scalar(ob[:, h, :], bank(3 + h // 2)[:, hs], colv[:, c, 2, g:g + 1], None, ALU.mult))
                        dve.tensor_tensor(ob[:, h, :], ob[:, h, :], bank(5 + h // 2)[:, hs], ALU.add).then_inc(S("scan_o"), 1)
                    dve.wait_ge(S("scan_o"), 4 * (no + 1))
                    g0 = chain_row(d, 0)
                    link(dve.scalar_tensor_tensor(rec, ob[:, :, DH], -1.0, colv[:, c, 3, g0:g0 + NH], ALU.mult, ALU.max))
                    link(dve.tensor_tensor(rec, rec, ob[:, :, DH], ALU.max))
                    link(dve.reciprocal(rec, rec))
                dve.wait_ge(S("scan_d"), i + 1)
                for h in range(NH):
                    o = bank(7)[:, h * VW:(h + 1) * VW] if h < 3 else bank(2)[:, 0:VW]
                    dve.scalar_tensor_tensor(Cst[:, 4 * d + h, :], Cst[:, 4 * d + h, :], dnb[:, 4 * d + h, c:c + 1], o,
                                             ALU.mult, ALU.add).then_inc(S("scan_c"), 1)
                if has:
                    hv = hsum[:, c - CT, :].rearrange("p (h n) -> p h n", h=NH)
                    first = not any(s[1] == c for s in steps[:i])
                    for h in range(NH):
                        if first:
                            ins = dve.tensor_scalar(hv[:, h, :], ob[:, h, 0:DH], rec[:, h:h + 1], None, ALU.mult)
                        else:
                            ins = dve.scalar_tensor_tensor(hv[:, h, :], ob[:, h, 0:DH], rec[:, h:h + 1], hv[:, h, :], ALU.mult, ALU.add)
                    ins.then_inc(S("scan_out"), 1)
                    dve.wait_ge(S("scan_out"), no + 1)
            dve.wait_ge(S("o_ev"), 8)
            for t in range(TT):
                dve.wait_ge(S("hm_mm"), t + 1)
                dve.tensor_tensor(hmT[:, :, span(t)], bank(4 + t % 2).rearrange("p (h n) -> p h n", h=NH), oT[:, :, span(t)],
                                  ALU.mult).then_inc(S("hm_ev"), 1)
            for j in range(16):
                dve.wait_ge(S("mg_sig"), 2 * (j + 1))
                dve.wait_ge(S("mg_y"), j + 1)
                for i in range(2):
                    dve.tensor_tensor(sgd[:, j % 2, i, :], sg[:, j % 2, i, :], bank(4 * (j % 2) + 2 + i), ALU.mult).then_inc(S("mg_mul"), 1)
                dve.wait_ge(S("mg_mul"), 2 * (j + 1))
                dve.tensor_tensor(mT[:, j // 2, (j % 2) * HALF:(j % 2 + 1) * HALF], sgd[:, j % 2, 0, :], sgd[:, j % 2, 1, :],
                                  ALU.add).then_inc(S("mg_add"), 1)
            if stop < 7:
                return
            dve.wait_ge(S("x_again"), 16)
            dve.wait_ge(S("ga1"), 16)
            for j in range(2 * TT):
                m, t = j // TT, j % TT
                ms = slice(m * HALF, (m + 1) * HALF)
                dve.wait_ge(S("wo_mm"), before("wo_mm") + j + 1)
                link(dve.tensor_tensor(x1[:, t, ms], bank(j % 4), ga1b[:, ms], ALU.mult))
                dve.tensor_tensor(x1[:, t, ms], x1[:, t, ms], x2nd[:, t, ms], ALU.add).then_inc(S("wo_ev"), 1)
            norm_dve(dve, link, *N2, stored=lambda eng, t: eng.wait_ge(S(f"xn_out{t % 2}"), 16 * (t // 2 + 1)))
            dve.wait_ge(S("logits"), 1)
            dve.tensor_reduce(lmax, bank(0)[:, 0:P].rearrange("p (t e) -> p t e", e=NEXP), AX.X, ALU.max, negate=True).then_inc(S("lmax"), 1)
            dve.wait_ge(S("lexp"), TT)
            link(dve.reciprocal(lmax, lsum))
            for t in range(TT):
                ins = dve.tensor_scalar(aff[:, t, :], aff[:, t, :], lmax[:, t:t + 1], None, ALU.mult)
            ins.then_inc(S("aff"), 1)
            dve.wait_ge(S("affT"), 1)
            link(dve.tensor_copy(affT, psum[0:NEXP, HALF:3 * HALF]))
            for r in range(CAP // 8):
                v = vals[:, 8 * r:8 * r + 8]
                link(dve.max(v, affT))
                link(dve.max_index(idx[:, 8 * r:8 * r + 8], v, affT))
                link(dve.match_replace(affT, v, affT, -1.0))
            dve.tensor_copy(idxf, idx).then_inc(S("topk"), 1)
            dve.wait_ge(S("picked"), 1)
            link(dve.tensor_copy(valc, bank(3)[:, 0:NEXP]))
            dve.tensor_copy(idxc, bank(3)[:, NEXP:2 * NEXP]).then_inc(S("route"), 1)
            dve.wait_ge(S("ga2"), 16)

            def x_evac(e):
                dve.wait_ge(S("moe_xtr"), e * 2 + 2)
                for k in range(4, 8):
                    ins = dve.tensor_scalar(xsT[:, k, :], bank(7)[:, span(k - 4)], mod[:, 2 * KT + k:2 * KT + k + 1],
                                            adaT[:, 3 * KT + k:3 * KT + k + 1], ALU.mult, ALU.add)
                ins.then_inc(S("moe_xevD"), 1)

            def hidden_of(e):
                for m in range(2):
                    ms = slice(m * HALF, (m + 1) * HALF)
                    dve.wait_ge(S("moe_sil"), e * 2 + m + 1)
                    dve.wait_ge(S("moe_u"), e * 2 + m + 1)
                    dve.tensor_tensor(hid[:, ms], sgate[:, ms], bank(2 + m), ALU.mult).then_inc(S("moe_hid"), 1)

            def h_evac(e):
                dve.wait_ge(S("moe_htr"), e * 2 + 2)
                dve.tensor_copy(hd[:, HALF:D], bank(7)).then_inc(S("moe_hevD"), 1)

            def outputs(e):
                for m in range(2):
                    ms = slice(m * HALF, (m + 1) * HALF)
                    dve.wait_ge(S("moe_d"), e * 2 + m + 1)
                    dve.scalar_tensor_tensor(yb[:, ms], bank(4 + m), valc[:, bass.ds(e, 1)], ga2b[:, ms],
                                             ALU.mult, ALU.mult).then_inc(S("moe_y"), 1)

            x_evac(0)
            hidden_of(0)
            x_evac(1)
            h_evac(0)

            def turn(e, more):
                dve.wait_ge(S("moe_htr"), e * 2)
                hidden_of(e)
                if not isinstance(e, int) or e >= 2:
                    dve.wait_ge(S("moe_sct"), e * 16 - 16)
                outputs(e - 1)
                if more:
                    x_evac(e + 1)
                h_evac(e)

            turn(1, True)
            with dve.Fori(2, NEXP - 1) as e:
                turn(e, True)
            turn(NEXP - 1, False)
            dve.wait_ge(S("moe_sct"), 16 * NEXP - 16)
            outputs(NEXP - 1)
            dve.wait_ge(S("nf_rt"), 1)
            dve.wait_ge(S("gf"), 16)
            link(dve.reciprocal(stat[:, 32:32 + TT], stat[:, 16:16 + TT]))
            for t in range(TT):
                dve.scalar_tensor_tensor(x1[:, t, :], x1[:, t, :], stat[:, 32 + t:33 + t], gfb, ALU.mult, ALU.mult).then_inc(S("xb"), 1)
            if stop < 8:
                return

            def qk_dve(key):
                _, g, ncol, dst = QK[key]
                nh = ncol // HD
                for t in range(TT + 1):
                    if t < TT:
                        dve.wait_ge(S(key + "_sq"), before(key + "_sq") + t + 1)
                        if t >= 2:
                            dve.wait_ge(S(key + "_rt"), before(key + "_rt") + t - 1)
                        dve.tensor_reduce(qst[:, 24 * (t % 2):24 * (t % 2) + nh], sqz[t % 2][:, 0:ncol].rearrange("p (h d) -> p h d", d=HD),
                                          AX.X, ALU.add).then_inc(S(key + "_ss"), 1)
                    if t >= 1:
                        u = t - 1
                        r = qst[:, 24 * (u % 2) + 16:24 * (u % 2) + 16 + nh]
                        dve.wait_ge(S(key + "_rt"), before(key + "_rt") + u + 1)
                        link(dve.reciprocal(r, qst[:, 24 * (u % 2) + 8:24 * (u % 2) + 8 + nh]))
                        if u >= 2:
                            dve.wait_ge(S(key + "_tr"), before(key + "_tr") + u - 1)
                        z, o = bank(u % 3)[:, 0:ncol], zn[u % 2][:, 0:ncol]
                        if key == "cq":
                            for hh in range(2):
                                ins = dve.tensor_tensor(o.rearrange("p (c h d) -> p h c d", c=4, h=2)[:, hh],
                                                        z.rearrange("p (h c d) -> p h c d", h=2, c=4)[:, hh],
                                                        r[:, 4 * hh:4 * hh + 4].unsqueeze(2).to_broadcast([P, 4, HD]), ALU.mult)
                        else:
                            ins = dve.tensor_tensor(o.rearrange("p (h d) -> p h d", d=HD), z.rearrange("p (h d) -> p h d", d=HD),
                                                    r.unsqueeze(2).to_broadcast([P, nh, HD]), ALU.mult)
                        ins.then_inc(S(key + "_zn"), 1)
                        if key == "ck":
                            dve.tensor_copy(v2[:, u, 0:P], bank(u % 3)[:, P:2 * P]).then_inc(S("cv_ev"), 1)

            def attn_dve(name):
                at = ATT[name]
                nbuf = len(SBUFS[name])

                def scores(g):
                    bias = bias_ready(dve, name, g)
                    for i, (c, h, b, qc, row, kc, k0, nk) in enumerate(at.groups[g]):
                        v = g * at.comps + i
                        dve.wait_ge(S(name + "_qk"), before(name + "_qk") + v + 1)
                        if v >= nbuf:
                            dve.wait_ge(S(name + "_tr"), before(name + "_tr") + (v - nbuf) // at.comps + 1)
                        o = {"A": (TT - 1 - b) * P, "B": 0, "C": (2 - nk) * P, "D": 0}[name]
                        bv = bias[:, 0:nk * P][:, ::-1] if name == "D" else bias[:, o:o + nk * P]
                        init = nsink[:, 2 * c + h:2 * c + h + 1] if name == "C" else 3.0e38
                        dve.tensor_tensor_reduce(out=SBUFS[name][v % nbuf][:, 0:nk * P],
                                                 in0=psum[:, 2 * (v % 2) * HALF:2 * (v % 2) * HALF + nk * P],
                                                 in1=bv, scale=-1.0, scalar=init, op0=ALU.add, op1=ALU.min,
                                                 accum_out=nmx[:, v % 8:v % 8 + 1]).then_inc(S(name + "_s"), 1)

                def weights(g):
                    nk, v = at.groups[g][0][7], 2 * g
                    dve.wait_ge(S("A_e"), before("A_e") + v + 2)
                    link(dve.reciprocal(rinv[:, v % 8:v % 8 + 2], esum[:, v % 8:v % 8 + 2]))
                    e0, e1 = (SBUFS[name][(v + i) % nbuf][:, 0:nk * P] for i in range(2))
                    r0, r1 = (rinv[:, (v + i) % 8:(v + i) % 8 + 1] for i in range(2))
                    link(dve.tensor_scalar(r1, r1, nlam, None, ALU.mult))
                    link(dve.tensor_scalar(e0, e0, r0, None, ALU.mult))
                    dve.scalar_tensor_tensor(e0, e1, r1, e0, ALU.mult, ALU.add).then_inc(S("A_w"), 1)

                def empty(g):
                    nk = at.groups[g][0][7]
                    if nk > 4:
                        dve.wait_ge(S(name + "_tr"), before(name + "_tr") + g + 1)
                        dve.tensor_copy(wT[g % 2][:, 4:nk, :], bank(5)[:, 0:(nk - 4) * P].rearrange("p (k n) -> p k n", n=P)).then_inc(S(name + "_wevD"), 1)

                def outputs(g):
                    c, h, b, qc, row, kc, k0, nk = at.groups[g][0]
                    r = g % 8
                    if name != "A":
                        dve.wait_ge(S(name + "_e"), before(name + "_e") + g + 1)
                        if name == "C":
                            dve.wait_ge(S("C_sink"), g + 1)
                            link(dve.tensor_tensor(esum[:, r:r + 1], esum[:, r:r + 1], esk[:, r:r + 1], ALU.add))
                        link(dve.reciprocal(rinv[:, r:r + 1], esum[:, r:r + 1]))
                    dve.wait_ge(S(name + "_pv"), before(name + "_pv") + g + 1)
                    if c >= 2:
                        dve.wait_ge(S(name + "_otr"), before(name + "_otr") + 2 * (c - 1))
                    if name == "A":
                        ins = dve.tensor_copy(obuf[c % 2][:, b, :], bank(6)[:, 0:P])
                    else:
                        ins = dve.tensor_scalar(obuf[c % 2][:, b, h * HD:(h + 1) * HD], bank(6)[:, 0:HD], rinv[:, r:r + 1], None, ALU.mult)
                    ins.then_inc(S(name + "_o"), 1)

                def complete(c):
                    dve.wait_ge(S("A_ort"), c + 1)
                    link(dve.reciprocal(qst[:, 16:24], qst[:, 8:16]))
                    for b in range(TT):
                        ins = dve.tensor_scalar(obuf[c % 2][:, b, :], obuf[c % 2][:, b, :], qst[:, 16 + b:17 + b], None, ALU.mult)
                    ins.then_inc(S("A_on"), 1)

                for a, b, c, done in at.steps():
                    if a is not None:
                        scores(a)
                    if b is not None:
                        if name == "A":
                            weights(b)
                        empty(b)
                    if c is not None:
                        outputs(c)
                    if name == "A":
                        for chunk in done:
                            complete(chunk)

            def gates_dve(key, layer):
                at = ATT[key[0].upper()]
                for j in range(8):
                    n = slice((j % 2) * HALF, (j % 2 + 1) * HALF)
                    dve.wait_ge(S(key + "_sg"), before(key + "_sg") + j + 1)
                    o = M2[layer][:, at.mix0 + j // 2, n]
                    dve.tensor_tensor(o, o, sgt[j % 2], ALU.mult).then_inc(S(key + "_mul"), 1)

            def v_dve(key):
                evac(dve, key, TT, lambda j: copy(dve, v2[:, j, :], bank(j % 4)))

            def out_dve(layer):
                dve.wait_ge(S(f"res{layer}_in"), before(f"res{layer}_in") + 16)
                for j in range(2 * TT):
                    m, t = j // TT, j % TT
                    ms = slice(m * HALF, (m + 1) * HALF)
                    dve.wait_ge(S(f"wo{layer}_mm"), before(f"wo{layer}_mm") + j + 1)
                    dve.tensor_tensor(x3[:, t, ms], bank(j % 4), R2[layer][:, t, ms], ALU.add).then_inc(S(f"wo{layer}_ev"), 1)

            dve.wait_ge(S("const2"), 16 * 6)
            for i in range(2):
                dve.tensor_tensor_reduce(out=lamx[:, i, :], in0=lamb[:, 2 * i, :], in1=lamb[:, 2 * i + 1, :], scale=1.0, scalar=0.0,
                                         op0=ALU.mult, op1=ALU.add, accum_out=lsums[:, i:i + 1]).then_inc(S("lam_sum"), 1)
            dve.wait_ge(S("lam_exp"), 1)
            link(dve.tensor_scalar(nlam, lsums[:, 1:2], lsums[:, 0:1], LAM0, ALU.subtract, ALU.subtract))
            link(dve.tensor_scalar(nsink, sinkb, -1.0, None, ALU.mult))
            for i in range(4):
                link(dve.tensor_scalar(gcol[:, 8 + i:9 + i], gcol[:, 2 * i:2 * i + 1], HD ** -0.5, None, ALU.mult))
            link(dve.tensor_scalar(gcol[:, 13:14], gcol[:, 12:13], 1.0 - LAM0, None, ALU.mult))
            dve.memset(att[:, 56:57], 0.0).then_inc(S("n3_start"), 1)
            norm_dve(dve, link, *N3)
            qk_dve("aq")
            qk_dve("ak")
            v_dve("av")
            dve.wait_ge(S("res0_out"), before("res0_out") + 16)
            dve.memset(att[:, 57:58], 0.0)
            attn_dve("A")
            dve.wait_ge(S("forget_ln"), 1)
            link(dve.tensor_scalar(frow[0], frow[0], 0.0, None, ALU.min))
            link(dve.tensor_tensor(frow[1], frow[1], frow[0], ALU.subtract))
            link(dve.memset(frow[2], 1.0))
            dve.tensor_tensor_scan(frow[0], frow[2], frow[1], 0.0, ALU.mult, ALU.add).then_inc(S("forget"), 1)
            dve.wait_ge(S("ncum_out"), 16)
            qk_dve("bq")
            qk_dve("bk")
            v_dve("bv")
            attn_dve("B")
            gates_dve("ag", 0)
            gates_dve("bg", 0)
            out_dve(0)
            dve.wait_ge(S("wo0_ev"), before("wo0_ev") + 2 * TT)
            dve.memset(att[:, 58:59], 0.0).then_inc(S("x3"), 2 * TT)
            norm_dve(dve, link, *N4)
            dve.wait_ge(S("res1_out"), before("res1_out") + 16)
            qk_dve("cq")
            qk_dve("ck")
            attn_dve("C")
            qk_dve("dq")
            qk_dve("dk")
            v_dve("dv")
            attn_dve("D")
            gates_dve("cg", 1)
            gates_dve("dg", 1)
            out_dve(1)
    return


SCRATCH = {"fu": (P, 4, D), "ada": (6 * D,), "acc": (SEQ, D), "xn": (SEQ, D), "xb": (SEQ, D), "x3": (SEQ, D), "ncum": (8, SEQ)}


def host_layout(i):
    n = np.arange(SEQ)
    ang = 2 * np.pi * ((n[:, None] * n[None, :]) % SEQ) / SEQ
    norm = 1.0 / math.sqrt(SEQ * P)
    m = np.arange(P)
    angc = 2 * np.pi * ((m[:, None] * m[None, :]) % P) / P
    w_in = i["w_in"][0]
    colT = lambda v: np.ascontiguousarray(v.reshape(-1, P).T)
    g = w_in[:, 2560:2576].reshape(D, 4, NH)
    wg = np.zeros((D, 2, NG), np.float32)
    bg = np.zeros((NG, 2), np.float32)
    for k in range(2):
        wg[:, k, 0:NH], wg[:, k, BWD:NG] = g[:, k], g[:, 2 + k]
        bg[0:NH, k], bg[BWD:NG, k] = i["b_gates"][0, k], i["b_gates"][0, 2 + k]
    sel = np.zeros((NG, 8, P), np.float32)
    for c in range(8):
        sel[c if c < NH else BWD + c - NH, c] = 1
    lower, upper = m[:, None] <= m[None, :], m[:, None] >= m[None, :]
    masks = np.stack([np.where(q, 0, NEG) for q in (lower, upper)])
    col = np.arange(SEQ)
    dist = np.abs(m[:, None] - (col[None, :] - (SEQ - P)))
    hide = (col[None, :] - (SEQ - P)) // HD > m[:, None] // HD
    slope = lambda n: 2.0 ** (-8.0 * np.arange(1, n + 1) / n)
    strip_a = np.stack([np.where(hide, NEG, -q * dist) for q in slope(4)]).astype(np.float32)
    col = np.arange(2 * P)
    dist = np.abs(m[:, None] - (col[None, :] - P))
    step = m[:, None] // HD + 2 - col[None, :] // HD
    strip_c = np.stack([np.where((step < 0) | (step > 2), NEG, -q * dist) for q in slope(8)]).astype(np.float32)
    rel = np.ascontiguousarray(np.pad(i["d_rel_bias_2"][0], ((0, 0), (64, 384)), mode="edge"))
    return {
        "x": i["x"][0], "ctx": i["ctx"][0], "w_ada": i["w_ada"][0], "w_in": w_in,
        "w_fourier": i["w_fourier"][0], "w_mlstm": i["w_mlstm"][0], "w_out": i["w_out"][0],
        "cT": np.ascontiguousarray(np.stack([i["c"][0], i["c_ctx"]]).reshape(2, KT, P).transpose(2, 1, 0)).reshape(P, -1),
        "b_adaT": colT(i["b_ada"][0]),
        "gT": np.concatenate([colT(v) for v in (i["g_norm1"][0], i["g_norm2"][0], i["even_ln_g_2"][0],
                                                i["odd_ln_g_2"][0], i["g_final"])], 1),
        "w_convT": np.ascontiguousarray(i["w_conv"][0].reshape(9, 8, P).transpose(2, 1, 0)).reshape(P, -1),
        "w_mgate": np.ascontiguousarray(wg.reshape(KT, P, 2, NG).transpose(1, 0, 2, 3)).reshape(P, -1),
        "w_routerT": np.ascontiguousarray(i["w_router"][0].reshape(KT, P, NEXP).transpose(1, 0, 2)).reshape(P, -1),
        "w_gate": i["w_gate_e"][0], "w_up": i["w_up_e"][0], "w_down": i["w_down_e"][0], "g_final": i["g_final"],
        "even_w_in": i["even_w_in_2"][0], "even_w_out": i["even_w_out_2"][0],
        "odd_w_in": i["odd_w_in_2"][0], "odd_w_out": i["odd_w_out_2"][0],
        "lams": np.concatenate([i[f"a_lambda_{n}_2"][0] for n in ("q1", "k1", "q2", "k2")]),
        "sinks": i["c_sinks_2"][0],
        "qk_gains": np.stack([np.tile(i[f"{n}_norm_g_2"][0], 2) for n in ("a_q", "a_k", "b_q", "b_k", "c_q", "c_k", "d_q", "d_k")], 1),
        "sub_gain": i["a_subln_g_2"][0].reshape(P, 1),
        "w_forget": np.ascontiguousarray(i["even_w_in_2"][0][:, 4096:4104].reshape(KT, P, 8).transpose(1, 0, 2)).reshape(P, -1),
        "b_forget": i["b_forget_bias_2"][0].reshape(8, 1),
        "strip_a": strip_a, "strip_c": strip_c, "rel": rel,
        "b_gate": bg, "sel": sel.reshape(NG, -1),
        "ident": np.eye(P, dtype=np.float32), 
        "masks": np.concatenate([np.tile(q, (1, NH)) for q in masks], 1).astype(np.float32),
        "dftc": np.concatenate([np.cos(angc), -np.sin(angc)], 1).astype(np.float32),
        "dft_cos": (np.cos(ang) * norm).astype(np.float32), "dft_sin": (np.sin(ang) * norm).astype(np.float32),
    }


def kernel(**inputs):
    import concourse.bacc as bacc
    from concourse.bass_utils import run_bass_kernel_spmd

    arrays = host_layout({n: np.asarray(v) for n, v in inputs.items()})
    nc = bacc.Bacc("TRN2", target_bir_lowering=False, num_devices=1)
    a = {n: nc.dram_tensor("in_" + n, v.shape, mybir.dt.from_np(v.dtype), kind="ExternalInput").ap() for n, v in arrays.items()}
    out = nc.dram_tensor("out", (SEQ, D), F32, kind="ExternalOutput").ap()
    scratch = {n: nc.dram_tensor("scratch_" + n, v, F32, kind="Internal").ap() for n, v in SCRATCH.items()}
    build(nc, a, out, scratch)
    r = run_bass_kernel_spmd(nc, [{"in_" + n: v for n, v in arrays.items()}], core_ids=[0])
    return r.results[0]["out"].reshape(1, SEQ, D)
```

```python
import math
from contextlib import ExitStack

import numpy as np
import concourse.bass as bass
from concourse import mybir

F32 = mybir.dt.float32
BF16 = mybir.dt.bfloat16
I32 = mybir.dt.int32
U32 = mybir.dt.uint32
ALU = mybir.AluOpType
ACT = mybir.ActivationFunctionType
AX = mybir.AxisListType

P = 128
D = 1024
SEQ = 1024
CTX = 256
KT = D // P
TT = SEQ // P
CT = CTX // P
HALF = 512
EPS = 1e-6
NH, DH = 4, 128
GRID_W = 64
GRID_H = SEQ // GRID_W
NCH = CT + TT
KSC = DH ** -0.5
NEXP, CAP = 16, 128
RING = 3
BWD = 32
NG = BWD + NH
NEG = -1e30


HD = 64
LAM0 = 0.8 - 0.6 * math.exp(0.0)


class Attn:

    def __init__(self, p, layer, mix0, comps, span, dv, kv_shared=False):
        self.p, self.layer, self.mix0, self.comps, self.dv = p, layer, mix0, comps, dv
        self.units, self.groups = [], []
        for c in range(4):
            order = [(b, h) for b in range(TT) for h in range(2)] if comps == 2 else [(b, h) for h in range(2) for b in range(TT)]
            for b, h in order:
                k0 = max(0, b - span)
                head = 2 * c + h
                qc, row = (head % 4, HD * (head // 4)) if kv_shared else (c, HD * h)
                self.units.append((c, h, b, qc, row, 0 if kv_shared else c, k0, b - k0 + 1))
        for i in range(0, len(self.units), comps):
            self.groups.append(self.units[i:i + comps])
        G = len(self.groups)
        self.G = G
        self.big = [sum(1 for g in self.groups[:u] if g[0][7] > 4) for u in range(G + 1)]
        self.last = {}
        for u, g in enumerate(self.groups):
            self.last[g[0][0]] = u
        self.per_bias = G // 4 if comps == 2 else G // 8
        self.nbias = G // self.per_bias
        self.lag = {"A": 1, "B": 2, "C": 3, "D": 3}[p]

    def steps(self):
        n = self.G
        for i in range(n + self.lag + 3):
            pick = lambda j: j if 0 <= j < n else None
            yield (pick(i), pick(i - self.lag), pick(i - self.lag - 1),
                   [c for c, u in self.last.items() if i == u + self.lag + 2])


def build(nc, a, out, scratch, stop=99):
    ctx = ExitStack()
    sems, shared = {}, {}

    def S(name):
        name = shared[name][0] if name in shared else name
        if name not in sems:
            sems[name] = ctx.enter_context(nc.semaphore(name))
        return sems[name]

    class Chain:

        def __init__(self, eng, name):
            self.eng, self.sem, self.n, self.loop = eng, S(name), 0, 0

        def __call__(self, ins):
            self.n += 1
            ins.then_inc(self.sem, 1)
            self.eng.wait_ge(self.sem, self.loop + self.n)

    with ctx:
        ATT = {"A": Attn("A", 0, 0, 2, TT, 2 * HD), "B": Attn("B", 0, 4, 1, TT, HD),
               "C": Attn("C", 1, 0, 1, 1, HD, kv_shared=True), "D": Attn("D", 1, 4, 1, 4, HD)}

        def share(kind, stages):
            total = {}
            for prefix, signals in stages:
                for sig, n in signals.items():
                    shared[prefix + sig] = (kind + sig, total.get(sig, 0))
                    total[sig] = total.get(sig, 0) + n

        def before(name):
            return shared[name][1] if name in shared else 0

        share("norm", [(p, {"_sq": t, "_rt": t, "_xn": t, "_tr": 2 * t, "_evA": t, "_evD": t})
                       for p, t in (("n1", TT), ("nc", CT), ("n2", TT), ("n3", TT), ("n4", TT))])
        share("plain", [(p, {"_mm": j, "_evA": (j + 1) // 2, "_evD": j // 2})
                        for p, j in (("ada", 12), ("u", TT), ("dft", 16), ("fu", 8), ("v", NCH), ("av", TT), ("bv", TT), ("dv", TT))])
        share("proj", [(p, {q: TT for q in ("_z", "_sq", "_ss", "_rt", "_zn", "_tr", "_evA")})
                       for p in ("aq", "ak", "bq", "bk", "cq", "ck", "dq", "dk")])
        share("sigate", [(p, {"_mm": 8, "_sg": 8, "_mul": 8}) for p in ("ag", "bg", "cg", "dg")])
        share("wout", [(p, {"_mm": 2 * TT, "_ev": 2 * TT}) for p in ("wo", "wo0", "wo1")])
        share("res", [(p, {"_out": 16, "_in": 16}) for p in ("res0", "res1")])
        share("attn", [(n, {"_qk": len(at.units), "_s": len(at.units), "_e": len(at.units), "_w": at.G if n == "A" else 0, "_tr": at.G,
                            "_wevA": at.G, "_wevD": at.big[at.G], "_pv": at.G, "_o": at.G, "_on": 4 if n == "A" else 0, "_otr": 8, "_mix": 8,
                            **({} if n == "D" else {"_bias0": 64, "_bias1": 0 if n == "A" else 64})})
                       for n, at in ATT.items()])

        def sb(name, cols, dt=F32, parts=P):
            return ctx.enter_context(nc.sbuf_tensor(name, [parts, cols], dt))

        ring = sb("ring", RING * KT * HALF)
        hidden = sb("hidden", KT * SEQ)
        ctx_hidden = sb("ctx_hidden", KT * CTX)
        pair = sb("pair", 8192)
        wide = sb("wide", 9256)
        small = sb("small", 6500)
        kctx = sb("kctx", NH * CTX)
        cols = sb("cols", NCH * 4 * NG)
        ident = sb("ident", P)
        identb = sb("identb", P, BF16)
        maskb = sb("maskb", 2 * NH * P, BF16)
        sel_wT = sb("sel_wT", 8 * P)
        sel = sel_wT[0:NG, :]
        dftc = sb("dftc", 2 * P)
        cT = sb("cT", KT * 2)
        csil = sb("csil", KT * 2)
        adaT = sb("adaT", 2 * 48)
        badaT = sb("badaT", 48)
        gT = sb("gT", 5 * KT)
        mod = sb("mod", 3 * KT)
        wconv = sb("wconv", 8 * 9)
        wgate = sb("wgate", KT * 2 * NG)
        bgate = sb("bgate", 2)
        epsc = sb("epsc", 1)
        onec = sb("onec", 1)
        wrt = sb("wrt", KT * NEXP)
        extra = sb("extra", SEQ)
        att = sb("att", 64)
        qst = sb("qst", 48)
        gcol = sb("gcol", 16)
        wbf = wgate[:, 384:448]
        bbf = sb("bbf", 1)
        stat = sb("stat", 64)
        psum = ctx.enter_context(nc.psum_tensor("psum", [P, 8 * HALF], F32))

        def bank(b):
            return psum[:, b * HALF:(b + 1) * HALF]

        def ringv(s):
            return ring[:, s * KT * HALF:(s + 1) * KT * HALF].rearrange("p (k n) -> p k n", k=KT)

        hT = hidden[:].rearrange("p (k n) -> p k n", k=KT)
        hcT = ctx_hidden[:].rearrange("p (k n) -> p k n", k=KT)
        x_sb = wide[:, 0:TT * D].rearrange("p (t n) -> p t n", t=TT)
        xn_buf = small[:, 0:2 * D].rearrange("p (b n) -> p b n", b=2)
        sq_buf = small[:, 2 * D:3 * D]
        cx_sb = small[:, 3 * D:5 * D].rearrange("p (t n) -> p t n", t=CT)
        mask_in = ctx_hidden[:, 0:2 * NH * P]
        adarow = pair[0:2, 0:6 * D]
        u_sb = small[:, 0:4 * D].rearrange("p (t n) -> p t n", t=TT)
        pq = pair[:].rearrange("p (a c n) -> p a c n", a=2, c=4)
        fuT = wide[:, 0:4 * D].rearrange("p (c n) -> p c n", c=4)

        tiles, place, last_read = [], {}, []

        def kview(w, c0, n=HALF, r0=0, rows=D):
            return w[r0:r0 + rows, c0:c0 + n].rearrange("(k p) n -> p k n", p=P)

        def add_tile(key, read, w, c0, n=HALF):
            place[key] = len(tiles)
            last_read.append(read)
            tiles.append([(0, 4, n, kview(w, c0, n, 0, 512)), (4, 4, n, kview(w, c0, n, 512, 512))])

        OFF_QK, OFF_V, OFF_O, OFF_G, OFF_BR = 512, 1536, 2048, 2560, 2576
        for j in range(12):
            add_tile(("ada", j), ("ada_mm", j + 1), a["w_ada"], j * HALF)
        add_tile("f", ("u_mm", TT), a["w_in"], 0)
        for n in range(2):
            add_tile(("cos", n), ("dft_mm", 8 * n + 4), a["dft_cos"], n * HALF)
            add_tile(("sin", n), ("dft_mm", 8 * n + 8), a["dft_sin"], n * HALF)
        add_tile("q", ("qk_mm", NH), a["w_in"], OFF_QK)
        add_tile("k", ("qk_mm", 2 * NH), a["w_in"], OFF_QK + 512)
        add_tile("v", ("v_mm", NCH), a["w_in"], OFF_V)
        add_tile("o", ("o_mm", 8), a["w_in"], OFF_O)
        for m in range(2):
            place["fm", m] = len(tiles)
            last_read.append(("mg_y", 8 * (m + 1)))
            tiles.append([(0, 4, HALF, kview(a["w_fourier"], m * HALF, rows=512)),
                          (4, 4, HALF, kview(a["w_mlstm"], m * HALF, rows=512))])
            add_tile(("br1", m), ("mg_y", 8 * (m + 1)), a["w_in"], OFF_BR + m * HALF)
            add_tile(("br2", m), ("mg_y", 8 * (m + 1)), a["w_in"], OFF_BR + D + m * HALF)
        for m in range(2):
            add_tile(("wo", m), ("wo_mm", TT * (m + 1)), a["w_out"], m * HALF)

        n_moe = len(tiles)
        for e in range(NEXP + 1):
            if e < NEXP:
                for key, sig in (("gate", "moe_g"), ("up", "moe_u")):
                    for m in range(2):
                        add_tile((key, e, m), (sig, 2 * e + m + 1), a["w_" + key][e], m * HALF)
            if e >= 1:
                for m in range(2):
                    add_tile(("down", e - 1, m), ("moe_d", 2 * (e - 1) + m + 1), a["w_down"][e - 1], m * HALF)
        assert n_moe % RING == 2
        for layer, w, plan in ((0, a["even_w_in"], (("aq", 0), ("ak", 512), ("av", 1024), ("bq", 2048), ("bk", 2560), ("bv", 3072),
                                                    ("ag", 1536), ("bg", 3584))),
                               (1, a["odd_w_in"], (("cq", 0), ("ck", 512), ("dq", 1280), ("dk", 1792), ("dv", 2304),
                                                   ("cg", 768), ("dg", 2816)))):
            for key, c0 in plan:
                sig = {"v": ("_mm", TT), "g": ("_mm", 8)}.get(key[1], ("_z", TT))
                add_tile(key, (key + sig[0], sig[1]), w, c0, 256 if key == "ck" else HALF)
            for m in range(2):
                add_tile(("out", layer, m), (f"wo{layer}_mm", TT * (m + 1)), a[("even_w_out", "odd_w_out")[layer]], m * HALF)
        LOOPED = (place["gate", 2, 0], place["down", 15, 0])

        def load_tile(sp, n):
            if n >= RING:
                name, value = last_read[n - RING]
                sp.wait_ge(S(name), before(name) + value)
            for k0, kn, w, src in tiles[n]:
                sp.dma_start(ringv(n % RING)[:, k0:k0 + kn, 0:w], src).then_inc(S(f"ring_full{n % RING}"), 16)

        def tile_ready(pe, key):
            n = place[key]
            pe.wait_ge(S(f"ring_full{n % RING}"), 32 * (n // RING + 1))
            return ringv(n % RING)

        def group(pe, outp, pairs):
            for i, (l, r) in enumerate(pairs):
                mm = pe.matmul(outp, l, r, start=(i == 0), stop=(i == len(pairs) - 1))
            return mm

        def jobs_mm(pe, p, j, nb, outp, pairs):
            if j >= nb:
                pe.wait_ge(S(p + "_ev" + "AD"[j % 2]), before(p + "_ev" + "AD"[j % 2]) + (j - nb) // 2 + 1)
            mm = group(pe, outp, pairs)
            mm.then_inc(S(p + "_mm"), 1)
            return mm

        def emptied(eng, p, jobs):
            eng.wait_ge(S(p + "_evA"), before(p + "_evA") + (jobs + 1) // 2)
            if jobs > 1:
                eng.wait_ge(S(p + "_evD"), before(p + "_evD") + jobs // 2)

        def evac(eng, p, jobs, f):
            side = 0 if hasattr(eng, "activation") else 1
            for j in range(side, jobs, 2):
                eng.wait_ge(S(p + "_mm"), before(p + "_mm") + j + 1)
                f(j).then_inc(S(p + "_ev" + "AD"[side]), 1)

        def copy(eng, o, i):
            return eng.activation(o, i, ACT.Copy) if hasattr(eng, "activation") else eng.tensor_copy(o, i)

        class Norm:

            def __init__(self, p, T, src, ready, col, dst, A, B, banks=lambda t: (2 * (t % 2), 2 * (t % 2) + 1), depth=2, stored=None):
                self.p, self.T, self.src, self.ready, self.col, self.dst, self.A, self.B = p, T, src, ready, col, dst, A, B
                self.banks, self.depth, self.stored = banks, depth, stored

            def wait(self, eng, sig, n):
                eng.wait_ge(S(self.p + sig), before(self.p + sig) + n)

            def squares(self, act, t):
                c = self.col + t
                self.ready(act, t)
                if t:
                    self.wait(act, "_sq", t)
                act.activation(sq_buf, self.src(t), ACT.Square, accum_out=stat[:, c:c + 1]).then_inc(S(self.p + "_sq"), 1)
                self.wait(act, "_sq", t + 1)
                act.activation(stat[:, c + 16:c + 17], stat[:, c:c + 1], ACT.Sqrt, bias=epsc[:, 0:1], scale=1.0 / D).then_inc(S(self.p + "_rt"), 1)

            def scale(self, dve, link, t):
                c = self.col + t
                self.ready(dve, t)
                self.wait(dve, "_rt", t + 1)
                link(dve.reciprocal(stat[:, c + 32:c + 33], stat[:, c + 16:c + 17]))
                if t >= 2:
                    self.wait(dve, "_tr", 2 * (t - 1))
                    if self.stored:
                        self.stored(dve, t - 2)
                dve.tensor_scalar(xn_buf[:, t % 2, :], self.src(t), stat[:, c + 32:c + 33], None, ALU.mult).then_inc(S(self.p + "_xn"), 1)

            def transposes(self, pe, t):
                self.wait(pe, "_xn", t + 1)
                if t >= self.depth:
                    self.wait(pe, "_evA", t - self.depth + 1)
                    self.wait(pe, "_evD", t - self.depth + 1)
                for h in range(2):
                    for k in range(4):
                        mm = pe.transpose(bank(self.banks(t)[h])[:, k * P:(k + 1) * P],
                                          xn_buf[:, t % 2, (4 * h + k) * P:(4 * h + k + 1) * P], ident[:])
                    mm.then_inc(S(self.p + "_tr"), 1)

            def evac_act(self, act, t):
                self.wait(act, "_tr", 2 * t + 1)
                for k in range(4):
                    ins = act.activation(self.dst(t, k), bank(self.banks(t)[0])[:, k * P:(k + 1) * P], ACT.Identity,
                                         bias=(self.B(k) if self.B else 0.0), scale=self.A(k))
                ins.then_inc(S(self.p + "_evA"), 1)

            def evac_dve(self, dve, t):
                self.wait(dve, "_tr", 2 * t + 2)
                for k in range(4, 8):
                    i = bank(self.banks(t)[1])[:, (k - 4) * P:(k - 3) * P]
                    if self.B:
                        ins = dve.tensor_scalar(self.dst(t, k), i, self.A(k), self.B(k), ALU.mult, ALU.add)
                    else:
                        ins = dve.tensor_scalar(self.dst(t, k), i, self.A(k), None, ALU.mult)
                ins.then_inc(S(self.p + "_evD"), 1)

            def done(self, eng, t):
                self.wait(eng, "_evA", t + 1)
                self.wait(eng, "_evD", t + 1)

            def run_act(self, act):
                for t in range(self.T + 1):
                    if t < self.T:
                        self.squares(act, t)
                    if t:
                        self.evac_act(act, t - 1)

            def run_dve(self, dve, link):
                for t in range(self.T + 1):
                    if t < self.T:
                        self.scale(dve, link, t)
                    if t:
                        self.evac_dve(dve, t - 1)

            def run_pe(self, pe):
                for t in range(self.T):
                    self.transposes(pe, t)
                self.done(pe, self.T - 1)

        PADW, PADH = GRID_W + 2, GRID_H + 2
        pads = [small[:, i * 1280:i * 1280 + PADH * PADW] for i in range(2)]
        cpads = [small[:, 2560 + i * 320:2560 + i * 320 + CTX + 2] for i in range(2)]
        accs = [small[:, 3200 + i * 1280:3200 + i * 1280 + SEQ] for i in range(2)]
        caccs = [small[:, 3200 + i * 1280 + SEQ:3200 + (i + 1) * 1280] for i in range(2)]
        qT = pair[:, 0:4 * D].rearrange("p (h n) -> p h n", h=NH)
        kT = pair[:, 4 * D:8 * D].rearrange("p (h n) -> p h n", h=NH)
        kcT = kctx[:].rearrange("p (h n) -> p h n", h=NH)
        VW = DH + 1
        vex = wide[:, 0:NCH * NH * VW].rearrange("p (c h n) -> p c h n", c=NCH, h=NH)
        hsum = wide[:, NCH * NH * VW:NCH * NH * VW + 4 * D].rearrange("p (c n) -> p c n", c=TT)
        mT = wide[:, 0:KT * D].rearrange("p (k n) -> p k n", k=KT)
        TTOT = CTX + SEQ
        rowv = small[0:NG, 0:6400].rearrange("p (a n) -> p a n", n=1280)
        rF, rI, rC, rM, rR = (rowv[:, i, :] for i in (1, 2, 3, 4, 0))
        ones_row = cols[0:NG, 0:P]
        colv = cols[:].rearrange("p (c a g) -> p c a g", c=NCH, a=4)
        Cst = small[:, 1280:1280 + 8 * VW].rearrange("p (c n) -> p c n", c=8)
        kw = small[:, 2312:2312 + 1024].rearrange("p (b h n) -> p b h n", b=2, h=NH)
        se = small[:, 3336:3336 + 1024].rearrange("p (b h n) -> p b h n", b=2, h=NH)
        ee = small[:, 4360:4360 + 1024].rearrange("p (b h n) -> p b h n", b=2, h=NH)
        ob = small[:, 5384:5384 + NH * VW].rearrange("p (h n) -> p h n", h=NH)
        dnb = small[:, 5900:5900 + 8 * NCH].rearrange("p (c n) -> p c n", c=8)
        rec = small[:, 5980:5984]
        tmpn = small[:, 5984:6496].rearrange("p (h n) -> p h n", h=NH)
        oT = pair[:, 0:4 * D].rearrange("p (h n) -> p h n", h=NH)
        hmT = pair[:, 4 * D:8 * D].rearrange("p (h n) -> p h n", h=NH)
        fuR = small[:, 0:4 * D].rearrange("p (c n) -> p c n", c=4)
        sg = small[:, 4 * D:4 * D + 2048].rearrange("p (b a n) -> p b a n", b=2, a=2)
        sgd = ctx_hidden[:].rearrange("p (b a n) -> p b a n", b=2, a=2)

        x1 = hidden[:].rearrange("p (t n) -> p t n", t=TT)
        h2T = pair[:].rearrange("p (k n) -> p k n", k=KT)
        ga1b, ga2b = small[:, 3072:4096], small[:, 4096:5120]
        gfb = small[:, 5120:6144]
        affT = ctx_hidden[0:NEXP, 0:SEQ]
        aff = ctx_hidden[:, SEQ:SEQ + P].rearrange("p (t e) -> p t e", e=NEXP)
        route = kctx[:, 0:512]
        vals, idx, idxf = route[0:NEXP, 0:P], route[0:NEXP, P:2 * P].bitcast(U32), route[0:NEXP, 2 * P:3 * P]
        valc, idxc = route[:, 384:400], route[:, 400:416].bitcast(I32)
        idx1 = route[:, 416:420].bitcast(I32)
        lmax, lsum = route[:, 420:428], route[:, 428:436]
        xg, xs, sgate, hid, hd, yb = (wide[:, i * D:(i + 1) * D] for i in range(6))
        xsT, hidT = xs.rearrange("p (k n) -> p k n", k=KT), hd.rearrange("p (k n) -> p k n", k=KT)

        qT2 = wide[:, 0:4 * D].rearrange("p (c n) -> p c n", c=4)
        kT2 = wide[:, 4 * D:8 * D].rearrange("p (c n) -> p c n", c=4)
        v2 = small[:, 0:4 * D].rearrange("p (t n) -> p t n", t=TT)
        obuf = [small[:, (4 + i) * D:(5 + i) * D].rearrange("p (b n) -> p b n", b=TT) for i in range(2)]
        xlay = [pair[:].rearrange("p (k n) -> p k n", k=KT), hidden[:].rearrange("p (k n) -> p k n", k=KT)]
        H2 = xlay
        M2 = xlay[::-1]
        R2 = xlay
        x3 = wide[:, 0:TT * D].rearrange("p (t n) -> p t n", t=TT)
        wT = [w[:].rearrange("p (k n) -> p k n", k=KT) for w in (kctx, sel_wT)]
        sA = [ctx_hidden[:, 0:D], ctx_hidden[:, D:2 * D], wide[:, 8 * D:9 * D], extra[:]]
        SBUFS = {"A": sA, "B": sA[:3], "C": sA, "D": sA}
        BIAS = {"A": [cols[:, 0:D]], "B": [cols[:, 0:D], extra[:]],
                "C": [cols[:, 0:256], cols[:, 256:512]], "D": [cols[:, 0:640], cols[:, 640:1280]]}
        nmx, esum, rinv, esk = (att[:, 8 * i:8 * i + 8] for i in range(4))
        sinkb, nsink, nlam, lsums = att[:, 32:40], att[:, 40:48], att[:, 48:49], att[:, 50:52]
        lamb = wgate[:, 0:256].rearrange("p (a n) -> p a n", a=4)
        lamx = wgate[:, 256:384].rearrange("p (a n) -> p a n", a=2)
        sqz = [extra[:, 0:HALF], extra[:, HALF:D]]
        zn = [ctx_hidden[:, 0:HALF], ctx_hidden[:, HALF:D]]
        frow = [ctx_hidden[0:8, 0:D], ctx_hidden[0:8, D:2 * D], wide[0:8, 8 * D:9 * D]]
        xsq = cols[:, D:D + P]
        sgt = [extra[:, 0:HALF], extra[:, HALF:D]]
        QK = {"aq": (0, 8, HALF, qT2), "ak": (0, 1, HALF, kT2), "bq": (0, 9, HALF, qT2), "bk": (0, 3, HALF, kT2),
              "cq": (1, 10, HALF, qT2), "ck": (1, 5, P, kT2), "dq": (1, 11, HALF, qT2), "dk": (1, 7, HALF, kT2)}

        def rows_of(keys):
            return [(key, t) for key in keys for t in range(TT)]

        steps = []
        for i in range(NCH):
            f = i
            b = (CT - 1 - i) if i < CT else NCH - 1 - (i - CT)
            steps += [(0, f, i >= CT), (1, b, i >= CT)]
        outs_before = [sum(1 for s in steps[:i] if s[2]) for i in range(len(steps) + 1)]

        def span(c):
            return slice(c * P, (c + 1) * P)

        def chain_row(d, h):
            return (BWD if d else 0) + h

        def ksrc(h, c):
            return kcT[:, h, c * P:(c + 1) * P] if c < CT else kT[:, h, (c - CT) * P:(c - CT + 1) * P]

        block = ctx.enter_context(nc.Block())

        @block.sync
        def _(sp):
            for n in range(2):
                load_tile(sp, n)
            sp.dma_start(x_sb, a["x"].rearrange("(t p) n -> p t n", p=P)).then_inc(S("x_in"), 16)
            sp.dma_start(cx_sb, a["ctx"].rearrange("(t p) n -> p t n", p=P)).then_inc(S("cx_in"), 16)
            for n in range(2, len(tiles)):
                if n == LOOPED[0]:
                    with sp.Fori(2, NEXP) as e:
                        for j in range(6):
                            name, value = (("moe_u", e * 2), ("moe_d", e * 2 - 3), ("moe_d", e * 2 - 2),
                                           ("moe_g", e * 2 + 1), ("moe_g", e * 2 + 2), ("moe_u", e * 2 + 1))[j]
                            sp.wait_ge(S(name), before(name) + value)
                            w = a[("w_gate", "w_up", "w_down")[j // 2]]
                            w = w[bass.ds(e - j // 4, 1), :, (j % 2) * HALF:(j % 2 + 1) * HALF].rearrange("e (k p) n -> p (e k) n", p=P)
                            for k0 in (0, 4):
                                sp.dma_start(ringv(j % RING)[:, k0:k0 + 4, :], w[:, k0:k0 + 4, :]).then_inc(S(f"ring_full{j % RING}"), 16)
                if LOOPED[0] <= n < LOOPED[1]:
                    continue
                if stop < 8 and n == place["aq"]:
                    tiles[:] = tiles[:n]
                    break
                load_tile(sp, n)
                if n == place["wo", 1]:
                    sp.wait_ge(S("mg_add"), 16)
                    sp.dma_start(x1, a["x"].rearrange("(t p) n -> p t n", p=P)).then_inc(S("x_again"), 16)
                    if stop < 7:
                        return
                if n == place["o"] and stop < 4:
                    for q in range(RING):
                        sp.wait_ge(S(f"ring_full{q}"), 32 * sum(1 for z in range(n + 1) if z % RING == q))
                    return
                if n == place["k"]:
                    emptied(sp, "fu", 8)
                    sp.dma_start(scratch["fu"], fuT).then_inc(S("fu_out"), 16)
                if n == place["br1", 0]:
                    sp.wait_ge(S("scan_out"), TT * 2)
                    sp.wait_ge(S("fu_out"), 16)
                    sp.dma_start(fuR, scratch["fu"]).then_inc(S("fu_in"), 16)

            if stop < 8:
                for t in range(TT):
                    sp.wait_ge(S("xb"), t + 1)
                    sp.dma_start(out.rearrange("(t p) n -> p t n", p=P)[:, t, :], x1[:, t, :]).then_inc(S("out"), 16)
                sp.wait_ge(S("out"), 16 * TT)
            for q in range(RING):
                sp.wait_ge(S(f"ring_full{q}"), 32 * len(range(q, len(tiles), RING)))

        @block.gpsimd
        def _(pool):
            for o, i in ((cT[:], a["cT"]), (badaT[:], a["b_adaT"]), (gT[:], a["gT"]), (ident[:], a["ident"]),
                         (mask_in, a["masks"]), (sel, a["sel"]),
                         (dftc[:], a["dftc"]), (wconv[:], a["w_convT"]), (wgate[:], a["w_mgate"]),
                         (bgate[0:NG, :], a["b_gate"]), (wrt[:], a["w_routerT"])):
                pool.dma_start(o, i).then_inc(S("const"), 16)
            pool.memset(epsc[:], EPS).then_inc(S("epsc"), 1)
            pool.memset(onec[:], 1.0).then_inc(S("epsc"), 1)

            pool.wait_ge(S("mod"), 1)
            pool.dma_start(scratch["ada"].rearrange("(c p) -> p c", p=P), adaT[:, 0:48], allow_slow_non_contiguous=True).then_inc(S("ada_out"), 16)
            pool.wait_ge(S("ada_out"), 16)
            pool.wait_ge(S("mg_add"), 16)
            pool.dma_start(ga1b, scratch["ada"][2 * D:3 * D].partition_broadcast(P)).then_inc(S("ga1"), 16)
            pool.dma_start(ga2b, scratch["ada"][5 * D:6 * D].partition_broadcast(P)).then_inc(S("ga2"), 16)
            pool.dma_start(gfb, a["g_final"].partition_broadcast(P)).then_inc(S("gf"), 16)
            pool.wait_ge(S("rows"), 1)
            for o, i in ((lamb, a["lams"].partition_broadcast(P)), (sinkb, a["sinks"].partition_broadcast(P)),
                         (gcol[:, 0:8], a["qk_gains"]), (gcol[:, 12:13], a["sub_gain"]), (wbf, a["w_forget"]),
                         (bbf[0:8, :], a["b_forget"])):
                pool.dma_start(o, i).then_inc(S("const2"), 16)
            if stop < 7:
                pool.wait_ge(S("ga1"), 16); pool.wait_ge(S("ga2"), 16); pool.wait_ge(S("gf"), 16)
                return
            for t in range(TT):
                pool.wait_ge(S("wo_ev"), before("wo_ev") + TT + t + 1)
                pool.dma_start(scratch["acc"].rearrange("(t p) n -> p t n", p=P)[:, t, :], x1[:, t, :]).then_inc(S("acc_out"), 16)
                pool.wait_ge(S("n2_xn"), before("n2_xn") + t + 1)
                pool.dma_start(scratch["xn"].rearrange("(t p) n -> p t n", p=P)[:, t, :], xn_buf[:, t % 2, :]).then_inc(S(f"xn_out{t % 2}"), 16)
            pool.wait_ge(S("acc_out"), 16 * TT)
            for q in range(2):
                pool.wait_ge(S(f"xn_out{q}"), 16 * TT // 2)

            pool.wait_ge(S("route"), 1)
            pool.tensor_copy(idx1[:, 0:1], idxc[:, 0:1]).then_inc(S("moe_first"), 1)
            pool.wait_ge(S("moe_first"), 1)
            pool.indirect_dma_start(xg, None, scratch["xn"], bass.IndirectOffsetOnAxis(idx1[:, 0:1].bitcast(U32), 0)).then_inc(S("moe_gat"), 16)
            pool.wait_ge(S("moe_gat"), 16)
            pool.wait_ge(S("moe_xtr"), 2)
            pool.tensor_copy(idx1[:, 0:1], idxc[:, 1:2]).then_inc(S("moe_ix0"), 1)
            pool.wait_ge(S("moe_ix0"), 1)
            pool.indirect_dma_start(xg, None, scratch["xn"], bass.IndirectOffsetOnAxis(idx1[:, 0:1].bitcast(U32), 0)).then_inc(S("moe_gat"), 16)

            def one(e, more):
                if more:
                    pool.wait_ge(S("moe_xtr"), e * 2 + 2)
                    pool.wait_ge(S("moe_gat"), e * 16 + 16)
                    pool.tensor_copy(idx1[:, 0:1], idxc[:, bass.ds(e + 1, 1)])
                    pool.drain()
                    pool.indirect_dma_start(xg, None, scratch["xn"], bass.IndirectOffsetOnAxis(idx1[:, 0:1].bitcast(U32), 0)).then_inc(S("moe_gat"), 16)
                pool.wait_ge(S("moe_y"), e * 2)
                pool.tensor_copy(idx1[:, 1:2], idxc[:, bass.ds(e - 1, 1)])
                pool.drain()
                pool.indirect_dma_start(scratch["acc"], bass.IndirectOffsetOnAxis(idx1[:, 1:2].bitcast(U32), 0), yb, None,
                                        compute_op=ALU.add).then_inc(S("moe_sct"), 16)
                pool.wait_ge(S("moe_sct"), e * 16)

            with pool.Fori(1, NEXP - 1) as e:
                one(e, True)
            one(NEXP - 1, False)
            one(NEXP, False)
            for i in range(TT // 2):
                pool.dma_start(x1[:, 2 * i:2 * i + 2, :], scratch["acc"].rearrange("(t p) n -> p t n", p=P)[:, 2 * i:2 * i + 2, :]).then_inc(S(f"x2_in{i}"), 16)
            if stop < 8:
                pool.wait_ge(S("const2"), 16 * 6)
                return
            for layer in range(2):
                if layer == 0:
                    pool.wait_ge(S("xb"), TT)
                else:
                    pool.wait_ge(S("wo0_ev"), before("wo0_ev") + 2 * TT)
                rows = scratch[("xb", "x3")[layer]].rearrange("(t p) n -> p t n", p=P)
                pool.dma_start(rows, (x1, x3)[layer]).then_inc(S(f"res{layer}_out"), 16)
                for name in ("AB", "CD")[layer]:
                    att = ATT[name]
                    nb = len(BIAS[name])
                    if name == "B":
                        pool.wait_ge(S("forget"), 1)
                        pool.dma_start(scratch["ncum"], frow[0]).then_inc(S("ncum_out"), 16)
                        pool.wait_ge(S("ncum_out"), 16)
                    if name == "A":
                        pool.wait_ge(S("ak_evA"), before("ak_evA") + TT)
                    for i in range(att.nbias):
                        o = BIAS[name][i % nb]
                        if i >= nb:
                            pool.wait_ge(S(name + "_s"), before(name + "_s") + att.per_bias * att.comps * (i - nb + 1))
                        elif name in "BD":
                            pool.wait_ge(S(name.lower() + "k_evA"), before(name.lower() + "k_evA") + TT)
                        elif name == "C":
                            pool.wait_ge(S("ck_evA"), before("ck_evA") + TT)
                        src = {"A": lambda: a["strip_a"][i], "B": lambda: scratch["ncum"][i].partition_broadcast(P),
                               "C": lambda: a["strip_c"][i],
                               "D": lambda: bass.AP(tensor=a["rel"].tensor, offset=i * 768, ap=[[1, P], [1, 640]])}[name]()
                        if name != "D":
                            pool.dma_start(o, src).then_inc(S(name + f"_bias{i % nb}"), 16)
                        else:
                            pool.dma_start(o, src).then_inc(S(f"D_rel{i % nb}"), 16)
                            pool.wait_ge(S(f"D_rel{i % nb}"), 16 * (i // nb + 1))
                            pool.memset(o[HD:P, 640 - HD:640], NEG).then_inc(S(f"D_bias{i % nb}"), 8)
                            pool.memset(o[0:HD, 0:HD], NEG).then_inc(S(f"D_bias{i % nb}"), 8)
                pool.wait_ge(S(("bg", "dg")[layer] + "_mm"), before(("bg", "dg")[layer] + "_mm") + 8)
                pool.wait_ge(S(f"res{layer}_out"), before(f"res{layer}_out") + 16)
                pool.dma_start(R2[layer], rows).then_inc(S(f"res{layer}_in"), 16)
            for t in range(TT):
                pool.wait_ge(S("wo1_ev"), before("wo1_ev") + TT + t + 1)
                pool.dma_start(out.rearrange("(t p) n -> p t n", p=P)[:, t, :], x3[:, t, :]).then_inc(S("out"), 16)
            pool.wait_ge(S("out"), 16 * TT)

        def consts(eng):
            eng.wait_ge(S("const"), 16 * 11)
            eng.wait_ge(S("epsc"), 2)

        xr = lambda eng, t: eng.wait_ge(S("x_in"), 16)
        cr = lambda eng, t: eng.wait_ge(S("cx_in"), 16)
        NX = Norm("n1", TT, lambda t: x_sb[:, t, :], xr, 0, lambda t, k: hT[:, k, t * P:(t + 1) * P],
              lambda k: mod[:, k:k + 1], lambda k: adaT[:, k:k + 1])
        NC = Norm("nc", CT, lambda t: cx_sb[:, t, :], cr, 8, lambda t, k: hcT[:, k, t * P:(t + 1) * P],
              lambda k: mod[:, KT + k:KT + k + 1], lambda k: adaT[:, 48 + k:48 + k + 1])

        W1 = lambda eng, t: eng.wait_ge(S("wo_ev"), before("wo_ev") + TT + t + 1)
        N2 = Norm("n2", TT, lambda t: x1[:, t, :], W1, 0, lambda t, k: h2T[:, k, t * P:(t + 1) * P],
              lambda k: mod[:, 2 * KT + k:2 * KT + k + 1], lambda k: adaT[:, 3 * KT + k:3 * KT + k + 1], banks=lambda t: (4, 5), depth=1,
              stored=lambda eng, t: eng.wait_ge(S(f"xn_out{t % 2}"), 16 * (t // 2 + 1)))

        def n2_pe(pe, i):
            if 0 <= i - 2 < TT:
                N2.transposes(pe, i - 2)
            if 0 <= i - 3 < TT:
                t = i - 3
                N2.done(pe, t)
                group(pe, bank(6)[:, t * NEXP:(t + 1) * NEXP],
                      [(h2T[:, k, span(t)], wrt[:, k * NEXP:(k + 1) * NEXP]) for k in range(KT)]).then_inc(S("logits"), 1)

        def bias_ready(eng, name, g):
            att = ATT[name]
            i, nb = g // att.per_bias, len(BIAS[name])
            eng.wait_ge(S(name + f"_bias{i % nb}"), before(name + f"_bias{i % nb}") + 16 * (i // nb + 1))
            return BIAS[name][i % nb]

        XB = lambda eng, t: eng.wait_ge(S("xb"), t + 1)
        X3 = lambda eng, t: eng.wait_ge(S("wo0_ev"), before("wo0_ev") + TT + t + 1)
        N3 = Norm("n3", TT, lambda t: x1[:, t, :], XB, 8, lambda t, k: H2[0][:, k, t * P:(t + 1) * P],
              lambda k: gT[:, 2 * KT + k:2 * KT + k + 1], None, banks=lambda t: (6, 7), depth=1)
        N4 = Norm("n4", TT, lambda t: x3[:, t, :], X3, 0, lambda t, k: H2[1][:, k, t * P:(t + 1) * P],
              lambda k: gT[:, 3 * KT + k:3 * KT + k + 1], None, banks=lambda t: (4 + 2 * (t % 2), 5 + 2 * (t % 2)))

        @block.tensor
        def _(pe):
            consts(pe)
            pe.wait_ge(S("csil"), 1)
            for j in range(12):
                w = tile_ready(pe, ("ada", j))
                jobs_mm(pe, "ada", j, 2, bank(j % 2)[0:2, :],
                        [(csil[:, 2 * k:2 * k + 2], w[:, k, :]) for k in range(KT)])
            emptied(pe, "ada", 12)
            for j in range(48):
                mm = pe.transpose(bank(2)[:, 2 * j:2 * j + 2], adarow[:, j * P:(j + 1) * P], ident[0:2, 0:2])
            mm.then_inc(S("adaT_mm"), 1)
            NX.run_pe(pe)
            NC.run_pe(pe)
            w = tile_ready(pe, "f")
            for t in range(TT):
                mm = jobs_mm(pe, "u", t, 4, bank(t % 4), [(hT[:, k, span(t)], w[:, k, :]) for k in range(KT)])
            emptied(pe, "u", 8)
            j = 0
            for n in range(2):
                for part, key in enumerate(("cos", "sin")):
                    w = tile_ready(pe, (key, n))
                    for c in range(4):
                        mm = jobs_mm(pe, "dft", j, 4, bank(j % 4),
                                     [(u_sb[:, k, span(c)], w[:, k, :]) for k in range(KT)])
                        j += 1
            emptied(pe, "dft", 16)
            for j in range(8):
                c, n = j // 2, slice((j % 2) * HALF, (j % 2 + 1) * HALF)
                jobs_mm(pe, "fu", j, 4, bank(j % 4), [(dftc[:, 0:P], pq[:, 0, c, n]), (dftc[:, P:2 * P], pq[:, 1, c, n])])
            emptied(pe, "fu", 8)
            for qk, key in enumerate("qk"):
                w = tile_ready(pe, key)
                for h in range(NH):
                    u = qk * NH + h
                    if u >= 2:
                        pe.wait_ge(S("qk_pad"), u - 1)
                    b = 3 * (u % 2)
                    for n in range(2):
                        mm = group(pe, bank(b + n), [(w[:, k, span(h)], hT[:, k, n * HALF:(n + 1) * HALF]) for k in range(KT)])
                    if qk:
                        mm = group(pe, bank(b + 2)[:, 0:CTX], [(w[:, k, span(h)], hcT[:, k, :]) for k in range(KT)])
                    mm.then_inc(S("qk_mm"), 1)
            pe.wait_ge(S("qk_pad"), 8)
            w = tile_ready(pe, "v")
            for c in range(NCH):
                src = hcT[:, :, span(c)] if c < CT else hT[:, :, span(c - CT)]
                mm = jobs_mm(pe, "v", c, 4, bank(c % 4), [(src[:, k, :], w[:, k, :]) for k in range(KT)])
            emptied(pe, "v", NCH)
            for i in range(2):
                lw = lambda k: wgate[:, (k * 2 + i) * NG:(k * 2 + i + 1) * NG]
                group(pe, bank(3 * i)[0:NG, 0:CTX], [(lw(k), hcT[:, k, :]) for k in range(KT)])
                for n in range(2):
                    mm = group(pe, bank(3 * i + 1 + n)[0:NG, :], [(lw(k), hT[:, k, n * HALF:(n + 1) * HALF]) for k in range(KT)])
            mm.then_inc(S("gate_mm"), 1)
            pe.wait_ge(S("rows"), 1)
            for c in range(NCH):
                if c >= 2:
                    pe.wait_ge(S("cols"), c - 1)
                for i, r in enumerate((rI, rF, rC, rM)):
                    mm = pe.transpose(bank(c % 2)[:, i * NG:(i + 1) * NG], r[:, span(c)], ident[0:NG, 0:NG])
                mm.then_inc(S("cols_mm"), 1)
            for d in range(2):
                for h in range(NH):
                    e = P - 1 if d == 0 else 0
                    mm = pe.matmul(bank(2)[:, (4 * d + h) * NCH:(4 * d + h + 1) * NCH],
                                   sel[:, (4 * d + h) * P:(4 * d + h + 1) * P], rC[:, e:TTOT:P], start=True, stop=True)
            mm.then_inc(S("dn_mm"), 1)
            pe.wait_ge(S("dn"), 1)
            pe.wait_ge(S("cols"), NCH)
            if stop < 4:
                return
            pe.wait_ge(S("c_zero"), 2)
            for i, (d, c, has) in enumerate(steps):
                no = outs_before[i]
                if has:
                    x0 = c - CT
                    if no >= 1:
                        pe.wait_ge(S("scan_se"), no)
                        pe.wait_ge(S("scan_e"), 4 * no)
                    for h in range(NH):
                        mm = pe.matmul(bank(0)[:, span(h)], ksrc(h, c), qT[:, h, span(x0)], start=True, stop=True)
                    mm.then_inc(S("scan_s"), 1)
                    pe.matmul(bank(1), identb[:], maskb[:, d * NH * P:(d + 1) * NH * P], start=True, stop=False, skip_group_check=True)
                    for h in range(NH):
                        mm = pe.matmul(bank(1)[:, span(h)], sel[:, (4 * d + h) * P:(4 * d + h + 1) * P], rR[:, span(c)],
                                       start=False, stop=(h == NH - 1), skip_group_check=True)
                    mm.then_inc(S("scan_r"), 1)
                if i >= 1:
                    pe.wait_ge(S("scan_c"), 4 * i)
                for h in range(NH):
                    mm = pe.transpose(bank(2)[:, span(h)], ksrc(h, c), ident[:])
                mm.then_inc(S("scan_kt"), 1)
                if has:
                    if no >= 1:
                        pe.wait_ge(S("scan_o"), 4 * no)
                    for h in range(NH):
                        mm = pe.matmul(bank(3 + h // 2)[:, (h % 2) * VW:(h % 2 + 1) * VW], qT[:, h, span(c - CT)],
                                       Cst[:, 4 * d + h, :], start=True, stop=True)
                    pe.wait_ge(S("scan_se"), no + 1)
                    for h in range(NH):
                        mm = pe.matmul(bank(5 + h // 2)[:, (h % 2) * VW:(h % 2 + 1) * VW], se[:, no % 2, h, :],
                                       vex[:, c, h, :], start=True, stop=True)
                    mm.then_inc(S("scan_u"), 1)
                pe.wait_ge(S("scan_kw"), 4 * (i + 1))
                for h in range(NH):
                    o = bank(7)[:, h * VW:(h + 1) * VW] if h < 3 else bank(2)[:, 0:VW]
                    mm = pe.matmul(o, kw[:, i % 2, h, :], vex[:, c, h, :], start=True, stop=True)
                mm.then_inc(S("scan_d"), 1)
            pe.wait_ge(S("scan_c"), 4 * len(steps))
            pe.wait_ge(S("scan_o"), 4 * 2 * TT)
            pe.wait_ge(S("scan_out"), 2 * TT)
            w = tile_ready(pe, "o")
            for j in range(8):
                h, n = j // 2, slice((j % 2) * HALF, (j % 2 + 1) * HALF)
                pe_w = [(w[:, k, span(h)], hT[:, k, n]) for k in range(KT)]
                if j >= 4:
                    pe.wait_ge(S("o_ev"), j - 3)
                mm = group(pe, bank(j % 4), pe_w)
                mm.then_inc(S("o_mm"), 1)
            for t in range(TT):
                if t >= 2:
                    pe.wait_ge(S("hm_ev"), t - 1)
                for h in range(NH):
                    mm = pe.transpose(bank(4 + t % 2)[:, span(h)], hsum[:, t, span(h)], ident[:])
                mm.then_inc(S("hm_mm"), 1)
            pe.wait_ge(S("hm_ev"), TT)
            pe.wait_ge(S("o_ev"), 8)
            pe.wait_ge(S("fu_in"), 16)
            j = 0
            for m in range(2):
                fm, b1, b2 = (tile_ready(pe, (n, m)) for n in ("fm", "br1", "br2"))
                for c in range(4):
                    for n in range(2):
                        b, ns = 4 * (j % 2), slice(n * HALF, (n + 1) * HALF)
                        if j >= 2:
                            pe.wait_ge(S("mg_sig"), 2 * (j - 1))
                            pe.wait_ge(S("mg_mul"), 2 * (j - 1))
                        group(pe, bank(b), [(b1[:, k, span(c)], hT[:, k, ns]) for k in range(KT)])
                        group(pe, bank(b + 1), [(b2[:, k, span(c)], hT[:, k, ns]) for k in range(KT)]).then_inc(S("mg_br"), 1)
                        group(pe, bank(b + 2), [(fm[:, k, span(c)], fuR[:, k, ns]) for k in range(4)])
                        mm = group(pe, bank(b + 3), [(fm[:, 4 + k, span(c)], hmT[:, k, ns]) for k in range(4)])
                        mm.then_inc(S("mg_y"), 1)
                        j += 1
            pe.wait_ge(S("mg_sig"), 32)
            pe.wait_ge(S("mg_mul"), 32)
            pe.wait_ge(S("mg_add"), 16)
            if stop < 7:
                return
            for m in range(2):
                w = tile_ready(pe, ("wo", m))
                for t in range(TT):
                    j = m * TT + t
                    if j >= 4:
                        pe.wait_ge(S("wo_ev"), before("wo_ev") + j - 3)
                    group(pe, bank(j % 4), [(mT[:, k, span(t)], w[:, k, :]) for k in range(KT)]).then_inc(S("wo_mm"), 1)
                    if m:
                        n2_pe(pe, t)
            for i in range(TT, TT + 3):
                n2_pe(pe, i)
            pe.wait_ge(S("aff"), 1)
            for t in range(TT):
                mm = pe.transpose(bank(1 + t // 4)[0:NEXP, (t % 4) * P:(t % 4 + 1) * P], aff[:, t, :], ident[:])
            mm.then_inc(S("affT"), 1)
            pe.wait_ge(S("topk"), 1)
            pe.transpose(bank(3)[:, 0:NEXP], vals, ident[0:NEXP, 0:NEXP])
            pe.transpose(bank(3)[:, NEXP:2 * NEXP], idxf, ident[0:NEXP, 0:NEXP]).then_inc(S("picked"), 1)
            pe.wait_ge(S("route"), 1)

            def expert_tile(pe, e, j):
                pe.wait_ge(S(f"ring_full{j % RING}"), e * 64 + 32 * (10 + j // RING))
                return ringv(j % RING)

            def x_transposes(e):
                pe.wait_ge(S("moe_gat"), e * 16 + 16)
                for h in range(2):
                    for k in range(4):
                        mm = pe.transpose(bank(6 + h)[:, span(k)], xg[:, span(4 * h + k)], ident[:])
                    mm.then_inc(S("moe_xtr"), 1)

            def h_transposes(e):
                pe.wait_ge(S("moe_hid"), e * 2 + 2)
                for h in range(2):
                    for k in range(4):
                        mm = pe.transpose(bank(6 + h)[:, span(k)], hid[:, span(4 * h + k)], ident[:])
                    mm.then_inc(S("moe_htr"), 1)

            def gate_up(e, tiles_of):
                pe.wait_ge(S("moe_xevA"), e + 1)
                pe.wait_ge(S("moe_xevD"), e + 1)
                for i in range(4):
                    w = tiles_of(i)
                    group(pe, bank(i), [(xsT[:, k, :], w[:, k, :]) for k in range(KT)]).then_inc(S(("moe_g", "moe_u")[i // 2]), 1)

            def down(e, tiles_of):
                pe.wait_ge(S("moe_hevA"), e + 1)
                pe.wait_ge(S("moe_hevD"), e + 1)
                for i in range(2):
                    w = tiles_of(i)
                    group(pe, bank(4 + i), [(hidT[:, k, :], w[:, k, :]) for k in range(KT)]).then_inc(S("moe_d"), 1)

            def turn(e, more):
                pe.wait_ge(S("moe_sil"), e * 2)
                pe.wait_ge(S("moe_hid"), e * 2)
                gate_up(e, lambda i: expert_tile(pe, e, i))
                if not isinstance(e, int) or e >= 2:
                    pe.wait_ge(S("moe_y"), e * 2 - 2)
                down(e - 1, lambda i: expert_tile(pe, e, 4 + i))
                if more:
                    x_transposes(e + 1)
                    pe.wait_ge(S("moe_xevA"), e + 2)
                    pe.wait_ge(S("moe_xevD"), e + 2)
                h_transposes(e)

            x_transposes(0)
            gate_up(0, lambda i: tile_ready(pe, (("gate", "up")[i // 2], 0, i % 2)))
            x_transposes(1)
            pe.wait_ge(S("moe_xevA"), 2)
            pe.wait_ge(S("moe_xevD"), 2)
            h_transposes(0)
            turn(1, True)
            with pe.Fori(2, NEXP - 1) as e:
                turn(e, True)
            turn(NEXP - 1, False)
            pe.wait_ge(S("moe_y"), 2 * NEXP - 2)
            down(NEXP - 1, lambda i: tile_ready(pe, ("down", NEXP - 1, i)))
            if stop < 8:
                return

            def qk_pe(*keys, then_v=None, norm=None):
                items = rows_of(keys)
                for i in range(len(items) + 1):
                    if i < len(items):
                        key, t = items[i]
                        layer, wd = QK[key][0], (256 if key == "ck" else HALF)
                        if norm and i < TT:
                            if i + 1 < TT:
                                norm.transposes(pe, i + 1)
                            norm.done(pe, i)
                        if t == 0:
                            w = tile_ready(pe, key)
                        if i >= 3 and items[i - 3][0] == "ck":
                            pe.wait_ge(S("cv_ev"), items[i - 3][1] + 1)
                        group(pe, bank(i % 3)[:, 0:wd], [(H2[layer][:, k, span(t)], w[:, k, 0:wd]) for k in range(KT)]).then_inc(S(key + "_z"), 1)
                    elif then_v:
                        w = tile_ready(pe, then_v)
                        v_job(then_v, layer, w, 0)
                    if i >= 1:
                        key, u = items[i - 1]
                        pe.wait_ge(S(key + "_zn"), before(key + "_zn") + u + 1)
                        if i >= 3:
                            pkey, pu = items[i - 3]
                            pe.wait_ge(S(pkey + "_evA"), before(pkey + "_evA") + pu + 1)
                        for c in range(QK[key][2] // P):
                            mm = pe.transpose(bank(3 + (i - 1) % 2)[:, span(c)], zn[(i - 1) % 2][:, span(c)], ident[:])
                        mm.then_inc(S(key + "_tr"), 1)
                if then_v:
                    for t in range(1, TT):
                        v_job(then_v, layer, w, t)
                    emptied(pe, then_v, TT)
                pe.wait_ge(S(key + "_evA"), before(key + "_evA") + TT)
                if key == "ck":
                    pe.wait_ge(S("cv_ev"), TT)

            def v_job(key, layer, w, t):
                jobs_mm(pe, key, t, 2, bank(6 + t % 2), [(H2[layer][:, k, span(t)], w[:, k, :]) for k in range(KT)])

            def attn_pe(name):
                at = ATT[name]

                def scores(g):
                    for i, (c, h, b, qc, row, kc, k0, nk) in enumerate(at.groups[g]):
                        v = g * at.comps + i
                        if v >= 2:
                            pe.wait_ge(S(name + "_s"), before(name + "_s") + v - 1)
                        for m in range((nk + 3) // 4):
                            n = min(4, nk - 4 * m) * P
                            o = bank(2 * (v % 2) + m)[:, 0:n]
                            last = name == "B" and m == (nk - 1) // 4
                            mm = pe.matmul(o, qT2[row:row + HD, qc, span(b)], kT2[row:row + HD, kc, (k0 + 4 * m) * P:(k0 + 4 * m) * P + n],
                                           start=True, stop=not last, skip_group_check=last)
                            if last:
                                mm = pe.matmul(o[:, n - P:n], identb[:], maskb[:, NH * P:NH * P + P], start=False, stop=True,
                                               skip_group_check=True)
                        mm.then_inc(S(name + "_qk"), 1)

                def transposes(g):
                    nk, v = at.groups[g][0][7], g * at.comps
                    if name == "A":
                        pe.wait_ge(S("A_w"), before("A_w") + g + 1)
                    else:
                        pe.wait_ge(S(name + "_e"), before(name + "_e") + g + 1)
                    if g >= 1:
                        pe.wait_ge(S(name + "_wevA"), before(name + "_wevA") + g)
                        if at.big[g]:
                            pe.wait_ge(S(name + "_wevD"), before(name + "_wevD") + at.big[g])
                    sbuf = SBUFS[name][v % len(SBUFS[name])]
                    for i in range(nk):
                        mm = pe.transpose(bank(4 + i // 4)[:, span(i % 4)], sbuf[:, span(i)], ident[:])
                    mm.then_inc(S(name + "_tr"), 1)

                def outputs(g):
                    c, h, b, qc, row, kc, k0, nk = at.groups[g][0]
                    pe.wait_ge(S(name + "_wevA"), before(name + "_wevA") + g + 1)
                    if at.big[g + 1]:
                        pe.wait_ge(S(name + "_wevD"), before(name + "_wevD") + at.big[g + 1])
                    if g >= 1:
                        pe.wait_ge(S(name + "_o"), before(name + "_o") + g)
                    vc = {"A": c * P, "B": c * P + h * HD, "C": (2 * c + h) // 4 * HD, "D": c * P + h * HD}[name]
                    for i in range(nk):
                        mm = pe.matmul(bank(6)[:, 0:at.dv], wT[g % 2][:, i, :], v2[:, k0 + i, vc:vc + at.dv], start=(i == 0), stop=(i == nk - 1))
                    mm.then_inc(S(name + "_pv"), 1)

                def finish(c):
                    if name == "A":
                        pe.wait_ge(S("A_on"), before("A_on") + c + 1)
                    else:
                        pe.wait_ge(S(name + "_o"), before(name + "_o") + at.last[c] + 1)
                    for m in range(2):
                        if c or m:
                            pe.wait_ge(S(name + "_mix"), before(name + "_mix") + 2 * c + m)
                        for b in range(4):
                            mm = pe.transpose(bank(7)[:, span(b)], obuf[c % 2][:, 4 * m + b, :], ident[:])
                        mm.then_inc(S(name + "_otr"), 1)

                for a, b, c, done in at.steps():
                    if a is not None:
                        scores(a)
                    if b is not None:
                        transposes(b)
                    if c is not None:
                        outputs(c)
                    for chunk in done:
                        finish(chunk)
                pe.wait_ge(S(name + "_mix"), before(name + "_mix") + 8)

            def gates_pe(key, layer):
                w = tile_ready(pe, key)
                for j in range(8):
                    c, n = j // 2, slice((j % 2) * HALF, (j % 2 + 1) * HALF)
                    if j >= 4:
                        pe.wait_ge(S(key + "_sg"), before(key + "_sg") + j - 3)
                    group(pe, bank(j % 4), [(w[:, k, span(c)], H2[layer][:, k, n]) for k in range(KT)]).then_inc(S(key + "_mm"), 1)
                pe.wait_ge(S(key + "_sg"), before(key + "_sg") + 8)

            def out_pe(layer):
                pe.wait_ge(S(("bg", "dg")[layer] + "_mul"), before(("bg", "dg")[layer] + "_mul") + 8)
                pe.wait_ge(S(("ag", "cg")[layer] + "_mul"), before(("ag", "cg")[layer] + "_mul") + 8)
                for m in range(2):
                    w = tile_ready(pe, ("out", layer, m))
                    for t in range(TT):
                        j = m * TT + t
                        if j >= 4:
                            pe.wait_ge(S(f"wo{layer}_ev"), before(f"wo{layer}_ev") + j - 3)
                        group(pe, bank(j % 4), [(M2[layer][:, k, span(t)], w[:, k, :]) for k in range(KT)]).then_inc(S(f"wo{layer}_mm"), 1)
                        if layer == 0 and m and t >= 2:
                            N4.transposes(pe, t - 2)
                if layer == 0:
                    N4.transposes(pe, TT - 2)
                    N4.transposes(pe, TT - 1)
                pe.wait_ge(S(f"wo{layer}_ev"), before(f"wo{layer}_ev") + 2 * TT)

            N3.transposes(pe, 0)
            qk_pe("aq", "ak", then_v="av", norm=N3)
            attn_pe("A")
            for n in range(2):
                mm = group(pe, bank(n)[0:8, :], [(wbf[:, 8 * k:8 * k + 8], H2[0][:, k, n * HALF:(n + 1) * HALF]) for k in range(KT)])
            mm.then_inc(S("forget_mm"), 1)
            pe.wait_ge(S("ncum_out"), 16)
            qk_pe("bq", "bk", then_v="bv")
            attn_pe("B")
            gates_pe("ag", 0)
            gates_pe("bg", 0)
            out_pe(0)
            N4.done(pe, TT - 1)
            qk_pe("cq", "ck")
            attn_pe("C")
            qk_pe("dq", "dk", then_v="dv")
            attn_pe("D")
            gates_pe("cg", 1)
            gates_pe("dg", 1)
            out_pe(1)

        @block.scalar
        def _(act):
            link = Chain(act, "act_own")
            consts(act)
            act.activation(csil[:], cT[:], ACT.Silu).then_inc(S("csil"), 1)
            evac(act, "ada", 12, lambda j: copy(act, adarow[:, j * HALF:(j + 1) * HALF], bank(j % 2)[0:2, :]))
            act.wait_ge(S("mod"), 1)
            NX.run_act(act)
            NC.run_act(act)
            evac(act, "u", 8, lambda j: copy(act, u_sb[:, j, :], bank(j % 4)))
            evac(act, "dft", 16, lambda j: copy(act, pq[:, (j // 4) % 2, j % 4, (j // 8) * HALF:(j // 8 + 1) * HALF], bank(j % 4)))
            evac(act, "fu", 8, lambda j: copy(act, fuT[:, j // 2, (j % 2) * HALF:(j % 2 + 1) * HALF], bank(j % 4)))
            act.wait_ge(S("pad_zero"), 4)
            for u in range(9):
                if u < 8:
                    act.wait_ge(S("qk_mm"), u + 1)
                    if u >= 2:
                        act.wait_ge(S("qk_conv"), u - 1)
                    grid = pads[u % 2].rearrange("p (y x) -> p y x", x=PADW)
                    for n in range(2):
                        ins = act.activation(grid[:, 1 + 8 * n:9 + 8 * n, 1:1 + GRID_W],
                                             bank(3 * (u % 2) + n).rearrange("p (y x) -> p y x", x=GRID_W), ACT.Copy)
                    if u >= 4:
                        ins = act.activation(cpads[u % 2][:, 1:1 + CTX], bank(3 * (u % 2) + 2)[:, 0:CTX], ACT.Copy)
                    ins.then_inc(S("qk_pad"), 1)
                if u >= 1:
                    v = u - 1
                    act.wait_ge(S("qk_conv"), v + 1)
                    if v == 0:
                        emptied(act, "fu", 8)
                    dst = (qT if v < 4 else kT)[:, v % 4, :]
                    ins = act.activation(dst, accs[v % 2], ACT.Silu)
                    if v >= 4:
                        ins = act.activation(kcT[:, v - 4, :], caccs[v % 2], ACT.Silu)
                    ins.then_inc(S("qk_silu"), 1)
            act.wait_ge(S("fu_out"), 16)
            evac(act, "v", NCH, lambda j: copy(act, vex[:, j, :, 0:DH], bank(j % 4).rearrange("p (h n) -> p h n", h=NH)))
            act.wait_ge(S("gate_mm"), 1)
            act.wait_ge(S("qk_silu"), 8)
            for i, r in enumerate((rI, rM)):
                link(act.activation(r[:, 0:CTX], bank(3 * i)[0:NG, 0:CTX], ACT.Identity, bias=bgate[0:NG, i:i + 1]))
                link(act.activation(r[:, CTX:TTOT], psum[0:NG, (3 * i + 1) * HALF:(3 * i + 3) * HALF], ACT.Identity,
                                    bias=bgate[0:NG, i:i + 1]))
            link(act.activation(rC, rM, ACT.Abs))
            link(act.activation(rC, rC, ACT.Exp, scale=-1.0))
            act.activation(rC, rC, ACT.Ln, bias=onec[0:NG, 0:1]).then_inc(S("gates"), 1)
            act.wait_ge(S("gate_rows"), 1)
            for c in range(NCH):
                act.activation(rF[:, span(c)], rI[:, span(c)], ACT.Exp, bias=stat[0:NG, 20 + c:21 + c])
                act.activation(rC[:, span(c)], rR[:, span(c)], ACT.Exp, bias=stat[0:NG, 40 + c:41 + c])
            act.activation(rM, rM, ACT.Exp, scale=-1.0).then_inc(S("rows"), 1)
            if stop < 4:
                return
            act.wait_ge(S("c_zero"), 2)
            for i, (d, c, has) in enumerate(steps):
                no = outs_before[i]
                act.wait_ge(S("scan_kt"), i + 1)
                if i >= 2:
                    act.wait_ge(S("scan_d"), i - 1)
                for h in range(NH):
                    g = chain_row(d, h)
                    act.activation(kw[:, i % 2, h, :], bank(2)[:, span(h)], ACT.Copy,
                                   scale=colv[:, c, 1, g:g + 1]).then_inc(S("scan_kw"), 1)
                if has:
                    act.wait_ge(S("scan_r"), no + 1)
                    if no >= 2:
                        act.wait_ge(S("scan_se"), no - 1)
                    for h in range(NH):
                        g = chain_row(d, h)
                        act.activation(ee[:, no % 2, h, :], bank(1)[:, span(h)], ACT.Exp,
                                       bias=colv[:, c, 0, g:g + 1]).then_inc(S("scan_e"), 1)
            act.wait_ge(S("scan_out"), 2 * TT)
            for j in range(8):
                act.wait_ge(S("o_mm"), j + 1)
                act.activation(oT[:, j // 2, (j % 2) * HALF:(j % 2 + 1) * HALF], bank(j % 4), ACT.Sigmoid).then_inc(S("o_ev"), 1)
            for j in range(16):
                act.wait_ge(S("mg_br"), j + 1)
                if j >= 2:
                    act.wait_ge(S("mg_mul"), 2 * (j - 1))
                for i in range(2):
                    act.activation(sg[:, j % 2, i, :], bank(4 * (j % 2) + i), ACT.Sigmoid).then_inc(S("mg_sig"), 1)
            if stop < 7:
                return
            act.wait_ge(S("mg_add"), 16)
            act.wait_ge(S("lam_sum"), 2)
            act.activation(lsums, lsums, ACT.Exp).then_inc(S("lam_exp"), 1)
            for i in range(TT + 2):
                if i < TT:
                    N2.squares(act, i)
                if i >= 2:
                    N2.evac_act(act, i - 2)
            act.wait_ge(S("lmax"), 1)
            for t in range(TT):
                act.activation(aff[:, t, :], bank(6)[:, t * NEXP:(t + 1) * NEXP], ACT.Exp, bias=lmax[:, t:t + 1],
                               accum_out=lsum[:, t:t + 1]).then_inc(S("lexp"), 1)

            def x_evac(e):
                act.wait_ge(S("moe_xtr"), e * 2 + 1)
                for k in range(4):
                    ins = act.activation(xsT[:, k, :], bank(6)[:, span(k)], ACT.Identity, bias=adaT[:, 3 * KT + k:3 * KT + k + 1],
                                         scale=mod[:, 2 * KT + k:2 * KT + k + 1])
                ins.then_inc(S("moe_xevA"), 1)

            def silu_gate(e):
                for m in range(2):
                    act.wait_ge(S("moe_g"), e * 2 + m + 1)
                    act.activation(sgate[:, m * HALF:(m + 1) * HALF], bank(m), ACT.Silu).then_inc(S("moe_sil"), 1)

            def h_evac(e):
                act.wait_ge(S("moe_htr"), e * 2 + 1)
                act.activation(hd[:, 0:HALF], bank(6), ACT.Copy).then_inc(S("moe_hevA"), 1)

            x_evac(0)
            silu_gate(0)
            x_evac(1)
            h_evac(0)
            with act.Fori(1, NEXP - 1) as e:
                act.wait_ge(S("moe_hid"), e * 2)
                silu_gate(e)
                x_evac(e + 1)
                h_evac(e)
            act.wait_ge(S("moe_hid"), 2 * NEXP - 2)
            silu_gate(NEXP - 1)
            h_evac(NEXP - 1)
            if stop < 8:
                return

            def qk_act(*keys, norm=None, stats=None):
                items = rows_of(keys)
                for i in range(len(items) + 1):
                    if i < len(items):
                        key, t = items[i]
                        if norm and i + 1 < TT:
                            norm.evac_act(act, i + 1)
                            if i + 2 < TT:
                                stats(i + 2)
                        nc4 = QK[key][2]
                        q = 24 * (i % 2)
                        act.wait_ge(S(key + "_z"), before(key + "_z") + t + 1)
                        act.activation(sqz[i % 2][:, 0:nc4], bank(i % 3)[:, 0:nc4], ACT.Square).then_inc(S(key + "_sq"), 1)
                        act.wait_ge(S(key + "_ss"), before(key + "_ss") + t + 1)
                        act.activation(qst[:, q + 8:q + 8 + nc4 // HD], qst[:, q:q + nc4 // HD], ACT.Sqrt,
                                       bias=epsc[:, 0:1], scale=1.0 / HD).then_inc(S(key + "_rt"), 1)
                    if i >= 1:
                        key, u = items[i - 1]
                        _, g, ncol, dst = QK[key]
                        act.wait_ge(S(key + "_tr"), before(key + "_tr") + u + 1)
                        act.activation(dst[:, 0:ncol // P, span(u)], bank(3 + (i - 1) % 2)[:, 0:ncol].rearrange("p (c n) -> p c n", c=ncol // P),
                                       ACT.Copy, scale=gcol[:, g:g + 1]).then_inc(S(key + "_evA"), 1)

            def attn_act(name):
                at = ATT[name]
                nbuf = len(SBUFS[name])

                def weights(g):
                    for i, (c, h, b, qc, row, kc, k0, nk) in enumerate(at.groups[g]):
                        v = g * at.comps + i
                        act.wait_ge(S(name + "_s"), before(name + "_s") + v + 1)
                        sv = SBUFS[name][v % nbuf][:, 0:nk * P]
                        act.activation(sv, sv, ACT.Exp, bias=nmx[:, v % 8:v % 8 + 1], scale=-1.0,
                                       accum_out=esum[:, v % 8:v % 8 + 1]).then_inc(S(name + "_e"), 1)
                        if name == "C":
                            hd_ = 2 * c + h
                            act.activation(esk[:, v % 8:v % 8 + 1], sinkb[:, hd_:hd_ + 1], ACT.Exp,
                                           bias=nmx[:, v % 8:v % 8 + 1]).then_inc(S("C_sink"), 1)

                def empty(g):
                    nk = at.groups[g][0][7]
                    act.wait_ge(S(name + "_tr"), before(name + "_tr") + g + 1)
                    n = min(4, nk)
                    act.activation(wT[g % 2][:, 0:n, :], bank(4)[:, 0:n * P].rearrange("p (k n) -> p k n", k=n), ACT.Copy).then_inc(S(name + "_wevA"), 1)

                def squares(c):
                    act.wait_ge(S("A_o"), before("A_o") + at.last[c] + 1)
                    for b in range(TT):
                        if c or b:
                            act.wait_ge(S("A_osq"), TT * c + b)
                        act.activation(xsq, obuf[c % 2][:, b, :], ACT.Square,
                                       accum_out=qst[:, b:b + 1]).then_inc(S("A_osq"), 1)
                    act.wait_ge(S("A_osq"), TT * (c + 1))
                    act.activation(qst[:, 8:16], qst[:, 0:8], ACT.Sqrt, bias=epsc[:, 0:1], scale=1.0 / (2 * HD)).then_inc(S("A_ort"), 1)

                def mix(c):
                    for m in range(2):
                        act.wait_ge(S(name + "_otr"), before(name + "_otr") + 2 * c + m + 1)
                        act.activation(M2[at.layer][:, at.mix0 + c, m * HALF:(m + 1) * HALF], bank(7), ACT.Copy,
                                       scale=(gcol[:, 13:14] if name == "A" else 1.0)).then_inc(S(name + "_mix"), 1)

                for a, b, c, done in at.steps():
                    if a is not None:
                        weights(a)
                    if b is not None:
                        empty(b)
                    for chunk in done:
                        if name == "A":
                            squares(chunk)
                        mix(chunk)

            def gates_act(key, layer):
                for j in range(8):
                    act.wait_ge(S(key + "_mm"), before(key + "_mm") + j + 1)
                    if before(key + "_mul") + j >= 2:
                        act.wait_ge(S(key + "_mul"), before(key + "_mul") + j - 1)
                    act.activation(sgt[j % 2], bank(j % 4), ACT.Silu).then_inc(S(key + "_sg"), 1)

            def v_act(key):
                evac(act, key, TT, lambda j: copy(act, v2[:, j, :], bank(6 + j % 2)))

            def stats(t):
                act.wait_ge(S(f"x2_in{t // 2}"), 16)
                if t:
                    act.wait_ge(S("n3_sq"), before("n3_sq") + t)
                act.activation(sq_buf, x1[:, t, :], ACT.Square, accum_out=stat[:, t:t + 1]).then_inc(S("nf_sq"), 1)
                act.wait_ge(S("nf_sq"), t + 1)
                act.activation(stat[:, 16 + t:17 + t], stat[:, t:t + 1], ACT.Sqrt, bias=epsc[:, 0:1], scale=1.0 / D).then_inc(S("nf_rt"), 1)
                N3.squares(act, t)

            stats(0)
            N3.evac_act(act, 0)
            stats(1)
            qk_act("aq", "ak", norm=N3, stats=stats)
            v_act("av")
            attn_act("A")
            act.wait_ge(S("forget_mm"), 1)
            link(act.activation(frow[0], psum[0:8, 0:2 * HALF], ACT.Identity, bias=bbf[0:8, 0:1]))
            link(act.activation(frow[1], frow[0], ACT.Abs))
            link(act.activation(frow[1], frow[1], ACT.Exp, scale=-1.0))
            act.activation(frow[1], frow[1], ACT.Ln, bias=onec[0:8, 0:1]).then_inc(S("forget_ln"), 1)
            qk_act("bq", "bk")
            v_act("bv")
            attn_act("B")
            gates_act("ag", 0)
            gates_act("bg", 0)
            for i in range(TT + 2):
                if i < TT:
                    N4.squares(act, i)
                if i >= 2:
                    N4.evac_act(act, i - 2)
            qk_act("cq", "ck")
            attn_act("C")
            qk_act("dq", "dk")
            v_act("dv")
            attn_act("D")
            gates_act("cg", 1)
            gates_act("dg", 1)

        @block.vector
        def _(dve):
            link = Chain(dve, "dve_own")
            consts(dve)
            link(dve.tensor_copy(identb[:], ident[:]))
            link(dve.tensor_copy(maskb[:], mask_in))
            evac(dve, "ada", 12, lambda j: copy(dve, adarow[:, j * HALF:(j + 1) * HALF], bank(j % 2)[0:2, :]))
            dve.wait_ge(S("adaT_mm"), 1)
            av = bank(2)[:, 0:96].rearrange("p (c b) -> p c b", b=2)
            for b in range(2):
                link(dve.tensor_tensor(adaT[:, b * 48:(b + 1) * 48], av[:, :, b], badaT[:], ALU.add))
            for i, (g, s) in enumerate(((0, KT), (0, 48 + KT), (1, 4 * KT))):
                link(dve.scalar_tensor_tensor(mod[:, i * KT:(i + 1) * KT], adaT[:, s:s + KT], 1.0,
                                              gT[:, g * KT:(g + 1) * KT], ALU.add, ALU.mult))
            dve.memset(stat[:, 63:64], 0.0).then_inc(S("mod"), 1)
            NX.run_dve(dve, link)
            NC.run_dve(dve, link)
            evac(dve, "u", 8, lambda j: copy(dve, u_sb[:, j, :], bank(j % 4)))
            evac(dve, "dft", 16, lambda j: copy(dve, pq[:, (j // 4) % 2, j % 4, (j // 8) * HALF:(j // 8 + 1) * HALF], bank(j % 4)))
            evac(dve, "fu", 8, lambda j: copy(dve, fuT[:, j // 2, (j % 2) * HALF:(j % 2 + 1) * HALF], bank(j % 4)))
            emptied(dve, "dft", 16)
            for i in range(2):
                dve.memset(pads[i], 0.0).then_inc(S("pad_zero"), 1)
                dve.memset(cpads[i], 0.0).then_inc(S("pad_zero"), 1)
            for u in range(8):
                dve.wait_ge(S("qk_pad"), u + 1)
                if u >= 2:
                    dve.wait_ge(S("qk_silu"), u - 1)
                grid = pads[u % 2].rearrange("p (y x) -> p y x", x=PADW)
                acc = accs[u % 2].rearrange("p (y x) -> p y x", x=GRID_W)
                wc = lambda t: wconv[:, u * 9 + t:u * 9 + t + 1]
                tap = lambda t: grid[:, t // 3:t // 3 + GRID_H, t % 3:t % 3 + GRID_W]
                link(dve.tensor_scalar(acc, tap(0), wc(0), None, ALU.mult))
                if u >= 4:
                    ca, cp = caccs[u % 2], cpads[u % 2]
                    link(dve.tensor_scalar(ca, cp[:, 0:CTX], wc(3), None, ALU.mult))
                    for t in (4, 5):
                        link(dve.scalar_tensor_tensor(ca, cp[:, t - 3:t - 3 + CTX], wc(t), ca, ALU.mult, ALU.add))
                for t in range(1, 8):
                    link(dve.scalar_tensor_tensor(acc, tap(t), wc(t), acc, ALU.mult, ALU.add))
                dve.scalar_tensor_tensor(acc, tap(8), wc(8), acc, ALU.mult, ALU.add).then_inc(S("qk_conv"), 1)
            dve.wait_ge(S("fu_out"), 16)
            dve.memset(vex[:, :, :, DH:VW], 1.0).then_inc(S("v_one"), 1)
            evac(dve, "v", NCH, lambda j: copy(dve, vex[:, j, :, 0:DH], bank(j % 4).rearrange("p (h n) -> p h n", h=NH)))
            link(dve.memset(ones_row, 1.0))
            dve.wait_ge(S("gates"), 1)
            link(dve.tensor_scalar(rM, rM, 0.0, None, ALU.min))
            link(dve.tensor_tensor(rF, rM, rC, ALU.subtract))
            for d in range(2):
                r = slice(0, NH) if d == 0 else slice(BWD, NG)
                sv = (lambda x: x) if d == 0 else (lambda x: x[:, ::-1])
                ends = (CTX - 1, TTOT - 1) if d == 0 else (0, CTX)
                if d == 0:
                    link(dve.memset(rM, 0.0))
                link(dve.tensor_tensor_scan(sv(rM[r, 0:CTX]), sv(rF[r, 0:CTX]), sv(rI[r, 0:CTX]), 0.0, ALU.add, ALU.max))
                link(dve.tensor_tensor_scan(sv(rM[r, CTX:TTOT]), sv(rF[r, CTX:TTOT]), sv(rI[r, CTX:TTOT]),
                                            rM[r, ends[0]:ends[0] + 1], ALU.add, ALU.max))
            link(dve.memset(rC, 0.0))
            for d in range(2):
                r = slice(0, NH) if d == 0 else slice(BWD, NG)
                sv = (lambda x: x) if d == 0 else (lambda x: x[:, ::-1])
                for c in range(NCH):
                    ins = dve.tensor_tensor_scan(sv(rC[r, span(c)]), sv(ones_row[r, :]), sv(rF[r, span(c)]), 0.0, ALU.mult, ALU.add)
                link(ins)
            link(dve.tensor_tensor(rI, rI, rC, ALU.subtract))
            link(dve.tensor_tensor(rR, rC, rM, ALU.subtract))
            link(dve.memset(stat[0:NG, 20:60], 0.0))
            for d in range(2):
                r = slice(0, NH) if d == 0 else slice(BWD, NG)
                e = P - 1 if d == 0 else 0
                link(dve.tensor_copy(stat[r, 20:20 + NCH], rR[r, e:TTOT:P]))
                if d == 0:
                    link(dve.tensor_copy(stat[r, 41:40 + NCH], rM[r, e:TTOT - P:P]))
                else:
                    link(dve.tensor_copy(stat[r, 40:41], rM[r, P:P + 1]))
                    link(dve.tensor_copy(stat[r, 42:42 + TT - 1], rM[r, CTX + P:TTOT:P]))
                    link(dve.tensor_copy(stat[r, 42 + TT - 1:42 + TT], rM[r, 0:1]))
            dve.memset(stat[:, 63:64], 0.0).then_inc(S("gate_rows"), 1)
            for c in range(NCH):
                dve.wait_ge(S("cols_mm"), c + 1)
                dve.tensor_copy(colv[:, c, :, :], bank(c % 2)[:, 0:4 * NG].rearrange("p (a g) -> p a g", a=4)).then_inc(S("cols"), 1)
            dve.wait_ge(S("dn_mm"), 1)
            dve.tensor_copy(dnb, bank(2)[:, 0:8 * NCH].rearrange("p (c n) -> p c n", c=8)).then_inc(S("dn"), 1)
            dve.wait_ge(S("cols"), NCH)
            dve.memset(Cst, 0.0).then_inc(S("c_zero"), 1)
            dve.wait_ge(S("dn"), 1)
            dve.wait_ge(S("c_zero"), 1)
            if stop < 4:
                return
            link(dve.tensor_scalar(colv[:, :, 1, :], colv[:, :, 1, :], KSC, None, ALU.mult))
            dve.memset(stat[:, 63:64], 0.0).then_inc(S("c_zero"), 1)
            for i, (d, c, has) in enumerate(steps):
                no = outs_before[i]
                if has:
                    dve.wait_ge(S("scan_s"), no + 1)
                    dve.wait_ge(S("scan_e"), 4 * (no + 1))
                    if no >= 2:
                        dve.wait_ge(S("scan_u"), no - 1)
                    dve.scalar_tensor_tensor(se[:, no % 2, :, :], bank(0).rearrange("p (h n) -> p h n", h=NH), KSC,
                                             ee[:, no % 2, :, :], ALU.mult, ALU.mult).then_inc(S("scan_se"), 1)
                    dve.wait_ge(S("scan_u"), no + 1)
                    for h in range(NH):
                        g = chain_row(d, h)
                        hs = slice((h % 2) * VW, (h % 2 + 1) * VW)
                        link(dve.tensor_scalar(ob[:, h, :], bank(3 + h // 2)[:, hs], colv[:, c, 2, g:g + 1], None, ALU.mult))
                        dve.tensor_tensor(ob[:, h, :], ob[:, h, :], bank(5 + h // 2)[:, hs], ALU.add).then_inc(S("scan_o"), 1)
                    dve.wait_ge(S("scan_o"), 4 * (no + 1))
                    g0 = chain_row(d, 0)
                    link(dve.scalar_tensor_tensor(rec, ob[:, :, DH], -1.0, colv[:, c, 3, g0:g0 + NH], ALU.mult, ALU.max))
                    link(dve.tensor_tensor(rec, rec, ob[:, :, DH], ALU.max))
                    link(dve.reciprocal(rec, rec))
                dve.wait_ge(S("scan_d"), i + 1)
                for h in range(NH):
                    o = bank(7)[:, h * VW:(h + 1) * VW] if h < 3 else bank(2)[:, 0:VW]
                    dve.scalar_tensor_tensor(Cst[:, 4 * d + h, :], Cst[:, 4 * d + h, :], dnb[:, 4 * d + h, c:c + 1], o,
                                             ALU.mult, ALU.add).then_inc(S("scan_c"), 1)
                if has:
                    hv = hsum[:, c - CT, :].rearrange("p (h n) -> p h n", h=NH)
                    first = not any(s[1] == c for s in steps[:i])
                    for h in range(NH):
                        if first:
                            ins = dve.tensor_scalar(hv[:, h, :], ob[:, h, 0:DH], rec[:, h:h + 1], None, ALU.mult)
                        else:
                            ins = dve.scalar_tensor_tensor(hv[:, h, :], ob[:, h, 0:DH], rec[:, h:h + 1], hv[:, h, :], ALU.mult, ALU.add)
                    ins.then_inc(S("scan_out"), 1)
                    dve.wait_ge(S("scan_out"), no + 1)
            dve.wait_ge(S("o_ev"), 8)
            for t in range(TT):
                dve.wait_ge(S("hm_mm"), t + 1)
                dve.tensor_tensor(hmT[:, :, span(t)], bank(4 + t % 2).rearrange("p (h n) -> p h n", h=NH), oT[:, :, span(t)],
                                  ALU.mult).then_inc(S("hm_ev"), 1)
            for j in range(16):
                dve.wait_ge(S("mg_sig"), 2 * (j + 1))
                dve.wait_ge(S("mg_y"), j + 1)
                for i in range(2):
                    dve.tensor_tensor(sgd[:, j % 2, i, :], sg[:, j % 2, i, :], bank(4 * (j % 2) + 2 + i), ALU.mult).then_inc(S("mg_mul"), 1)
                dve.wait_ge(S("mg_mul"), 2 * (j + 1))
                dve.tensor_tensor(mT[:, j // 2, (j % 2) * HALF:(j % 2 + 1) * HALF], sgd[:, j % 2, 0, :], sgd[:, j % 2, 1, :],
                                  ALU.add).then_inc(S("mg_add"), 1)
            if stop < 7:
                return
            dve.wait_ge(S("const2"), 16 * 6)
            for i in range(2):
                dve.tensor_tensor_reduce(out=lamx[:, i, :], in0=lamb[:, 2 * i, :], in1=lamb[:, 2 * i + 1, :], scale=1.0, scalar=0.0,
                                         op0=ALU.mult, op1=ALU.add, accum_out=lsums[:, i:i + 1]).then_inc(S("lam_sum"), 1)
            dve.wait_ge(S("lam_exp"), 1)
            link(dve.tensor_scalar(nlam, lsums[:, 1:2], lsums[:, 0:1], LAM0, ALU.subtract, ALU.subtract))
            link(dve.tensor_scalar(nsink, sinkb, -1.0, None, ALU.mult))
            for i in range(4):
                link(dve.tensor_scalar(gcol[:, 8 + i:9 + i], gcol[:, 2 * i:2 * i + 1], HD ** -0.5, None, ALU.mult))
            link(dve.tensor_scalar(gcol[:, 13:14], gcol[:, 12:13], 1.0 - LAM0, None, ALU.mult))
            dve.wait_ge(S("x_again"), 16)
            dve.wait_ge(S("ga1"), 16)
            for j in range(2 * TT + 2):
                if j < 2 * TT:
                    m, t = j // TT, j % TT
                    ms, part = slice(m * HALF, (m + 1) * HALF), extra[:, (j % 2) * HALF:(j % 2 + 1) * HALF]
                    dve.wait_ge(S("wo_mm"), before("wo_mm") + j + 1)
                    link(dve.tensor_tensor(part, bank(j % 4), ga1b[:, ms], ALU.mult))
                    dve.tensor_tensor(x1[:, t, ms], part, x1[:, t, ms], ALU.add).then_inc(S("wo_ev"), 1)
                i = j - TT
                if 1 <= i <= TT:
                    N2.scale(dve, link, i - 1)
                if 2 <= i:
                    N2.evac_dve(dve, i - 2)
            dve.wait_ge(S("logits"), TT)
            dve.tensor_reduce(lmax, bank(6)[:, 0:P].rearrange("p (t e) -> p t e", e=NEXP), AX.X, ALU.max, negate=True).then_inc(S("lmax"), 1)
            dve.wait_ge(S("lexp"), TT)
            link(dve.reciprocal(lmax, lsum))
            for t in range(TT):
                ins = dve.tensor_scalar(aff[:, t, :], aff[:, t, :], lmax[:, t:t + 1], None, ALU.mult)
            ins.then_inc(S("aff"), 1)
            dve.wait_ge(S("affT"), 1)
            link(dve.tensor_copy(affT, psum[0:NEXP, HALF:3 * HALF]))
            for r in range(CAP // 8):
                v = vals[:, 8 * r:8 * r + 8]
                link(dve.max(v, affT))
                link(dve.max_index(idx[:, 8 * r:8 * r + 8], v, affT))
                link(dve.match_replace(affT, v, affT, -1.0))
            dve.tensor_copy(idxf, idx).then_inc(S("topk"), 1)
            dve.wait_ge(S("picked"), 1)
            link(dve.tensor_copy(valc, bank(3)[:, 0:NEXP]))
            dve.tensor_copy(idxc, bank(3)[:, NEXP:2 * NEXP]).then_inc(S("route"), 1)
            dve.wait_ge(S("ga2"), 16)

            def x_evac(e):
                dve.wait_ge(S("moe_xtr"), e * 2 + 2)
                for k in range(4, 8):
                    ins = dve.tensor_scalar(xsT[:, k, :], bank(7)[:, span(k - 4)], mod[:, 2 * KT + k:2 * KT + k + 1],
                                            adaT[:, 3 * KT + k:3 * KT + k + 1], ALU.mult, ALU.add)
                ins.then_inc(S("moe_xevD"), 1)

            def hidden_of(e):
                for m in range(2):
                    ms = slice(m * HALF, (m + 1) * HALF)
                    dve.wait_ge(S("moe_sil"), e * 2 + m + 1)
                    dve.wait_ge(S("moe_u"), e * 2 + m + 1)
                    dve.tensor_tensor(hid[:, ms], sgate[:, ms], bank(2 + m), ALU.mult).then_inc(S("moe_hid"), 1)

            def h_evac(e):
                dve.wait_ge(S("moe_htr"), e * 2 + 2)
                dve.tensor_copy(hd[:, HALF:D], bank(7)).then_inc(S("moe_hevD"), 1)

            def outputs(e):
                for m in range(2):
                    ms = slice(m * HALF, (m + 1) * HALF)
                    dve.wait_ge(S("moe_d"), e * 2 + m + 1)
                    dve.scalar_tensor_tensor(yb[:, ms], bank(4 + m), valc[:, bass.ds(e, 1)], ga2b[:, ms],
                                             ALU.mult, ALU.mult).then_inc(S("moe_y"), 1)

            x_evac(0)
            hidden_of(0)
            x_evac(1)
            h_evac(0)

            def turn(e, more):
                dve.wait_ge(S("moe_htr"), e * 2)
                hidden_of(e)
                if not isinstance(e, int) or e >= 2:
                    dve.wait_ge(S("moe_sct"), e * 16 - 16)
                outputs(e - 1)
                if more:
                    x_evac(e + 1)
                h_evac(e)

            turn(1, True)
            with dve.Fori(2, NEXP - 1) as e:
                turn(e, True)
            turn(NEXP - 1, False)
            dve.wait_ge(S("moe_sct"), 16 * NEXP - 16)
            outputs(NEXP - 1)
            if stop < 8:
                return

            def qk_dve(*keys, norm=None, norms=None):
                items = rows_of(keys)
                for i, (key, t) in enumerate(items):
                    if norm and i + 1 < TT:
                        norm.evac_dve(dve, i + 1)
                        if i + 2 < TT:
                            norms(i + 2)
                    ncol = QK[key][2]
                    nh, q = ncol // HD, 24 * (i % 2)
                    r = qst[:, q + 16:q + 16 + nh]
                    dve.wait_ge(S(key + "_sq"), before(key + "_sq") + t + 1)
                    dve.tensor_reduce(qst[:, q:q + nh], sqz[i % 2][:, 0:ncol].rearrange("p (h d) -> p h d", d=HD),
                                      AX.X, ALU.add).then_inc(S(key + "_ss"), 1)
                    dve.wait_ge(S(key + "_rt"), before(key + "_rt") + t + 1)
                    link(dve.reciprocal(r, qst[:, q + 8:q + 8 + nh]))
                    if i >= 2:
                        pkey, pu = items[i - 2]
                        dve.wait_ge(S(pkey + "_tr"), before(pkey + "_tr") + pu + 1)
                    z, o = bank(i % 3)[:, 0:ncol], zn[i % 2][:, 0:ncol]
                    if key == "cq":
                        for hh in range(2):
                            ins = dve.tensor_tensor(o.rearrange("p (c h d) -> p h c d", c=4, h=2)[:, hh],
                                                    z.rearrange("p (h c d) -> p h c d", h=2, c=4)[:, hh],
                                                    r[:, 4 * hh:4 * hh + 4].unsqueeze(2).to_broadcast([P, 4, HD]), ALU.mult)
                    else:
                        ins = dve.tensor_tensor(o.rearrange("p (h d) -> p h d", d=HD), z.rearrange("p (h d) -> p h d", d=HD),
                                                r.unsqueeze(2).to_broadcast([P, nh, HD]), ALU.mult)
                    ins.then_inc(S(key + "_zn"), 1)
                    if key == "ck":
                        dve.tensor_copy(v2[:, t, 0:P], bank(i % 3)[:, P:2 * P]).then_inc(S("cv_ev"), 1)

            def attn_dve(name):
                at = ATT[name]
                nbuf = len(SBUFS[name])

                def scores(g):
                    bias = bias_ready(dve, name, g)
                    for i, (c, h, b, qc, row, kc, k0, nk) in enumerate(at.groups[g]):
                        v = g * at.comps + i
                        dve.wait_ge(S(name + "_qk"), before(name + "_qk") + v + 1)
                        if v >= nbuf:
                            dve.wait_ge(S(name + "_tr"), before(name + "_tr") + (v - nbuf) // at.comps + 1)
                        o = {"A": (TT - 1 - b) * P, "B": 0, "C": (2 - nk) * P, "D": 0}[name]
                        bv = bias[:, 0:nk * P][:, ::-1] if name == "D" else bias[:, o:o + nk * P]
                        init = nsink[:, 2 * c + h:2 * c + h + 1] if name == "C" else 3.0e38
                        dve.tensor_tensor_reduce(out=SBUFS[name][v % nbuf][:, 0:nk * P],
                                                 in0=psum[:, 2 * (v % 2) * HALF:2 * (v % 2) * HALF + nk * P],
                                                 in1=bv, scale=-1.0, scalar=init, op0=ALU.add, op1=ALU.min,
                                                 accum_out=nmx[:, v % 8:v % 8 + 1]).then_inc(S(name + "_s"), 1)

                def weights(g):
                    nk, v = at.groups[g][0][7], 2 * g
                    dve.wait_ge(S("A_e"), before("A_e") + v + 2)
                    link(dve.reciprocal(rinv[:, v % 8:v % 8 + 2], esum[:, v % 8:v % 8 + 2]))
                    e0, e1 = (SBUFS[name][(v + i) % nbuf][:, 0:nk * P] for i in range(2))
                    r1 = rinv[:, v % 8 + 1:v % 8 + 2]
                    link(dve.tensor_scalar(r1, r1, nlam, esum[:, v % 8:v % 8 + 1], ALU.mult, ALU.mult))
                    dve.scalar_tensor_tensor(e0, e1, r1, e0, ALU.mult, ALU.add).then_inc(S("A_w"), 1)

                def empty(g):
                    nk = at.groups[g][0][7]
                    if nk > 4:
                        dve.wait_ge(S(name + "_tr"), before(name + "_tr") + g + 1)
                        dve.tensor_copy(wT[g % 2][:, 4:nk, :], bank(5)[:, 0:(nk - 4) * P].rearrange("p (k n) -> p k n", n=P)).then_inc(S(name + "_wevD"), 1)

                def outputs(g):
                    c, h, b, qc, row, kc, k0, nk = at.groups[g][0]
                    r = g % 8
                    if name != "A":
                        dve.wait_ge(S(name + "_e"), before(name + "_e") + g + 1)
                        if name == "C":
                            dve.wait_ge(S("C_sink"), g + 1)
                            link(dve.tensor_tensor(esum[:, r:r + 1], esum[:, r:r + 1], esk[:, r:r + 1], ALU.add))
                        link(dve.reciprocal(rinv[:, r:r + 1], esum[:, r:r + 1]))
                    dve.wait_ge(S(name + "_pv"), before(name + "_pv") + g + 1)
                    if c >= 2:
                        dve.wait_ge(S(name + "_otr"), before(name + "_otr") + 2 * (c - 1))
                    if name == "A":
                        q = 2 * g % 8
                        ins = dve.tensor_scalar(obuf[c % 2][:, b, :], bank(6)[:, 0:P], rinv[:, q:q + 1], None, ALU.mult)
                    else:
                        ins = dve.tensor_scalar(obuf[c % 2][:, b, h * HD:(h + 1) * HD], bank(6)[:, 0:HD], rinv[:, r:r + 1], None, ALU.mult)
                    ins.then_inc(S(name + "_o"), 1)

                def complete(c):
                    dve.wait_ge(S("A_ort"), c + 1)
                    link(dve.reciprocal(qst[:, 16:24], qst[:, 8:16]))
                    for b in range(TT):
                        ins = dve.tensor_scalar(obuf[c % 2][:, b, :], obuf[c % 2][:, b, :], qst[:, 16 + b:17 + b], None, ALU.mult)
                    ins.then_inc(S("A_on"), 1)

                for a, b, c, done in at.steps():
                    if b is not None and name == "A":
                        weights(b)
                    if a is not None:
                        scores(a)
                    if b is not None:
                        empty(b)
                    if c is not None:
                        outputs(c)
                    if name == "A":
                        for chunk in done:
                            complete(chunk)

            def gates_dve(key, layer):
                at = ATT[key[0].upper()]
                for j in range(8):
                    n = slice((j % 2) * HALF, (j % 2 + 1) * HALF)
                    dve.wait_ge(S(key + "_sg"), before(key + "_sg") + j + 1)
                    o = M2[layer][:, at.mix0 + j // 2, n]
                    dve.tensor_tensor(o, o, sgt[j % 2], ALU.mult).then_inc(S(key + "_mul"), 1)

            def v_dve(key):
                evac(dve, key, TT, lambda j: copy(dve, v2[:, j, :], bank(6 + j % 2)))

            def out_dve(layer):
                dve.wait_ge(S(f"res{layer}_in"), before(f"res{layer}_in") + 16)
                for j in range(2 * TT + (0 if layer else 2)):
                    m, t = j // TT, j % TT
                    if j < 2 * TT:
                        ms = slice(m * HALF, (m + 1) * HALF)
                        dve.wait_ge(S(f"wo{layer}_mm"), before(f"wo{layer}_mm") + j + 1)
                        dve.tensor_tensor(x3[:, t, ms], bank(j % 4), R2[layer][:, t, ms], ALU.add).then_inc(S(f"wo{layer}_ev"), 1)
                    i = j - TT
                    if layer == 0 and 1 <= i <= TT:
                        N4.scale(dve, link, i - 1)
                    if layer == 0 and 2 <= i:
                        N4.evac_dve(dve, i - 2)

            def norms(t):
                dve.wait_ge(S("nf_rt"), t + 1)
                link(dve.reciprocal(stat[:, 32 + t:33 + t], stat[:, 16 + t:17 + t]))
                dve.scalar_tensor_tensor(x1[:, t, :], x1[:, t, :], stat[:, 32 + t:33 + t], gfb, ALU.mult, ALU.mult).then_inc(S("xb"), 1)
                N3.scale(dve, link, t)

            dve.wait_ge(S("gf"), 16)
            norms(0)
            N3.evac_dve(dve, 0)
            norms(1)
            qk_dve("aq", "ak", norm=N3, norms=norms)
            v_dve("av")
            dve.wait_ge(S("res0_out"), before("res0_out") + 16)
            dve.memset(att[:, 57:58], 0.0)
            attn_dve("A")
            dve.wait_ge(S("forget_ln"), 1)
            link(dve.tensor_scalar(frow[0], frow[0], 0.0, None, ALU.min))
            link(dve.tensor_tensor(frow[1], frow[1], frow[0], ALU.subtract))
            link(dve.memset(frow[2], 1.0))
            dve.tensor_tensor_scan(frow[0], frow[2], frow[1], 0.0, ALU.mult, ALU.add).then_inc(S("forget"), 1)
            dve.wait_ge(S("ncum_out"), 16)
            qk_dve("bq", "bk")
            v_dve("bv")
            attn_dve("B")
            gates_dve("ag", 0)
            gates_dve("bg", 0)
            out_dve(0)
            dve.wait_ge(S("res1_out"), before("res1_out") + 16)
            qk_dve("cq", "ck")
            attn_dve("C")
            qk_dve("dq", "dk")
            v_dve("dv")
            attn_dve("D")
            gates_dve("cg", 1)
            gates_dve("dg", 1)
            out_dve(1)
    return


SCRATCH = {"fu": (P, 4, D), "ada": (6 * D,), "acc": (SEQ, D), "xn": (SEQ, D), "xb": (SEQ, D), "x3": (SEQ, D), "ncum": (8, SEQ)}


def host_layout(i):
    n = np.arange(SEQ)
    ang = 2 * np.pi * ((n[:, None] * n[None, :]) % SEQ) / SEQ
    norm = 1.0 / math.sqrt(SEQ * P)
    m = np.arange(P)
    angc = 2 * np.pi * ((m[:, None] * m[None, :]) % P) / P
    w_in = i["w_in"][0]
    colT = lambda v: np.ascontiguousarray(v.reshape(-1, P).T)
    g = w_in[:, 2560:2576].reshape(D, 4, NH)
    wg = np.zeros((D, 2, NG), np.float32)
    bg = np.zeros((NG, 2), np.float32)
    for k in range(2):
        wg[:, k, 0:NH], wg[:, k, BWD:NG] = g[:, k], g[:, 2 + k]
        bg[0:NH, k], bg[BWD:NG, k] = i["b_gates"][0, k], i["b_gates"][0, 2 + k]
    sel = np.zeros((NG, 8, P), np.float32)
    for c in range(8):
        sel[c if c < NH else BWD + c - NH, c] = 1
    lower, upper = m[:, None] <= m[None, :], m[:, None] >= m[None, :]
    masks = np.stack([np.where(q, 0, NEG) for q in (lower, upper)])
    col = np.arange(SEQ)
    dist = np.abs(m[:, None] - (col[None, :] - (SEQ - P)))
    hide = (col[None, :] - (SEQ - P)) // HD > m[:, None] // HD
    slope = lambda n: 2.0 ** (-8.0 * np.arange(1, n + 1) / n)
    strip_a = np.stack([np.where(hide, NEG, -q * dist) for q in slope(4)]).astype(np.float32)
    col = np.arange(2 * P)
    dist = np.abs(m[:, None] - (col[None, :] - P))
    step = m[:, None] // HD + 2 - col[None, :] // HD
    strip_c = np.stack([np.where((step < 0) | (step > 2), NEG, -q * dist) for q in slope(8)]).astype(np.float32)
    rel = np.ascontiguousarray(np.pad(i["d_rel_bias_2"][0], ((0, 0), (64, 384)), mode="edge"))
    return {
        "x": i["x"][0], "ctx": i["ctx"][0], "w_ada": i["w_ada"][0], "w_in": w_in,
        "w_fourier": i["w_fourier"][0], "w_mlstm": i["w_mlstm"][0], "w_out": i["w_out"][0],
        "cT": np.ascontiguousarray(np.stack([i["c"][0], i["c_ctx"]]).reshape(2, KT, P).transpose(2, 1, 0)).reshape(P, -1),
        "b_adaT": colT(i["b_ada"][0]),
        "gT": np.concatenate([colT(v) for v in (i["g_norm1"][0], i["g_norm2"][0], i["even_ln_g_2"][0],
                                                i["odd_ln_g_2"][0], i["g_final"])], 1),
        "w_convT": np.ascontiguousarray(i["w_conv"][0].reshape(9, 8, P).transpose(2, 1, 0)).reshape(P, -1),
        "w_mgate": np.ascontiguousarray(wg.reshape(KT, P, 2, NG).transpose(1, 0, 2, 3)).reshape(P, -1),
        "w_routerT": np.ascontiguousarray(i["w_router"][0].reshape(KT, P, NEXP).transpose(1, 0, 2)).reshape(P, -1),
        "w_gate": i["w_gate_e"][0], "w_up": i["w_up_e"][0], "w_down": i["w_down_e"][0], "g_final": i["g_final"],
        "even_w_in": i["even_w_in_2"][0], "even_w_out": i["even_w_out_2"][0],
        "odd_w_in": i["odd_w_in_2"][0], "odd_w_out": i["odd_w_out_2"][0],
        "lams": np.concatenate([i[f"a_lambda_{n}_2"][0] for n in ("q1", "k1", "q2", "k2")]),
        "sinks": i["c_sinks_2"][0],
        "qk_gains": np.stack([np.tile(i[f"{n}_norm_g_2"][0], 2) for n in ("a_q", "a_k", "b_q", "b_k", "c_q", "c_k", "d_q", "d_k")], 1),
        "sub_gain": i["a_subln_g_2"][0].reshape(P, 1),
        "w_forget": np.ascontiguousarray(i["even_w_in_2"][0][:, 4096:4104].reshape(KT, P, 8).transpose(1, 0, 2)).reshape(P, -1),
        "b_forget": i["b_forget_bias_2"][0].reshape(8, 1),
        "strip_a": strip_a, "strip_c": strip_c, "rel": rel,
        "b_gate": bg, "sel": sel.reshape(NG, -1),
        "ident": np.eye(P, dtype=np.float32), 
        "masks": np.concatenate([np.tile(q, (1, NH)) for q in masks], 1).astype(np.float32),
        "dftc": np.concatenate([np.cos(angc), -np.sin(angc)], 1).astype(np.float32),
        "dft_cos": (np.cos(ang) * norm).astype(np.float32), "dft_sin": (np.sin(ang) * norm).astype(np.float32),
    }


def kernel(**inputs):
    import concourse.bacc as bacc
    from concourse.bass_utils import run_bass_kernel_spmd

    arrays = host_layout({n: np.asarray(v) for n, v in inputs.items()})
    nc = bacc.Bacc("TRN2", target_bir_lowering=False, num_devices=1)
    a = {n: nc.dram_tensor("in_" + n, v.shape, mybir.dt.from_np(v.dtype), kind="ExternalInput").ap() for n, v in arrays.items()}
    out = nc.dram_tensor("out", (SEQ, D), F32, kind="ExternalOutput").ap()
    scratch = {n: nc.dram_tensor("scratch_" + n, v, F32, kind="Internal").ap() for n, v in SCRATCH.items()}
    build(nc, a, out, scratch)
    r = run_bass_kernel_spmd(nc, [{"in_" + n: v for n, v in arrays.items()}], core_ids=[0])
    return r.results[0]["out"].reshape(1, SEQ, D)
```

```python
import math
from contextlib import ExitStack

import numpy as np
import concourse.bass as bass
from concourse import mybir

F32 = mybir.dt.float32
BF16 = mybir.dt.bfloat16
F32R = mybir.dt.float32r
I32 = mybir.dt.int32
U32 = mybir.dt.uint32
ALU = mybir.AluOpType
ACT = mybir.ActivationFunctionType
AX = mybir.AxisListType

P = 128
D = 1024
SEQ = 1024
CTX = 256
KT = D // P
TT = SEQ // P
CT = CTX // P
HALF = 512
EPS = 1e-6
NH, DH = 4, 128
GRID_W = 64
GRID_H = SEQ // GRID_W
NCH = CT + TT
KSC = DH ** -0.5
NEXP, CAP = 16, 128
RING = 3
BWD = 32
NG = BWD + NH
FROW = 64
NEG = -1e30


HD = 64
LAM0 = 0.8 - 0.6 * math.exp(0.0)


class Attn:

    def __init__(self, p, layer, mix0, comps, span, dv, kv_shared=False):
        self.p, self.layer, self.mix0, self.comps, self.dv = p, layer, mix0, comps, dv
        self.units, self.groups = [], []
        for c in range(4):
            blocks = [b for i in range(TT // 2) for b in (TT - 1 - i, i)]
            order = [(b, h) for b in blocks for h in range(2)] if comps == 2 else [(b, h) for h in range(2) for b in blocks]
            for b, h in order:
                k0 = max(0, b - span)
                head = 2 * c + h
                qc, row = (head % 4, HD * (head // 4)) if kv_shared else (c, HD * h)
                self.units.append((c, h, b, qc, row, 0 if kv_shared else c, k0, b - k0 + 1))
        for i in range(0, len(self.units), comps):
            self.groups.append(self.units[i:i + comps])
        G = len(self.groups)
        self.G = G
        self.big = [sum(1 for g in self.groups[:u] if g[0][7] > 4) for u in range(G + 1)]
        self.last = {}
        for u, g in enumerate(self.groups):
            self.last[g[0][0]] = u
        self.per_bias = G // 4 if comps == 2 else G // 8
        self.nbias = G // self.per_bias
        self.lag = {"A": 1, "B": 2, "C": 3, "D": 3}[p]

    def steps(self):
        n = self.G
        for i in range(n + self.lag + 5):
            pick = lambda j: j if 0 <= j < n else None
            yield (pick(i), pick(i - self.lag), pick(i - self.lag - 1),
                   [c for c, u in self.last.items() if i == u + self.lag + 2], [c for c, u in self.last.items() if i == u + self.lag + 4])


def build(nc, a, out, scratch):
    ctx = ExitStack()
    sems, shared = {}, {}

    def S(name):
        name = shared[name][0] if name in shared else name
        if name not in sems:
            sems[name] = ctx.enter_context(nc.semaphore(name))
        return sems[name]

    class Chain:

        def __init__(self, eng, name):
            self.eng, self.sem, self.n, self.loop = eng, S(name), 0, 0

        def __call__(self, ins):
            self.n += 1
            ins.then_inc(self.sem, 1)
            self.eng.wait_ge(self.sem, self.loop + self.n)

    with ctx:
        ATT = {"A": Attn("A", 0, 0, 2, TT, 2 * HD), "B": Attn("B", 0, 4, 1, TT, HD),
               "C": Attn("C", 1, 0, 1, 1, HD, kv_shared=True), "D": Attn("D", 1, 4, 1, 4, HD)}

        def share(kind, stages):
            total = {}
            for prefix, signals in stages:
                for sig, n in signals.items():
                    shared[prefix + sig] = (kind + sig, total.get(sig, 0))
                    total[sig] = total.get(sig, 0) + n

        def before(name):
            return shared[name][1] if name in shared else 0

        share("norm", [(p, {"_sq": t, "_rt": t, "_xn": t, "_tr": 2 * t, "_evA": t, "_evD": t})
                       for p, t in (("n1", TT), ("nc", CT), ("n2", TT), ("n3", TT), ("n4", TT))])
        share("plain", [(p, {"_mm": j, "_evA": (j + 1) // 2, "_evD": j // 2})
                        for p, j in (("ada", 12), ("u", TT), ("dft", 8), ("av", TT), ("bv", TT), ("dv", TT))])
        share("proj", [(p, {q: TT for q in ("_z", "_sq", "_ss", "_rt", "_zn", "_tr", "_evA")})
                       for p in ("aq", "ak", "bq", "bk", "cq", "ck", "dq", "dk")])
        share("sigate", [(p, {"_mm": 16, "_sg": 16, "_mul": 16, "_h": 2 * KT, "_l": 2 * KT}) for p in ("g0", "g1")])
        share("wout", [(p, {"_mm": 2 * TT, "_ev": 2 * TT}) for p in ("wo", "wo0", "wo1")])
        share("res", [(p, {"_out": 16}) for p in ("res0", "res1")])
        share("back", [(p, {str(i): 16 for i in range(4)}) for p in ("x_again", "x2_in", "res0_in", "res1_in")])
        share("attn", [(n, {"_qk": len(at.units), "_s": len(at.units), "_e": len(at.units), "_w": at.G if n == "A" else 0, "_tr": at.G,
                            "_wevA": at.G, "_wevD": at.big[at.G], "_pv": at.G, "_o": at.G, "_on": 4 if n == "A" else 0, "_otr": 8, "_mix": 8,
                            **({} if n == "D" else {"_bias0": 64, "_bias1": 0 if n == "A" else 64})})
                       for n, at in ATT.items()])

        def sb(name, cols, dt=F32, parts=P):
            return ctx.enter_context(nc.sbuf_tensor(name, [parts, cols], dt))

        REGIONS = (("ring", RING * KT * HALF),
                   ("hidden", KT * SEQ),
                   ("ctx_hidden", KT * CTX),
                   ("pair", 8192),
                   ("wide", 9256),
                   ("small", 6500),
                   ("kctx", NH * CTX), ("cols", NCH * 4 * NG),
                   ("sel_wT", 8 * P))
        with ExitStack() as views:
            split = {n: views.enter_context(nc.sbuf_tensor(n + "_r", [P, c], F32R)) for n, c in REGIONS}
        ring, hidden, ctx_hidden, pair, wide, small, kctx, cols, sel_wT = (sb(n, c) for n, c in REGIONS)
        ident = sb("ident", P)
        identb = sb("identb", P, BF16)
        maskb = sb("maskb", 2 * NH * P, BF16)
        sel = sel_wT[0:NG, :]
        dftc = sb("dftc", 2 * P + 1)
        cT = sb("cT", KT * 2)
        csil = sb("csil", KT * 2)
        adaT = sb("adaT", 2 * 48)
        badaT = sb("badaT", 48)
        gT = sb("gT", 5 * KT)
        mod = sb("mod", 3 * KT)
        wconv = sb("wconv", 8 * 9)
        lam_f = sb("lam_f", 448)
        bgate = sb("bgate", 2)
        epsc = sb("epsc", 1)
        onec = sb("onec", 1)
        wrt = sb("wrt", KT * NEXP)
        extra = sb("extra", SEQ)
        wgate = extra[:, 0:KT * (FROW + NG)]
        att = sb("att", 64)
        qst = sb("qst", 48)
        gcol = sb("gcol", 16)
        wbf = lam_f[:, 384:448]
        bbf = sb("bbf", 1)
        stat = sb("stat", 64)
        psum = ctx.enter_context(nc.psum_tensor("psum", [P, 8 * HALF], F32))

        def bank(b):
            return psum[:, b * HALF:(b + 1) * HALF]

        def ringv(s):
            return ring[:, s * KT * HALF:(s + 1) * KT * HALF].rearrange("p (k n) -> p k n", k=KT)

        hT = hidden[:].rearrange("p (k n) -> p k n", k=KT)
        hcT = ctx_hidden[:].rearrange("p (k n) -> p k n", k=KT)
        x_sb = wide[:, 0:TT * D].rearrange("p (t n) -> p t n", t=TT)
        xn_buf = small[:, 0:2 * D].rearrange("p (b n) -> p b n", b=2)
        sq_buf = small[:, 2 * D:3 * D]
        cx_sb = small[:, 3 * D:5 * D].rearrange("p (t n) -> p t n", t=CT)
        mask_in = ctx_hidden[:, 0:2 * NH * P]
        adarow = pair[0:2, 0:6 * D]
        u_sb = small[:, 0:4 * D].rearrange("p (t n) -> p t n", t=TT)
        pq = pair[:, 0:4 * D].rearrange("p (a c n) -> p a c n", a=2, c=4)
        middle = stat[:, 56:60]
        sinp = [pair[:, 4 * D + i * HALF:4 * D + (i + 1) * HALF] for i in range(2)]
        fuT = wide[:, 0:4 * D].rearrange("p (c n) -> p c n", c=4)

        tiles, place, last_read = [], {}, []

        def kview(w, c0, n=HALF, r0=0, rows=D):
            return w[r0:r0 + rows, c0:c0 + n].rearrange("(k p) n -> p k n", p=P)

        def add_tile(key, read, w, c0, n=HALF):
            place[key] = len(tiles)
            last_read.append(read)
            tiles.append([(0, 4, n, kview(w, c0, n, 0, 512)), (4, 4, n, kview(w, c0, n, 512, 512))])

        OFF_QK, OFF_V, OFF_O, OFF_G, OFF_BR = 512, 1536, 2048, 2560, 2576
        for j in range(12):
            add_tile(("ada", j), ("ada_mm", j + 1), a["w_ada"], j * HALF)
        add_tile("f", ("u_mm", TT), a["w_in"], 0)
        add_tile("cos", ("dft_mm", 4), a["dft_cos"], 0)
        add_tile("sin", ("dft_mm", 8), a["dft_sin"], 0)
        add_tile("q", ("qk_mm", NH), a["w_in"], OFF_QK)
        add_tile("k", ("qk_mm", 2 * NH), a["w_in"], OFF_QK + 512)
        add_tile("v", ("v_mm", NCH), a["w_in"], OFF_V)
        add_tile("o", ("o_mm", 8), a["w_in"], OFF_O)
        for m in range(2):
            place["fm", m] = len(tiles)
            last_read.append(("mg_y", 8 * (m + 1)))
            tiles.append([(0, 4, HALF, kview(a["w_fourier"], m * HALF, rows=512)),
                          (4, 4, HALF, kview(a["w_mlstm"], m * HALF, rows=512))])
            add_tile(("br1", m), ("mg_y", 8 * (m + 1)), a["w_in"], OFF_BR + m * HALF)
            add_tile(("br2", m), ("mg_y", 8 * (m + 1)), a["w_in"], OFF_BR + D + m * HALF)
        for m in range(2):
            add_tile(("wo", m), ("wo_mm", TT * (m + 1)), a["w_out"], m * HALF)

        n_moe = len(tiles)
        for e in range(NEXP + 1):
            if e < NEXP:
                for key, sig in (("gate", "moe_g"), ("up", "moe_u")):
                    for m in range(2):
                        add_tile((key, e, m), (sig, 2 * e + m + 1), a["w_" + key][e], m * HALF)
            if e >= 1:
                for m in range(2):
                    add_tile(("down", e - 1, m), ("moe_d", 2 * (e - 1) + m + 1), a["w_down"][e - 1], m * HALF)
        turn0 = n_moe + 4
        for layer, w, plan in ((0, a["even_w_in"], (("aq", 0), ("ak", 512), ("av", 1024), ("bq", 2048), ("bk", 2560), ("bv", 3072),
                                                    ("ag", 1536), ("bg", 3584))),
                               (1, a["odd_w_in"], (("cq", 0), ("ck", 512), ("dq", 1280), ("dk", 1792), ("dv", 2304),
                                                   ("cg", 768), ("dg", 2816)))):
            for key, c0 in plan:
                sig = {"v": (key + "_mm", TT), "g": (f"g{layer}_mm", 16)}.get(key[1], (key + "_z", TT))
                add_tile(key, sig, w, c0, 256 if key == "ck" else HALF)
            for m in range(2):
                add_tile(("out", layer, m), (f"wo{layer}_mm", TT * (m + 1)), a[("even_w_out", "odd_w_out")[layer]], m * HALF)
        LOOPED = (place["gate", 2, 0], place["down", 15, 0])

        def load_tile(sp, n):
            if n >= RING:
                name, value = last_read[n - RING]
                sp.wait_ge(S(name), before(name) + value)
            for k0, kn, w, src in tiles[n]:
                sp.dma_start(ringv(n % RING)[:, k0:k0 + kn, 0:w], src).then_inc(S(f"ring_full{n % RING}"), 16)

        def tile_ready(pe, key):
            n = place[key]
            pe.wait_ge(S(f"ring_full{n % RING}"), 32 * (n // RING + 1))
            return ringv(n % RING)

        def group(pe, outp, pairs):
            for i, (l, r) in enumerate(pairs):
                mm = pe.matmul(outp, l, r, start=(i == 0), stop=(i == len(pairs) - 1))
            return mm

        def jobs_mm(pe, p, j, nb, outp, pairs):
            if j >= nb:
                pe.wait_ge(S(p + "_ev" + "AD"[j % 2]), before(p + "_ev" + "AD"[j % 2]) + (j - nb) // 2 + 1)
            mm = group(pe, outp, pairs)
            mm.then_inc(S(p + "_mm"), 1)
            return mm

        def emptied(eng, p, jobs):
            eng.wait_ge(S(p + "_evA"), before(p + "_evA") + (jobs + 1) // 2)
            if jobs > 1:
                eng.wait_ge(S(p + "_evD"), before(p + "_evD") + jobs // 2)

        def evac(eng, p, jobs, f):
            side = 0 if hasattr(eng, "activation") else 1
            for j in range(side, jobs, 2):
                eng.wait_ge(S(p + "_mm"), before(p + "_mm") + j + 1)
                f(j).then_inc(S(p + "_ev" + "AD"[side]), 1)

        def copy(eng, o, i):
            return eng.activation(o, i, ACT.Copy) if hasattr(eng, "activation") else eng.tensor_copy(o, i)

        class Norm:

            def __init__(self, p, T, src, ready, col, dst, A, B, banks=lambda t: (2 * (t % 2), 2 * (t % 2) + 1), depth=2, stored=None):
                self.p, self.T, self.src, self.ready, self.col, self.dst, self.A, self.B = p, T, src, ready, col, dst, A, B
                self.banks, self.depth, self.stored = banks, depth, stored

            def wait(self, eng, sig, n):
                eng.wait_ge(S(self.p + sig), before(self.p + sig) + n)

            def squares(self, act, t):
                c = self.col + t
                self.ready(act, t)
                if t:
                    self.wait(act, "_sq", t)
                act.activation(sq_buf, self.src(t), ACT.Square, accum_out=stat[:, c:c + 1]).then_inc(S(self.p + "_sq"), 1)
                self.wait(act, "_sq", t + 1)
                act.activation(stat[:, c + 16:c + 17], stat[:, c:c + 1], ACT.Sqrt, bias=epsc[:, 0:1], scale=1.0 / D).then_inc(S(self.p + "_rt"), 1)

            def scale(self, dve, link, t):
                c = self.col + t
                self.ready(dve, t)
                self.wait(dve, "_rt", t + 1)
                link(dve.reciprocal(stat[:, c + 32:c + 33], stat[:, c + 16:c + 17]))
                if t >= 2:
                    self.wait(dve, "_tr", 2 * (t - 1))
                    if self.stored:
                        self.stored(dve, t - 2)
                dve.tensor_scalar(xn_buf[:, t % 2, :], self.src(t), stat[:, c + 32:c + 33], None, ALU.mult).then_inc(S(self.p + "_xn"), 1)

            def transposes(self, pe, t):
                self.wait(pe, "_xn", t + 1)
                if t >= self.depth:
                    self.wait(pe, "_evA", t - self.depth + 1)
                    self.wait(pe, "_evD", t - self.depth + 1)
                for h in range(2):
                    for k in range(4):
                        mm = pe.transpose(bank(self.banks(t)[h])[:, k * P:(k + 1) * P],
                                          xn_buf[:, t % 2, (4 * h + k) * P:(4 * h + k + 1) * P], ident[:])
                    mm.then_inc(S(self.p + "_tr"), 1)

            def evac_act(self, act, t):
                self.wait(act, "_tr", 2 * t + 1)
                for k in range(4):
                    ins = act.activation(self.dst(t, k), bank(self.banks(t)[0])[:, k * P:(k + 1) * P], ACT.Identity,
                                         bias=(self.B(k) if self.B else 0.0), scale=self.A(k))
                ins.then_inc(S(self.p + "_evA"), 1)

            def evac_dve(self, dve, t):
                self.wait(dve, "_tr", 2 * t + 2)
                for k in range(4, 8):
                    i = bank(self.banks(t)[1])[:, (k - 4) * P:(k - 3) * P]
                    if self.B:
                        ins = dve.tensor_scalar(self.dst(t, k), i, self.A(k), self.B(k), ALU.mult, ALU.add)
                    else:
                        ins = dve.tensor_scalar(self.dst(t, k), i, self.A(k), None, ALU.mult)
                ins.then_inc(S(self.p + "_evD"), 1)

            def done(self, eng, t):
                self.wait(eng, "_evA", t + 1)
                self.wait(eng, "_evD", t + 1)

            def run_act(self, act):
                for t in range(self.T + 1):
                    if t < self.T:
                        self.squares(act, t)
                    if t:
                        self.evac_act(act, t - 1)

            def run_dve(self, dve, link):
                for t in range(self.T + 1):
                    if t < self.T:
                        self.scale(dve, link, t)
                    if t:
                        self.evac_dve(dve, t - 1)

            def run_pe(self, pe):
                for t in range(self.T):
                    self.transposes(pe, t)
                self.done(pe, self.T - 1)

        PADW, PADH = GRID_W + 2, GRID_H + 2
        pads = [small[:, i * 1280:i * 1280 + PADH * PADW] for i in range(2)]
        cpads = [small[:, 2560 + i * 320:2560 + i * 320 + CTX + 2] for i in range(2)]
        accs = [small[:, 3200 + i * 1280:3200 + i * 1280 + SEQ] for i in range(2)]
        caccs = [small[:, 3200 + i * 1280 + SEQ:3200 + (i + 1) * 1280] for i in range(2)]
        qT = pair[:, 0:4 * D].rearrange("p (h n) -> p h n", h=NH)
        kT = pair[:, 4 * D:8 * D].rearrange("p (h n) -> p h n", h=NH)
        kcT = kctx[:].rearrange("p (h n) -> p h n", h=NH)
        VW = DH + 1
        vex = wide[:, 0:NCH * NH * VW].rearrange("p (c h n) -> p c h n", c=NCH, h=NH)
        hsum = wide[:, NCH * NH * VW:NCH * NH * VW + 4 * D].rearrange("p (c n) -> p c n", c=TT)
        mT = wide[:, 0:KT * D].rearrange("p (k n) -> p k n", k=KT)
        TTOT = CTX + SEQ
        rowv = small[0:NG, 0:6400].rearrange("p (a n) -> p a n", n=1280)
        rF, rI, rC, rM, rR = (rowv[:, i, :] for i in (1, 2, 3, 4, 0))
        ones_row = cols[0:NG, 0:P]
        colv = cols[:].rearrange("p (c a g) -> p c a g", c=NCH, a=4)
        Cst = small[:, 1280:1280 + 8 * VW].rearrange("p (c n) -> p c n", c=8)
        kw = small[:, 2312:2312 + 1024].rearrange("p (b h n) -> p b h n", b=2, h=NH)
        se = small[:, 3336:3336 + 1024].rearrange("p (b h n) -> p b h n", b=2, h=NH)
        ee = small[:, 4360:4360 + 1024].rearrange("p (b h n) -> p b h n", b=2, h=NH)
        ob = small[:, 5384:5384 + NH * VW].rearrange("p (h n) -> p h n", h=NH)
        dnb = small[:, 5900:5900 + 8 * NCH].rearrange("p (c n) -> p c n", c=8)
        rec = small[:, 5980:5984]
        oT = pair[:, 0:4 * D].rearrange("p (h n) -> p h n", h=NH)
        hmT = pair[:, 4 * D:8 * D].rearrange("p (h n) -> p h n", h=NH)
        fuR = small[:, 0:4 * D].rearrange("p (c n) -> p c n", c=4)
        sg = small[:, 4 * D:4 * D + 2048].rearrange("p (b a n) -> p b a n", b=2, a=2)
        sgd = ctx_hidden[:].rearrange("p (b a n) -> p b a n", b=2, a=2)

        x1 = hidden[:].rearrange("p (t n) -> p t n", t=TT)
        h2T = pair[:].rearrange("p (k n) -> p k n", k=KT)
        ga1b, ga2b = small[:, 3072:4096], small[:, 4096:5120]
        gfb = wide[:, 6 * D:7 * D]
        affT = ctx_hidden[0:NEXP, 0:SEQ]
        aff = ctx_hidden[:, SEQ:SEQ + P].rearrange("p (t e) -> p t e", e=NEXP)
        route = kctx[:, 0:512]
        vals, idx, idxf = route[0:NEXP, 0:P], route[0:NEXP, P:2 * P].bitcast(U32), route[0:NEXP, 2 * P:3 * P]
        valc, idxc = route[:, 384:400], route[:, 400:416].bitcast(I32)
        idx1 = route[:, 416:420].bitcast(I32)
        lmax, lsum = route[:, 420:428], route[:, 428:436]
        xg, xs, sgate, hid, hd, yb = (wide[:, i * D:(i + 1) * D] for i in range(6))
        xsT, hidT = xs.rearrange("p (k n) -> p k n", k=KT), hd.rearrange("p (k n) -> p k n", k=KT)

        qT2 = wide[:, 0:4 * D].rearrange("p (c n) -> p c n", c=4)
        kT2 = wide[:, 4 * D:8 * D].rearrange("p (c n) -> p c n", c=4)
        v2 = small[:, 0:4 * D].rearrange("p (t n) -> p t n", t=TT)
        obuf = [small[:, (4 + i) * D:(5 + i) * D].rearrange("p (b n) -> p b n", b=TT) for i in range(2)]
        xlay = [pair[:].rearrange("p (k n) -> p k n", k=KT), hidden[:].rearrange("p (k n) -> p k n", k=KT)]
        H2 = xlay
        M2 = xlay[::-1]
        R2 = xlay
        x3 = wide[:, 0:TT * D].rearrange("p (t n) -> p t n", t=TT)
        wT = [w[:].rearrange("p (k n) -> p k n", k=KT) for w in (kctx, sel_wT)]
        sA = [ctx_hidden[:, 0:D], ctx_hidden[:, D:2 * D], wide[:, 8 * D:9 * D], extra[:]]
        SBUFS = {"A": sA, "B": sA[:3], "C": sA, "D": sA}
        BIAS = {"A": [cols[:, 0:D]], "B": [cols[:, 0:D], extra[:]],
                "C": [cols[:, 0:256], cols[:, 256:512]], "D": [cols[:, 0:640], cols[:, 640:1280]]}
        nmx, esum, rinv, esk = (att[:, 8 * i:8 * i + 8] for i in range(4))
        sinkb, nsink, nlam, lsums = att[:, 32:40], att[:, 40:48], att[:, 48:49], att[:, 50:52]
        lamb = lam_f[:, 0:256].rearrange("p (a n) -> p a n", a=4)
        lamx = lam_f[:, 256:384].rearrange("p (a n) -> p a n", a=2)
        sqz, zn = extra[:, 0:HALF], extra[:, HALF:D]
        frow = [small[0:8, i * D:(i + 1) * D] for i in range(3)]
        xsq = cols[:, D:D + P]
        sgt = [extra[:, 0:HALF], extra[:, HALF:D]]
        QK = {"aq": (0, 8, HALF, qT2), "ak": (0, 1, HALF, kT2), "bq": (0, 9, HALF, qT2), "bk": (0, 3, HALF, kT2),
              "cq": (1, 10, HALF, qT2), "ck": (1, 5, P, kT2), "dq": (1, 11, HALF, qT2), "dk": (1, 7, HALF, kT2)}

        PIECES, PK = 4, KT // 4
        WHIGH = [split["small"][:, 4 * D:6 * D].rearrange("p (k n) -> p k n", k=4),
                 split["ctx_hidden"][:, 0:2 * D].rearrange("p (k n) -> p k n", k=4)]
        WHIGH2 = split["small"][:, 0:4 * D].rearrange("p (k n) -> p k n", k=KT)
        XHIGH = [split[n][:, 0:D].rearrange("p (k n) -> p k n", k=KT) for n in ("kctx", "cols")]
        XLOW = [v.rearrange("p (k n) -> p k n", k=KT) for v in (split["sel_wT"][:], split["wide"][:, 8 * D:9 * D])]
        GHIGH = split["wide"][:, 0:4 * D].rearrange("p (k n) -> p k n", k=KT)
        GLOW = split["wide"][:, 4 * D:8 * D].rearrange("p (k n) -> p k n", k=KT)
        JOBS, WSEQ = [], []
        for layer, keys in enumerate((("aq", "ak", "av", "bq", "bk", "bv"), ("cq", "ck", "dq", "dk", "dv"))):
            for key in keys:
                JOBS += [(key + ("_mm" if key[1] == "v" else "_z"), t + 1) for t in range(TT)]
            JOBS += [(f"wo{layer}_mm", j + 1) for j in range(2 * TT)]
            WSEQ += list(keys) + [("ag", "cg")[layer], ("bg", "dg")[layer], ("out", layer, 0), ("out", layer, 1)]

        def whigh(key, k):
            return WHIGH2[:, k, :] if key in ("bg", "dg") else WHIGH[k // 4][:, k % 4, :]

        def ringr(s):
            return split["ring"][:, s * KT * HALF:(s + 1) * KT * HALF].rearrange("p (k n) -> p k n", k=KT)

        class Split:

            def __init__(self, eng):
                self.eng, self.jobs, self.tiles = eng, 0, 0

            def rows_free(self):
                if self.jobs >= 2:
                    name, value = JOBS[self.jobs - 2]
                    self.eng.wait_ge(S(name), before(name) + value)

            def piece_free(self, p):
                q, key = self.tiles, WSEQ[self.tiles]
                if q == 0 or key in ("bg", "dg"):
                    return
                if WSEQ[q - 1] in ("bg", "dg"):
                    g = ("g0", "g1")[WSEQ[q - 1] == "dg"]
                    self.eng.wait_ge(S(g + "_mm"), before(g + "_mm") + 12)
                    return
                jobs = sum(1 for z in WSEQ[:q] if z not in ("ag", "bg", "cg", "dg"))
                if p < PIECES - 1:
                    self.eng.wait_ge(S("w_used"), (PIECES - 1) * (jobs - 1) + p + 1)
                else:
                    name, value = JOBS[TT * jobs - 1]
                    self.eng.wait_ge(S(name), before(name) + value)

            def rows(self, src):
                b, n = self.jobs % 2, self.jobs
                if hasattr(self.eng, "activation"):
                    self.rows_free()
                    self.eng.activation(XHIGH[b], src, ACT.Copy).then_inc(S("x_high"), 1)
                else:
                    self.eng.wait_ge(S("x_high"), n + 1)
                    self.rows_free()
                    self.eng.tensor_tensor(XLOW[b], src, XHIGH[b].bitcast(F32), ALU.subtract).then_inc(S("x_low"), 1)
                self.jobs += 1

            def piece(self, p):
                key = WSEQ[self.tiles]
                wd, ks = (256 if key == "ck" else HALF), slice(PK * p, PK * (p + 1))
                w = tile_ready(self.eng, key)[:, ks, 0:wd]
                high = WHIGH2[:, ks, 0:wd] if key in ("bg", "dg") else WHIGH[p // 2][:, PK * (p % 2):PK * (p % 2 + 1), 0:wd]
                if hasattr(self.eng, "activation"):
                    self.piece_free(p)
                    self.eng.activation(high, w, ACT.Copy).then_inc(S("w_high"), 1)
                else:
                    self.eng.wait_ge(S("w_high"), PIECES * self.tiles + p + 1)
                    self.eng.tensor_tensor(ringr(place[key] % RING)[:, ks, 0:wd], w, high.bitcast(F32), ALU.subtract).then_inc(S("w_low"), 1)
                if p == PIECES - 1:
                    self.tiles += 1

            def weights(self):
                for p in range(PIECES):
                    self.piece(p)

            def product(self, key, t, outp):
                wd = 256 if key == "ck" else HALF
                low = ringr(place[key] % RING)
                b = self.jobs % 2
                self.eng.wait_ge(S("x_low"), self.jobs + 1)
                for k in range(KT):
                    if t == 0 and k % PK == 0:
                        self.eng.wait_ge(S("w_low"), PIECES * WSEQ.index(key) + k // PK + 1)
                    self.eng.matmul(outp, XHIGH[b][:, k, :], whigh(key, k)[:, 0:wd], start=(k == 0), stop=False)
                    self.eng.matmul(outp, XHIGH[b][:, k, :], low[:, k, 0:wd], start=False, stop=False)
                    mm = self.eng.matmul(outp, XLOW[b][:, k, :], whigh(key, k)[:, 0:wd], start=False, stop=(k == KT - 1))
                    if t == TT - 1 and k % PK == PK - 1 and k < KT - 1:
                        mm.then_inc(S("w_used"), 1)
                self.jobs += 1
                return mm

        def next_job(s, i, items, src, then=None):
            if i + 1 < len(items):
                s.rows(src(items[i + 1][1]))
                if items[i + 1][1] == 0:
                    s.weights()

        def rows_of(keys):
            return [(key, t) for key in keys for t in range(TT)]

        steps = []
        for i in range(NCH):
            f = i
            b = (CT - 1 - i) if i < CT else NCH - 1 - (i - CT)
            steps += [(0, f, i >= CT), (1, b, i >= CT)]
        outs_before = [sum(1 for s in steps[:i] if s[2]) for i in range(len(steps) + 1)]

        def span(c):
            return slice(c * P, (c + 1) * P)

        def chain_row(d, h):
            return (BWD if d else 0) + h

        def ksrc(h, c):
            return kcT[:, h, c * P:(c + 1) * P] if c < CT else kT[:, h, (c - CT) * P:(c - CT + 1) * P]

        block = ctx.enter_context(nc.Block())

        @block.sync
        def _(sp):
            for n in range(RING):
                load_tile(sp, n)
            sp.dma_start(x_sb, a["x"].rearrange("(t p) n -> p t n", p=P)).then_inc(S("x_in"), 16)
            sp.dma_start(cx_sb, a["ctx"].rearrange("(t p) n -> p t n", p=P)).then_inc(S("cx_in"), 16)
            for n in range(RING, len(tiles)):
                if n == LOOPED[0]:
                    with sp.Fori(2, NEXP) as e:
                        for j in range(6):
                            name, value = (("moe_u", e * 2), ("moe_d", e * 2 - 3), ("moe_d", e * 2 - 2),
                                           ("moe_g", e * 2 + 1), ("moe_g", e * 2 + 2), ("moe_u", e * 2 + 1))[j]
                            sp.wait_ge(S(name), before(name) + value)
                            w = a[("w_gate", "w_up", "w_down")[j // 2]]
                            w = w[bass.ds(e - j // 4, 1), :, (j % 2) * HALF:(j % 2 + 1) * HALF].rearrange("e (k p) n -> p (e k) n", p=P)
                            q = (turn0 + j) % RING
                            for k0 in (0, 4):
                                sp.dma_start(ringv(q)[:, k0:k0 + 4, :], w[:, k0:k0 + 4, :]).then_inc(S(f"ring_full{q}"), 16)
                if LOOPED[0] <= n < LOOPED[1]:
                    continue
                load_tile(sp, n)
                if n == place["k"]:
                    sp.wait_ge(S("fu_ev"), 9)
                    sp.dma_start(scratch["fu"], fuT).then_inc(S("fu_out"), 16)
                if n == place["br1", 0]:
                    sp.wait_ge(S("scan_out"), TT * 2)
                    sp.wait_ge(S("fu_out"), 16)
                    sp.dma_start(fuR, scratch["fu"]).then_inc(S("fu_in"), 16)

            for q in range(RING):
                sp.wait_ge(S(f"ring_full{q}"), 32 * len(range(q, len(tiles), RING)))

        @block.gpsimd
        def _(pool):
            for o, i in ((badaT[:], a["b_adaT"]), (gT[:], a["gT"]), (ident[:], a["ident"]),
                         (mask_in, a["masks"]), (sel, a["sel"]),
                         (dftc[:], a["dftc"]), (wconv[:], a["w_convT"]), (wgate, a["w_mgate"]),
                         (bgate[0:NG, :], a["b_gate"]), (wrt[:], a["w_routerT"])):
                pool.dma_start(o, i).then_inc(S("const"), 16)
            pool.memset(epsc[:], EPS).then_inc(S("epsc"), 1)
            pool.memset(onec[:], 1.0).then_inc(S("epsc"), 1)

            pool.wait_ge(S("mod"), 2)
            pool.dma_start(scratch["ada"].rearrange("(c p) -> p c", p=P), adaT[:, 0:48], allow_slow_non_contiguous=True).then_inc(S("ada_out"), 16)
            pool.wait_ge(S("ada_out"), 16)
            pool.wait_ge(S("mg_add"), 16)
            for i in range(4):
                pool.dma_start(x1[:, 2 * i:2 * i + 2, :], a["x"].rearrange("(t p) n -> p t n", p=P)[:, 2 * i:2 * i + 2, :]).then_inc(S(f"x_again{i}"), 16)
            pool.dma_start(ga1b, scratch["ada"][2 * D:3 * D].partition_broadcast(P)).then_inc(S("ga1"), 16)
            pool.dma_start(ga2b, scratch["ada"][5 * D:6 * D].partition_broadcast(P)).then_inc(S("ga2"), 16)
            for o, i in ((lamb, a["lams"].partition_broadcast(P)), (sinkb, a["sinks"].partition_broadcast(P)),
                         (gcol[:, 0:8], a["qk_gains"]), (gcol[:, 12:13], a["sub_gain"]), (wbf, a["w_forget"]),
                         (bbf[0:8, :], a["b_forget"])):
                pool.dma_start(o, i).then_inc(S("const2"), 16)
            for t in range(TT):
                pool.wait_ge(S("wo_ev"), before("wo_ev") + TT + t + 1)
                pool.dma_start(scratch["acc"].rearrange("(t p) n -> p t n", p=P)[:, t, :], x1[:, t, :]).then_inc(S("acc_out"), 16)
                pool.wait_ge(S("n2_xn"), before("n2_xn") + t + 1)
                pool.dma_start(scratch["xn"].rearrange("(t p) n -> p t n", p=P)[:, t, :], xn_buf[:, t % 2, :]).then_inc(S(f"xn_out{t % 2}"), 16)
            pool.dma_start(gfb, a["g_final"].partition_broadcast(P)).then_inc(S("gf"), 16)
            pool.wait_ge(S("acc_out"), 16 * TT)
            for q in range(2):
                pool.wait_ge(S(f"xn_out{q}"), 16 * TT // 2)

            pool.wait_ge(S("route"), 1)
            pool.tensor_copy(idx1[:, 0:1], idxc[:, 0:1]).then_inc(S("moe_first"), 1)
            pool.wait_ge(S("moe_first"), 1)
            pool.indirect_dma_start(xg, None, scratch["xn"], bass.IndirectOffsetOnAxis(idx1[:, 0:1].bitcast(U32), 0)).then_inc(S("moe_gat"), 16)
            pool.wait_ge(S("moe_gat"), 16)
            pool.wait_ge(S("moe_xtr"), 2)
            pool.tensor_copy(idx1[:, 0:1], idxc[:, 1:2]).then_inc(S("moe_ix0"), 1)
            pool.wait_ge(S("moe_ix0"), 1)
            pool.indirect_dma_start(xg, None, scratch["xn"], bass.IndirectOffsetOnAxis(idx1[:, 0:1].bitcast(U32), 0)).then_inc(S("moe_gat"), 16)

            def one(e, more):
                if more:
                    pool.wait_ge(S("moe_xtr"), e * 2 + 2)
                    pool.wait_ge(S("moe_gat"), e * 16 + 16)
                    pool.tensor_copy(idx1[:, 0:1], idxc[:, bass.ds(e + 1, 1)])
                    pool.drain()
                    pool.indirect_dma_start(xg, None, scratch["xn"], bass.IndirectOffsetOnAxis(idx1[:, 0:1].bitcast(U32), 0)).then_inc(S("moe_gat"), 16)
                pool.wait_ge(S("moe_y"), e * 2)
                pool.tensor_copy(idx1[:, 1:2], idxc[:, bass.ds(e - 1, 1)])
                pool.drain()
                pool.indirect_dma_start(scratch["acc"], bass.IndirectOffsetOnAxis(idx1[:, 1:2].bitcast(U32), 0), yb, None,
                                        compute_op=ALU.add).then_inc(S("moe_sct"), 16)
                pool.wait_ge(S("moe_sct"), e * 16)

            with pool.Fori(1, NEXP - 1) as e:
                one(e, True)
            one(NEXP - 1, False)
            one(NEXP, False)
            for i in range(TT // 2):
                pool.dma_start(x1[:, 2 * i:2 * i + 2, :], scratch["acc"].rearrange("(t p) n -> p t n", p=P)[:, 2 * i:2 * i + 2, :]).then_inc(S(f"x2_in{i}"), 16)
            for layer in range(2):
                if layer == 0:
                    pool.wait_ge(S("xb"), TT)
                else:
                    pool.wait_ge(S("wo0_ev"), before("wo0_ev") + 2 * TT)
                rows = scratch[("xb", "x3")[layer]].rearrange("(t p) n -> p t n", p=P)
                pool.dma_start(rows, (x1, x3)[layer]).then_inc(S(f"res{layer}_out"), 16)
                for name in ("AB", "CD")[layer]:
                    att = ATT[name]
                    nb = len(BIAS[name])
                    if name == "B":
                        pool.wait_ge(S("forget"), 1)
                        pool.dma_start(scratch["ncum"], frow[0]).then_inc(S("ncum_out"), 16)
                        pool.wait_ge(S("ncum_out"), 16)
                    if name == "A":
                        pool.wait_ge(S("av_mm"), before("av_mm") + TT)
                    for i in range(att.nbias):
                        o = BIAS[name][i % nb]
                        if i >= nb:
                            pool.wait_ge(S(name + "_s"), before(name + "_s") + att.per_bias * att.comps * (i - nb + 1))
                        elif name in "BD":
                            pool.wait_ge(S(name.lower() + "v_mm"), before(name.lower() + "v_mm") + TT)
                        elif name == "C":
                            pool.wait_ge(S("ck_evA"), before("ck_evA") + TT)
                        src = {"A": lambda: a["strip_a"][i], "B": lambda: scratch["ncum"][i].partition_broadcast(P),
                               "C": lambda: a["strip_c"][i],
                               "D": lambda: bass.AP(tensor=a["rel"].tensor, offset=i * 768, ap=[[1, P], [1, 640]])}[name]()
                        if name != "D":
                            pool.dma_start(o, src).then_inc(S(name + f"_bias{i % nb}"), 16)
                        else:
                            pool.dma_start(o, src).then_inc(S(f"D_rel{i % nb}"), 16)
                            pool.wait_ge(S(f"D_rel{i % nb}"), 16 * (i // nb + 1))
                            pool.memset(o[HD:P, 640 - HD:640], NEG).then_inc(S(f"D_bias{i % nb}"), 8)
                            pool.memset(o[0:HD, 0:HD], NEG).then_inc(S(f"D_bias{i % nb}"), 8)
                pool.wait_ge(S(f"g{layer}_l"), before(f"g{layer}_l") + 2 * KT)
                pool.wait_ge(S(f"res{layer}_out"), before(f"res{layer}_out") + 16)
                for i in range(4):
                    pool.dma_start(R2[layer][:, 2 * i:2 * i + 2, :], rows[:, 2 * i:2 * i + 2, :]).then_inc(S(f"res{layer}_in{i}"), 16)
            for t in range(TT):
                pool.wait_ge(S("wo1_ev"), before("wo1_ev") + TT + t + 1)
                pool.dma_start(out.rearrange("(t p) n -> p t n", p=P)[:, t, :], x3[:, t, :]).then_inc(S("out"), 16)
            pool.wait_ge(S("out"), 16 * TT)

        def consts(eng):
            eng.wait_ge(S("const"), 16 * 10)
            eng.wait_ge(S("epsc"), 2)

        xr = lambda eng, t: eng.wait_ge(S("x_in"), 16)
        cr = lambda eng, t: eng.wait_ge(S("cx_in"), 16)
        NX = Norm("n1", TT, lambda t: x_sb[:, t, :], xr, 0, lambda t, k: hT[:, k, t * P:(t + 1) * P],
              lambda k: mod[:, k:k + 1], lambda k: adaT[:, k:k + 1], banks=lambda t: (4 + 2 * (t % 2), 5 + 2 * (t % 2)))
        NC = Norm("nc", CT, lambda t: cx_sb[:, t, :], cr, 8, lambda t, k: hcT[:, k, t * P:(t + 1) * P],
              lambda k: mod[:, KT + k:KT + k + 1], lambda k: adaT[:, 48 + k:48 + k + 1], banks=lambda t: (4 * t, 4 * t + 1))

        W1 = lambda eng, t: eng.wait_ge(S("wo_ev"), before("wo_ev") + TT + t + 1)
        N2 = Norm("n2", TT, lambda t: x1[:, t, :], W1, 0, lambda t, k: h2T[:, k, t * P:(t + 1) * P],
              lambda k: mod[:, 2 * KT + k:2 * KT + k + 1], lambda k: adaT[:, 3 * KT + k:3 * KT + k + 1], banks=lambda t: (4, 5), depth=1,
              stored=lambda eng, t: eng.wait_ge(S(f"xn_out{t % 2}"), 16 * (t // 2 + 1)))

        def n2_pe(pe, i):
            if 0 <= i - 2 < TT:
                N2.transposes(pe, i - 2)
            if 0 <= i - 3 < TT:
                t = i - 3
                N2.done(pe, t)
                group(pe, bank(6)[:, t * NEXP:(t + 1) * NEXP],
                      [(h2T[:, k, span(t)], wrt[:, k * NEXP:(k + 1) * NEXP]) for k in range(KT)]).then_inc(S("logits"), 1)

        def bias_ready(eng, name, g):
            att = ATT[name]
            i, nb = g // att.per_bias, len(BIAS[name])
            eng.wait_ge(S(name + f"_bias{i % nb}"), before(name + f"_bias{i % nb}") + 16 * (i // nb + 1))
            return BIAS[name][i % nb]

        XB = lambda eng, t: eng.wait_ge(S("xb"), t + 1)
        X3 = lambda eng, t: eng.wait_ge(S("wo0_ev"), before("wo0_ev") + TT + t + 1)
        N3 = Norm("n3", TT, lambda t: x1[:, t, :], XB, 8, lambda t, k: H2[0][:, k, t * P:(t + 1) * P],
              lambda k: gT[:, 2 * KT + k:2 * KT + k + 1], None, banks=lambda t: (6, 7), depth=1)
        N4 = Norm("n4", TT, lambda t: x3[:, t, :], X3, 0, lambda t, k: H2[1][:, k, t * P:(t + 1) * P],
              lambda k: gT[:, 3 * KT + k:3 * KT + k + 1], None, banks=lambda t: (4 + 2 * (t % 2), 5 + 2 * (t % 2)))

        @block.tensor
        def _(pe):
            def ada_pe(j):
                w = tile_ready(pe, ("ada", j))
                jobs_mm(pe, "ada", j, 2, bank(j % 2)[0:2, :], [(csil[:, 2 * k:2 * k + 2], w[:, k, :]) for k in range(KT)])

            def adaT_pe(first, last):
                for j in range(first, last):
                    mm = pe.transpose(bank(2)[:, 2 * j:2 * j + 2], adarow[:, j * P:(j + 1) * P], ident[0:2, 0:2])
                mm.then_inc(S("adaT_mm"), 1)

            pe.wait_ge(S("csil"), 1)
            for j in range(4):
                ada_pe(j)
            emptied(pe, "ada", 4)
            consts(pe)
            adaT_pe(0, 2 * KT)
            for j in range(4, 12):
                ada_pe(j)
                NX.transposes(pe, j - 4)
            emptied(pe, "ada", 12)
            pe.wait_ge(S("mod"), 1)
            adaT_pe(2 * KT, 48)
            NX.done(pe, TT - 1)
            NC.run_pe(pe)
            pe.wait_ge(S("mod"), 2)
            w = tile_ready(pe, "f")
            for t in range(TT):
                mm = jobs_mm(pe, "u", t, 4, bank(t % 4), [(hT[:, k, span(t)], w[:, k, :]) for k in range(KT)])
            emptied(pe, "u", 8)
            for part, key in enumerate(("cos", "sin")):
                w = tile_ready(pe, key)
                for c in range(4):
                    j = 4 * part + c
                    jobs_mm(pe, "dft", j, 4, bank(j % 4), [(u_sb[:, k, span(c)], w[:, k, :]) for k in range(KT)])
            for c in range(4):
                mm = group(pe, bank(6)[:, c:c + 1], [(u_sb[:, k, span(c)], dftc[:, 2 * P:2 * P + 1]) for k in range(KT)])
            mm.then_inc(S("mid_mm"), 1)
            emptied(pe, "dft", 8)
            for c in range(4):
                if c >= 2:
                    pe.wait_ge(S("fu_ev"), 2 * (c - 1))
                b = 2 * (c % 2)
                pe.matmul(bank(b), dftc[:, 0:P], pq[:, 0, c, :], start=True, stop=True)
                pe.matmul(bank(b + 1), dftc[:, P:2 * P], pq[:, 1, c, :], start=True, stop=True).then_inc(S("fu_mm"), 1)
            pe.wait_ge(S("mid"), 1)
            pe.matmul(bank(7)[:, 0:4], dftc[:, 0:P], middle, start=True, stop=True).then_inc(S("fu_mm"), 1)
            pe.wait_ge(S("fu_ev"), 9)
            for qk, key in enumerate("qk"):
                w = tile_ready(pe, key)
                for h in range(NH):
                    u = qk * NH + h
                    if u >= 2:
                        pe.wait_ge(S("qk_pad"), u - 1)
                    b = 3 * (u % 2)
                    for n in range(2):
                        mm = group(pe, bank(b + n), [(w[:, k, span(h)], hT[:, k, n * HALF:(n + 1) * HALF]) for k in range(KT)])
                    if qk:
                        mm = group(pe, bank(b + 2)[:, 0:CTX], [(w[:, k, span(h)], hcT[:, k, :]) for k in range(KT)])
                    mm.then_inc(S("qk_mm"), 1)
            pe.wait_ge(S("qk_pad"), 8)
            w = tile_ready(pe, "v")
            for c in range(NCH):
                if c == 2:
                    pe.wait_ge(S("qk_pad"), 8)
                    lw = lambda k: wgate[:, k * (FROW + NG):(k + 1) * (FROW + NG)]
                    group(pe, bank(0)[0:FROW + NG, 0:CTX], [(lw(k), hcT[:, k, :]) for k in range(KT)])
                    for n in range(2):
                        mm = group(pe, bank(1 + n)[0:FROW + NG, :], [(lw(k), hT[:, k, n * HALF:(n + 1) * HALF]) for k in range(KT)])
                    mm.then_inc(S("gate_mm"), 1)
                src = hcT[:, :, span(c)] if c < CT else hT[:, :, span(c - CT)]
                if c >= 2:
                    pe.wait_ge(S("v_ev"), c - 1)
                group(pe, bank(6 + c % 2), [(src[:, k, :], w[:, k, :]) for k in range(KT)]).then_inc(S("v_mm"), 1)
            pe.wait_ge(S("v_ev"), NCH)
            pe.wait_ge(S("rows"), 1)
            for c in range(NCH):
                if c >= 2:
                    pe.wait_ge(S("cols"), c - 1)
                for i, r in enumerate((rI, rF, rC, rM)):
                    mm = pe.transpose(bank(c % 2)[:, i * NG:(i + 1) * NG], r[:, span(c)], ident[0:NG, 0:NG])
                mm.then_inc(S("cols_mm"), 1)
            for d in range(2):
                for h in range(NH):
                    e = P - 1 if d == 0 else 0
                    mm = pe.matmul(bank(2)[:, (4 * d + h) * NCH:(4 * d + h + 1) * NCH],
                                   sel[:, (4 * d + h) * P:(4 * d + h + 1) * P], rC[:, e:TTOT:P], start=True, stop=True)
            mm.then_inc(S("dn_mm"), 1)
            pe.wait_ge(S("dn"), 1)
            pe.wait_ge(S("cols"), NCH)
            pe.wait_ge(S("c_zero"), 2)
            for i, (d, c, has) in enumerate(steps):
                no = outs_before[i]
                if has:
                    x0 = c - CT
                    if no >= 1:
                        pe.wait_ge(S("scan_se"), no)
                        pe.wait_ge(S("scan_e"), 4 * no)
                    for h in range(NH):
                        mm = pe.matmul(bank(0)[:, span(h)], ksrc(h, c), qT[:, h, span(x0)], start=True, stop=True)
                    mm.then_inc(S("scan_s"), 1)
                    pe.matmul(bank(1), identb[:], maskb[:, d * NH * P:(d + 1) * NH * P], start=True, stop=False, skip_group_check=True)
                    for h in range(NH):
                        mm = pe.matmul(bank(1)[:, span(h)], sel[:, (4 * d + h) * P:(4 * d + h + 1) * P], rR[:, span(c)],
                                       start=False, stop=(h == NH - 1), skip_group_check=True)
                    mm.then_inc(S("scan_r"), 1)
                if i >= 1:
                    pe.wait_ge(S("scan_c"), 4 * i)
                for h in range(NH):
                    mm = pe.transpose(bank(2)[:, span(h)], ksrc(h, c), ident[:])
                mm.then_inc(S("scan_kt"), 1)
                if has:
                    if no >= 1:
                        pe.wait_ge(S("scan_o"), 4 * no)
                    for h in range(NH):
                        mm = pe.matmul(bank(3 + h // 2)[:, (h % 2) * VW:(h % 2 + 1) * VW], qT[:, h, span(c - CT)],
                                       Cst[:, 4 * d + h, :], start=True, stop=True)
                    pe.wait_ge(S("scan_se"), no + 1)
                    for h in range(NH):
                        mm = pe.matmul(bank(5 + h // 2)[:, (h % 2) * VW:(h % 2 + 1) * VW], se[:, no % 2, h, :],
                                       vex[:, c, h, :], start=True, stop=True)
                    mm.then_inc(S("scan_u"), 1)
                pe.wait_ge(S("scan_kw"), 4 * (i + 1))
                for h in range(NH):
                    o = bank(7)[:, h * VW:(h + 1) * VW] if h < 3 else bank(2)[:, 0:VW]
                    mm = pe.matmul(o, kw[:, i % 2, h, :], vex[:, c, h, :], start=True, stop=True)
                mm.then_inc(S("scan_d"), 1)
            pe.wait_ge(S("scan_c"), 4 * len(steps))
            pe.wait_ge(S("scan_o"), 4 * 2 * TT)
            pe.wait_ge(S("scan_out"), 2 * TT)
            w = tile_ready(pe, "o")
            for j in range(8):
                h, n = j // 2, slice((j % 2) * HALF, (j % 2 + 1) * HALF)
                pe_w = [(w[:, k, span(h)], hT[:, k, n]) for k in range(KT)]
                if j >= 4:
                    pe.wait_ge(S("o_ev"), j - 3)
                mm = group(pe, bank(j % 4), pe_w)
                mm.then_inc(S("o_mm"), 1)
            for t in range(TT):
                if t >= 2:
                    pe.wait_ge(S("hm_ev"), t - 1)
                for h in range(NH):
                    mm = pe.transpose(bank(4 + t % 2)[:, span(h)], hsum[:, t, span(h)], ident[:])
                mm.then_inc(S("hm_mm"), 1)
            pe.wait_ge(S("hm_ev"), TT)
            pe.wait_ge(S("o_ev"), 8)
            pe.wait_ge(S("fu_in"), 16)
            j = 0
            for m in range(2):
                fm, b1, b2 = (tile_ready(pe, (n, m)) for n in ("fm", "br1", "br2"))
                for c in range(4):
                    for n in range(2):
                        b, ns = 4 * (j % 2), slice(n * HALF, (n + 1) * HALF)
                        if j >= 2:
                            pe.wait_ge(S("mg_sig"), 2 * (j - 1))
                            pe.wait_ge(S("mg_mul"), 2 * (j - 1))
                        group(pe, bank(b), [(b1[:, k, span(c)], hT[:, k, ns]) for k in range(KT)])
                        group(pe, bank(b + 1), [(b2[:, k, span(c)], hT[:, k, ns]) for k in range(KT)]).then_inc(S("mg_br"), 1)
                        group(pe, bank(b + 2), [(fm[:, k, span(c)], fuR[:, k, ns]) for k in range(4)])
                        mm = group(pe, bank(b + 3), [(fm[:, 4 + k, span(c)], hmT[:, k, ns]) for k in range(4)])
                        mm.then_inc(S("mg_y"), 1)
                        j += 1
            pe.wait_ge(S("mg_sig"), 32)
            pe.wait_ge(S("mg_mul"), 32)
            pe.wait_ge(S("mg_add"), 16)
            for m in range(2):
                w = tile_ready(pe, ("wo", m))
                for t in range(TT):
                    j = m * TT + t
                    if j >= 4:
                        pe.wait_ge(S("wo_ev"), before("wo_ev") + j - 3)
                    group(pe, bank(j % 4), [(mT[:, k, span(t)], w[:, k, :]) for k in range(KT)]).then_inc(S("wo_mm"), 1)
                    if m:
                        n2_pe(pe, t)
            for i in range(TT, TT + 3):
                n2_pe(pe, i)
            pe.wait_ge(S("aff"), 1)
            for t in range(TT):
                mm = pe.transpose(bank(1 + t // 4)[0:NEXP, (t % 4) * P:(t % 4 + 1) * P], aff[:, t, :], ident[:])
            mm.then_inc(S("affT"), 1)
            pe.wait_ge(S("topk"), 1)
            pe.transpose(bank(3)[:, 0:NEXP], vals, ident[0:NEXP, 0:NEXP])
            pe.transpose(bank(3)[:, NEXP:2 * NEXP], idxf, ident[0:NEXP, 0:NEXP]).then_inc(S("picked"), 1)
            pe.wait_ge(S("route"), 1)

            def expert_tile(pe, e, j):
                n = turn0 + j
                pe.wait_ge(S(f"ring_full{n % RING}"), e * 64 + 32 * (n // RING + 1) - 64)
                return ringv(n % RING)

            def x_transposes(e):
                pe.wait_ge(S("moe_gat"), e * 16 + 16)
                for h in range(2):
                    for k in range(4):
                        mm = pe.transpose(bank(6 + h)[:, span(k)], xg[:, span(4 * h + k)], ident[:])
                    mm.then_inc(S("moe_xtr"), 1)

            def h_transposes(e):
                pe.wait_ge(S("moe_hid"), e * 2 + 2)
                for h in range(2):
                    for k in range(4):
                        mm = pe.transpose(bank(6 + h)[:, span(k)], hid[:, span(4 * h + k)], ident[:])
                    mm.then_inc(S("moe_htr"), 1)

            def gate_up(e, tiles_of):
                pe.wait_ge(S("moe_xevA"), e + 1)
                pe.wait_ge(S("moe_xevD"), e + 1)
                for i in range(4):
                    w = tiles_of(i)
                    group(pe, bank(i), [(xsT[:, k, :], w[:, k, :]) for k in range(KT)]).then_inc(S(("moe_g", "moe_u")[i // 2]), 1)

            def down(e, tiles_of):
                pe.wait_ge(S("moe_hevA"), e + 1)
                pe.wait_ge(S("moe_hevD"), e + 1)
                for i in range(2):
                    w = tiles_of(i)
                    group(pe, bank(4 + i), [(hidT[:, k, :], w[:, k, :]) for k in range(KT)]).then_inc(S("moe_d"), 1)

            def turn(e, more):
                pe.wait_ge(S("moe_sil"), e * 2)
                pe.wait_ge(S("moe_hid"), e * 2)
                gate_up(e, lambda i: expert_tile(pe, e, i))
                if not isinstance(e, int) or e >= 2:
                    pe.wait_ge(S("moe_y"), e * 2 - 2)
                down(e - 1, lambda i: expert_tile(pe, e, 4 + i))
                if more:
                    x_transposes(e + 1)
                    pe.wait_ge(S("moe_xevA"), e + 2)
                    pe.wait_ge(S("moe_xevD"), e + 2)
                h_transposes(e)

            x_transposes(0)
            gate_up(0, lambda i: tile_ready(pe, (("gate", "up")[i // 2], 0, i % 2)))
            x_transposes(1)
            pe.wait_ge(S("moe_xevA"), 2)
            pe.wait_ge(S("moe_xevD"), 2)
            h_transposes(0)
            turn(1, True)
            with pe.Fori(2, NEXP - 1) as e:
                turn(e, True)
            turn(NEXP - 1, False)
            pe.wait_ge(S("moe_y"), 2 * NEXP - 2)
            down(NEXP - 1, lambda i: tile_ready(pe, ("down", NEXP - 1, i)))

            def qk_pe(*keys, then_v=None, norm=None):
                items = rows_of(keys)
                for i in range(len(items) + 1):
                    if i < len(items):
                        key, t = items[i]
                        wd = 256 if key == "ck" else HALF
                        if norm and i < TT:
                            if i + 1 < TT:
                                norm.transposes(pe, i + 1)
                        if i >= 3 and items[i - 3][0] == "ck":
                            pe.wait_ge(S("cv_ev"), items[i - 3][1] + 1)
                        s2.product(key, t, bank(i % 3)[:, 0:wd]).then_inc(S(key + "_z"), 1)
                    elif then_v:
                        v_job(then_v, 0)
                    if i >= 1:
                        key, u = items[i - 1]
                        pe.wait_ge(S(key + "_zn"), before(key + "_zn") + u + 1)
                        if i >= 3:
                            pkey, pu = items[i - 3]
                            pe.wait_ge(S(pkey + "_evA"), before(pkey + "_evA") + pu + 1)
                        for c in range(QK[key][2] // P):
                            mm = pe.transpose(bank(3 + (i - 1) % 2)[:, span(c)], zn[:, span(c)], ident[:])
                        mm.then_inc(S(key + "_tr"), 1)
                if then_v:
                    for t in range(1, TT):
                        v_job(then_v, t)
                    emptied(pe, then_v, TT)
                pe.wait_ge(S(key + "_evA"), before(key + "_evA") + TT)
                if key == "ck":
                    pe.wait_ge(S("cv_ev"), TT)

            def v_job(key, t):
                if t >= 2:
                    side = "_ev" + "AD"[t % 2]
                    pe.wait_ge(S(key + side), before(key + side) + t // 2)
                s2.product(key, t, bank(6 + t % 2)).then_inc(S(key + "_mm"), 1)

            def attn_pe(name):
                at = ATT[name]

                def scores(g):
                    for i, (c, h, b, qc, row, kc, k0, nk) in enumerate(at.groups[g]):
                        v = g * at.comps + i
                        if v >= 2:
                            pe.wait_ge(S(name + "_s"), before(name + "_s") + v - 1)
                        for m in range((nk + 3) // 4):
                            n = min(4, nk - 4 * m) * P
                            o = bank(2 * (v % 2) + m)[:, 0:n]
                            last = name == "B" and m == (nk - 1) // 4
                            mm = pe.matmul(o, qT2[row:row + HD, qc, span(b)], kT2[row:row + HD, kc, (k0 + 4 * m) * P:(k0 + 4 * m) * P + n],
                                           start=True, stop=not last, skip_group_check=last)
                            if last:
                                mm = pe.matmul(o[:, n - P:n], identb[:], maskb[:, NH * P:NH * P + P], start=False, stop=True,
                                               skip_group_check=True)
                        mm.then_inc(S(name + "_qk"), 1)

                def transposes(g):
                    nk, v = at.groups[g][0][7], g * at.comps
                    if name == "A":
                        pe.wait_ge(S("A_w"), before("A_w") + g + 1)
                    else:
                        pe.wait_ge(S(name + "_e"), before(name + "_e") + g + 1)
                    if g >= 1:
                        pe.wait_ge(S(name + "_wevA"), before(name + "_wevA") + g)
                        if at.big[g]:
                            pe.wait_ge(S(name + "_wevD"), before(name + "_wevD") + at.big[g])
                    sbuf = SBUFS[name][v % len(SBUFS[name])]
                    for i in range(nk):
                        mm = pe.transpose(bank(4 + i // 4)[:, span(i % 4)], sbuf[:, span(i)], ident[:])
                    mm.then_inc(S(name + "_tr"), 1)

                def outputs(g):
                    c, h, b, qc, row, kc, k0, nk = at.groups[g][0]
                    pe.wait_ge(S(name + "_wevA"), before(name + "_wevA") + g + 1)
                    if at.big[g + 1]:
                        pe.wait_ge(S(name + "_wevD"), before(name + "_wevD") + at.big[g + 1])
                    if g >= 1:
                        pe.wait_ge(S(name + "_o"), before(name + "_o") + g)
                    vc = {"A": c * P, "B": c * P + h * HD, "C": (2 * c + h) // 4 * HD, "D": c * P + h * HD}[name]
                    for i in range(nk):
                        mm = pe.matmul(bank(6)[:, 0:at.dv], wT[g % 2][:, i, :], v2[:, k0 + i, vc:vc + at.dv], start=(i == 0), stop=(i == nk - 1))
                    mm.then_inc(S(name + "_pv"), 1)

                def finish(c):
                    if name == "A":
                        pe.wait_ge(S("A_on"), before("A_on") + c + 1)
                    else:
                        pe.wait_ge(S(name + "_o"), before(name + "_o") + at.last[c] + 1)
                    for m in range(2):
                        if c or m:
                            pe.wait_ge(S(name + "_mix"), before(name + "_mix") + 2 * c + m)
                        for b in range(4):
                            mm = pe.transpose(bank(7)[:, span(b)], obuf[c % 2][:, 4 * m + b, :], ident[:])
                        mm.then_inc(S(name + "_otr"), 1)

                for i, (a, b, c, full, done) in enumerate(at.steps()):
                    if name != "A" and i == at.lag + 1:
                        for k in range(6):
                            pe.matmul(bank(7), H2[at.layer][:, k, 0:P], H2[at.layer][:, k, 0:HALF], start=(k == 0), stop=(k == 5))
                    if a is not None:
                        scores(a)
                    if b is not None:
                        transposes(b)
                    if c is not None:
                        outputs(c)
                    for chunk in done:
                        finish(chunk)
                pe.wait_ge(S(name + "_mix"), before(name + "_mix") + 8)

            def gates_pe(layer):
                g = f"g{layer}"
                for j in range(16):
                    n, key, c = j // 8, (("ag", "bg"), ("cg", "dg"))[layer][j // 4 % 2], j % 4
                    low = ringr(place[key] % RING)
                    if j >= 4:
                        pe.wait_ge(S(g + "_sg"), before(g + "_sg") + j - 3)
                    for k in range(KT):
                        if j % 8 == 0:
                            pe.wait_ge(S(g + "_l"), before(g + "_l") + KT * n + k + 1)
                        if j in (0, 4) and k % PK == 0:
                            pe.wait_ge(S("w_low"), PIECES * WSEQ.index(key) + k // PK + 1)
                        high = whigh(key, k)[:, span(c)]
                        pe.matmul(bank(j % 4), high, GHIGH[:, k, :], start=(k == 0), stop=False)
                        pe.matmul(bank(j % 4), high, GLOW[:, k, :], start=False, stop=False)
                        mm = pe.matmul(bank(j % 4), low[:, k, span(c)], GHIGH[:, k, :], start=False, stop=(k == KT - 1))
                    mm.then_inc(S(g + "_mm"), 1)
                pe.wait_ge(S(g + "_sg"), before(g + "_sg") + 16)

            def out_pe(layer):
                for m in range(2):
                    for t in range(TT):
                        j = m * TT + t
                        if j >= 4:
                            pe.wait_ge(S(f"wo{layer}_ev"), before(f"wo{layer}_ev") + j - 3)
                        s2.product(("out", layer, m), t, bank(j % 4)).then_inc(S(f"wo{layer}_mm"), 1)
                        if layer == 0 and m and t >= 2:
                            N4.transposes(pe, t - 2)
                if layer == 0:
                    N4.transposes(pe, TT - 2)
                    N4.transposes(pe, TT - 1)
                pe.wait_ge(S(f"wo{layer}_ev"), before(f"wo{layer}_ev") + 2 * TT)

            s2 = Split(pe)
            N3.transposes(pe, 0)
            qk_pe("aq", "ak", then_v="av", norm=N3)
            attn_pe("A")
            for n in range(2):
                mm = group(pe, bank(5 + n)[0:8, :], [(wbf[:, 8 * k:8 * k + 8], H2[0][:, k, n * HALF:(n + 1) * HALF]) for k in range(KT)])
            mm.then_inc(S("forget_mm"), 1)
            qk_pe("bq", "bk", then_v="bv")
            attn_pe("B")
            gates_pe(0)
            out_pe(0)
            N4.done(pe, TT - 1)
            qk_pe("cq", "ck")
            attn_pe("C")
            qk_pe("dq", "dk", then_v="dv")
            attn_pe("D")
            gates_pe(1)
            out_pe(1)

        @block.scalar
        def _(act):
            link = Chain(act, "act_own")
            act.dma_start(cT[:], a["cT"]).then_inc(S("c_in"), 16)
            act.wait_ge(S("c_in"), 16)
            act.activation(csil[:], cT[:], ACT.Silu).then_inc(S("csil"), 1)

            def ada_act(j):
                act.wait_ge(S("ada_mm"), j + 1)
                act.activation(adarow[:, j * HALF:(j + 1) * HALF], bank(j % 2)[0:2, :], ACT.Copy).then_inc(S("ada_evA"), 1)

            ada_act(0)
            ada_act(2)
            consts(act)
            for i in range(TT + 1):
                if i < TT:
                    NX.squares(act, i)
                    if i % 2 == 0:
                        ada_act(i + 4)
                if i == 0:
                    act.wait_ge(S("mod"), 1)
                else:
                    NX.evac_act(act, i - 1)
            NC.run_act(act)
            evac(act, "u", 8, lambda j: copy(act, u_sb[:, j, :], bank(j % 4)))
            evac(act, "dft", 8, lambda j: copy(act, pq[:, j // 4, j % 4, :], bank(j % 4)))
            for c in range(4):
                act.wait_ge(S("fu_mm"), c + 1)
                if c >= 2:
                    act.wait_ge(S("fu_ev"), 2 * (c - 1))
                act.activation(sinp[c % 2], bank(2 * (c % 2) + 1), ACT.Copy).then_inc(S("sinp"), 1)
            act.wait_ge(S("pad_zero"), 4)
            for u in range(9):
                if u < 8:
                    act.wait_ge(S("qk_mm"), u + 1)
                    if u >= 2:
                        act.wait_ge(S("qk_conv"), u - 1)
                    grid = pads[u % 2].rearrange("p (y x) -> p y x", x=PADW)
                    for n in range(2):
                        ins = act.activation(grid[:, 1 + 8 * n:9 + 8 * n, 1:1 + GRID_W],
                                             bank(3 * (u % 2) + n).rearrange("p (y x) -> p y x", x=GRID_W), ACT.Copy)
                    if u >= 4:
                        ins = act.activation(cpads[u % 2][:, 1:1 + CTX], bank(3 * (u % 2) + 2)[:, 0:CTX], ACT.Copy)
                    ins.then_inc(S("qk_pad"), 1)
                if u >= 1:
                    v = u - 1
                    act.wait_ge(S("qk_conv"), v + 1)
                    if v == 0:
                        act.wait_ge(S("fu_ev"), 9)
                    dst = (qT if v < 4 else kT)[:, v % 4, :]
                    ins = act.activation(dst, accs[v % 2], ACT.Silu)
                    if v >= 4:
                        ins = act.activation(kcT[:, v - 4, :], caccs[v % 2], ACT.Silu)
                    ins.then_inc(S("qk_silu"), 1)
            act.wait_ge(S("fu_out"), 16)
            def v_act(chunks):
                for c in chunks:
                    act.wait_ge(S("v_mm"), c + 1)
                    act.activation(vex[:, c, :, 0:DH], bank(6 + c % 2).rearrange("p (h n) -> p h n", h=NH), ACT.Copy).then_inc(S("v_ev"), 1)

            v_act(range(2))
            act.wait_ge(S("gate_mm"), 1)
            act.wait_ge(S("qk_silu"), 8)
            for i, r in enumerate((rI, rM)):
                rows = slice(FROW * i, FROW * i + NG)
                link(act.activation(r[:, 0:CTX], bank(0)[rows, 0:CTX], ACT.Identity, bias=bgate[0:NG, i:i + 1]))
                link(act.activation(r[:, CTX:TTOT], psum[rows, HALF:3 * HALF], ACT.Identity, bias=bgate[0:NG, i:i + 1]))
            link(act.activation(rC, rM, ACT.Abs))
            link(act.activation(rC, rC, ACT.Exp, scale=-1.0))
            act.activation(rC, rC, ACT.Ln, bias=onec[0:NG, 0:1]).then_inc(S("gates"), 1)
            v_act(range(2, NCH - 2))
            act.wait_ge(S("gate_rows"), 1)
            for c in range(NCH):
                act.activation(rF[:, span(c)], rI[:, span(c)], ACT.Exp, bias=stat[0:NG, 20 + c:21 + c])
                act.activation(rC[:, span(c)], rR[:, span(c)], ACT.Exp, bias=stat[0:NG, 40 + c:41 + c])
            act.activation(rM, rM, ACT.Exp, scale=-1.0).then_inc(S("rows"), 1)
            v_act(range(NCH - 2, NCH))
            act.wait_ge(S("c_zero"), 2)
            for i, (d, c, has) in enumerate(steps):
                no = outs_before[i]
                act.wait_ge(S("scan_kt"), i + 1)
                if i >= 2:
                    act.wait_ge(S("scan_d"), i - 1)
                for h in range(NH):
                    g = chain_row(d, h)
                    act.activation(kw[:, i % 2, h, :], bank(2)[:, span(h)], ACT.Copy,
                                   scale=colv[:, c, 1, g:g + 1]).then_inc(S("scan_kw"), 1)
                if has:
                    act.wait_ge(S("scan_r"), no + 1)
                    if no >= 2:
                        act.wait_ge(S("scan_se"), no - 1)
                    for h in range(NH):
                        g = chain_row(d, h)
                        act.activation(ee[:, no % 2, h, :], bank(1)[:, span(h)], ACT.Exp,
                                       bias=colv[:, c, 0, g:g + 1]).then_inc(S("scan_e"), 1)
            act.wait_ge(S("scan_out"), 2 * TT)
            for j in range(8):
                act.wait_ge(S("o_mm"), j + 1)
                act.activation(oT[:, j // 2, (j % 2) * HALF:(j % 2 + 1) * HALF], bank(j % 4), ACT.Sigmoid).then_inc(S("o_ev"), 1)
            for j in range(16):
                act.wait_ge(S("mg_br"), j + 1)
                if j >= 2:
                    act.wait_ge(S("mg_mul"), 2 * (j - 1))
                for i in range(2):
                    act.activation(sg[:, j % 2, i, :], bank(4 * (j % 2) + i), ACT.Sigmoid).then_inc(S("mg_sig"), 1)
            act.wait_ge(S("mg_add"), 16)
            act.wait_ge(S("lam_sum"), 2)
            act.activation(lsums, lsums, ACT.Exp).then_inc(S("lam_exp"), 1)
            for i in range(TT + 2):
                if i < TT:
                    N2.squares(act, i)
                if i >= 2:
                    N2.evac_act(act, i - 2)
            act.wait_ge(S("lmax"), 1)
            for t in range(TT):
                act.activation(aff[:, t, :], bank(6)[:, t * NEXP:(t + 1) * NEXP], ACT.Exp, bias=lmax[:, t:t + 1],
                               accum_out=lsum[:, t:t + 1]).then_inc(S("lexp"), 1)

            def x_evac(e):
                act.wait_ge(S("moe_xtr"), e * 2 + 1)
                for k in range(4):
                    ins = act.activation(xsT[:, k, :], bank(6)[:, span(k)], ACT.Identity, bias=adaT[:, 3 * KT + k:3 * KT + k + 1],
                                         scale=mod[:, 2 * KT + k:2 * KT + k + 1])
                ins.then_inc(S("moe_xevA"), 1)

            def silu_gate(e):
                for m in range(2):
                    act.wait_ge(S("moe_g"), e * 2 + m + 1)
                    act.activation(sgate[:, m * HALF:(m + 1) * HALF], bank(m), ACT.Silu).then_inc(S("moe_sil"), 1)

            def h_evac(e):
                act.wait_ge(S("moe_htr"), e * 2 + 1)
                act.activation(hd[:, 0:HALF], bank(6), ACT.Copy).then_inc(S("moe_hevA"), 1)

            x_evac(0)
            silu_gate(0)
            x_evac(1)
            h_evac(0)
            with act.Fori(1, NEXP - 1) as e:
                act.wait_ge(S("moe_hid"), e * 2)
                silu_gate(e)
                x_evac(e + 1)
                h_evac(e)
            act.wait_ge(S("moe_hid"), 2 * NEXP - 2)
            silu_gate(NEXP - 1)
            h_evac(NEXP - 1)

            def qk_act(*keys, then_v=None, norm=None, stats=None, aside=None):
                items = rows_of(keys)
                every = items + (rows_of([then_v]) if then_v else [])
                src = lambda t: H2[QK[keys[0]][0]][:, :, span(t)]
                for i in range(len(items) + 1):
                    if i < len(items):
                        key, t = items[i]
                        if norm and i + 1 < TT:
                            norm.evac_act(act, i + 1)
                            norm.done(act, i + 1)
                        next_job(s2, i, every, src)
                        if norm and i + 2 < TT:
                            stats(i + 2)
                        nc4 = QK[key][2]
                        q = 24 * (i % 2)
                        act.wait_ge(S(key + "_z"), before(key + "_z") + t + 1)
                        act.activation(sqz[:, 0:nc4], bank(i % 3)[:, 0:nc4], ACT.Square).then_inc(S(key + "_sq"), 1)
                        act.wait_ge(S(key + "_ss"), before(key + "_ss") + t + 1)
                        act.activation(qst[:, q + 8:q + 8 + nc4 // HD], qst[:, q:q + nc4 // HD], ACT.Sqrt,
                                       bias=epsc[:, 0:1], scale=1.0 / HD).then_inc(S(key + "_rt"), 1)
                    if i >= 1:
                        key, u = items[i - 1]
                        _, g, ncol, dst = QK[key]
                        act.wait_ge(S(key + "_tr"), before(key + "_tr") + u + 1)
                        act.activation(dst[:, 0:ncol // P, span(u)], bank(3 + (i - 1) % 2)[:, 0:ncol].rearrange("p (c n) -> p c n", c=ncol // P),
                                       ACT.Copy, scale=gcol[:, g:g + 1]).then_inc(S(key + "_evA"), 1)
                    if aside:
                        aside(i)
                if then_v:
                    for t in range(TT):
                        next_job(s2, len(items) + t, every, src)
                        if t % 2 == 0:
                            act.wait_ge(S(then_v + "_mm"), before(then_v + "_mm") + t + 1)
                            act.activation(v2[:, t, :], bank(6), ACT.Copy).then_inc(S(then_v + "_evA"), 1)

            def first_job(layer):
                s2.rows(H2[layer][:, :, span(0)])
                s2.weights()

            def attn_act(name):
                at = ATT[name]
                nbuf = len(SBUFS[name])

                def weights(g):
                    for i, (c, h, b, qc, row, kc, k0, nk) in enumerate(at.groups[g]):
                        v = g * at.comps + i
                        act.wait_ge(S(name + "_s"), before(name + "_s") + v + 1)
                        sv = SBUFS[name][v % nbuf][:, 0:nk * P]
                        act.activation(sv, sv, ACT.Exp, bias=nmx[:, v % 8:v % 8 + 1], scale=-1.0,
                                       accum_out=esum[:, v % 8:v % 8 + 1]).then_inc(S(name + "_e"), 1)
                        if name == "C":
                            hd_ = 2 * c + h
                            act.activation(esk[:, v % 8:v % 8 + 1], sinkb[:, hd_:hd_ + 1], ACT.Exp,
                                           bias=nmx[:, v % 8:v % 8 + 1]).then_inc(S("C_sink"), 1)

                def empty(g):
                    nk = at.groups[g][0][7]
                    act.wait_ge(S(name + "_tr"), before(name + "_tr") + g + 1)
                    n = min(4, nk)
                    act.activation(wT[g % 2][:, 0:n, :], bank(4)[:, 0:n * P].rearrange("p (k n) -> p k n", k=n), ACT.Copy).then_inc(S(name + "_wevA"), 1)

                def squares(c):
                    act.wait_ge(S("A_o"), before("A_o") + at.last[c] + 1)
                    for b in range(TT):
                        if c or b:
                            act.wait_ge(S("A_osq"), TT * c + b)
                        act.activation(xsq, obuf[c % 2][:, b, :], ACT.Square,
                                       accum_out=qst[:, b:b + 1]).then_inc(S("A_osq"), 1)
                    act.wait_ge(S("A_osq"), TT * (c + 1))
                    act.activation(qst[:, 8:16], qst[:, 0:8], ACT.Sqrt, bias=epsc[:, 0:1], scale=1.0 / (2 * HD)).then_inc(S("A_ort"), 1)

                def mix(c):
                    for m in range(2):
                        act.wait_ge(S(name + "_otr"), before(name + "_otr") + 2 * c + m + 1)
                        act.activation(M2[at.layer][:, at.mix0 + c, m * HALF:(m + 1) * HALF], bank(7), ACT.Copy,
                                       scale=(gcol[:, 13:14] if name == "A" else 1.0)).then_inc(S(name + "_mix"), 1)

                for a, b, c, full, done in at.steps():
                    if a is not None:
                        weights(a)
                    if b is not None:
                        empty(b)
                    for chunk in full:
                        if name == "A":
                            squares(chunk)
                    for chunk in done:
                        mix(chunk)

            def gates_act(layer):
                g = f"g{layer}"

                def tokens(n, k):
                    if n:
                        act.wait_ge(S(g + "_mm"), before(g + "_mm") + 8)
                    act.activation(GHIGH[:, k, :], H2[layer][:, k, n * HALF:(n + 1) * HALF], ACT.Copy).then_inc(S(g + "_h"), 1)

                for p in range(PIECES):
                    s2.piece(p)
                    for k in range(PK * p, PK * (p + 1)):
                        tokens(0, k)
                s2.weights()
                for j in range(16):
                    if j == 7:
                        for k in range(KT):
                            tokens(1, k)
                    if j == 14:
                        s2.weights()
                    act.wait_ge(S(g + "_mm"), before(g + "_mm") + j + 1)
                    if j >= 2:
                        act.wait_ge(S(g + "_mul"), before(g + "_mul") + j - 1)
                    act.activation(sgt[j % 2], bank(j % 4), ACT.Silu).then_inc(S(g + "_sg"), 1)
                act.wait_ge(S(g + "_mul"), before(g + "_mul") + 16)
                s2.rows(M2[layer][:, :, span(0)])

            def out_act(layer):
                items = rows_of([("out", layer, m) for m in range(2)])
                for i in range(2 * TT + (0 if layer else 2)):
                    if i < len(items):
                        next_job(s2, i, items, lambda t: M2[layer][:, :, span(t)])
                    i -= TT
                    if layer == 0 and 0 <= i < TT:
                        N4.squares(act, i)
                    if layer == 0 and i >= 2:
                        N4.evac_act(act, i - 2)
                if layer == 0:
                    N4.done(act, TT - 1)

            def stats(t):
                act.wait_ge(S(f"x2_in{t // 2}"), before(f"x2_in{t // 2}") + 16)
                if t:
                    act.wait_ge(S("n3_sq"), before("n3_sq") + t)
                act.activation(sq_buf, x1[:, t, :], ACT.Square, accum_out=stat[:, t:t + 1]).then_inc(S("nf_sq"), 1)
                act.wait_ge(S("nf_sq"), t + 1)
                act.activation(stat[:, 16 + t:17 + t], stat[:, t:t + 1], ACT.Sqrt, bias=epsc[:, 0:1], scale=1.0 / D).then_inc(S("nf_rt"), 1)
                N3.squares(act, t)

            s2 = Split(act)
            act.wait_ge(S("moe_y"), 2 * NEXP)
            s2.weights()
            stats(0)
            N3.evac_act(act, 0)
            N3.done(act, 0)
            s2.rows(H2[0][:, :, span(0)])
            stats(1)
            qk_act("aq", "ak", then_v="av", norm=N3, stats=stats)
            attn_act("A")

            def forget_act(i):
                if i == 0:
                    act.wait_ge(S("forget_mm"), 1)
                    link(act.activation(frow[0], psum[0:8, 5 * HALF:7 * HALF], ACT.Identity, bias=bbf[0:8, 0:1]))
                if i == 1:
                    link(act.activation(frow[1], frow[0], ACT.Abs))
                if i == 2:
                    link(act.activation(frow[1], frow[1], ACT.Exp, scale=-1.0))
                if i == 3:
                    act.activation(frow[1], frow[1], ACT.Ln, bias=onec[0:8, 0:1]).then_inc(S("forget_ln"), 1)
                if i == 2 * TT:
                    act.wait_ge(S("ncum_out"), 16)

            first_job(0)
            qk_act("bq", "bk", then_v="bv", aside=forget_act)
            attn_act("B")
            gates_act(0)
            out_act(0)
            first_job(1)
            qk_act("cq", "ck")
            attn_act("C")
            first_job(1)
            qk_act("dq", "dk", then_v="dv")
            attn_act("D")
            gates_act(1)
            out_act(1)

        @block.vector
        def _(dve):
            link = Chain(dve, "dve_own")
            def ada_dve(j):
                dve.wait_ge(S("ada_mm"), j + 1)
                dve.tensor_copy(adarow[:, j * HALF:(j + 1) * HALF], bank(j % 2)[0:2, :]).then_inc(S("ada_evD"), 1)

            def modulation(first, last, gains):
                av = bank(2)[:, 0:96].rearrange("p (c b) -> p c b", b=2)
                for b in range(2):
                    link(dve.tensor_tensor(adaT[:, b * 48 + first:b * 48 + last], av[:, first:last, b], badaT[:, first:last], ALU.add))
                for i, g, s in gains:
                    ins = dve.scalar_tensor_tensor(mod[:, i * KT:(i + 1) * KT], adaT[:, s:s + KT], 1.0,
                                                   gT[:, g * KT:(g + 1) * KT], ALU.add, ALU.mult)
                    if i != gains[-1][0]:
                        link(ins)
                ins.then_inc(S("mod"), 1)

            ada_dve(1)
            ada_dve(3)
            consts(dve)
            link(dve.tensor_copy(identb[:], ident[:]))
            link(dve.tensor_copy(maskb[:], mask_in))
            dve.wait_ge(S("adaT_mm"), 1)
            modulation(0, 2 * KT, ((0, 0, KT), (1, 0, 48 + KT)))
            for i in range(TT + 1):
                if i < TT:
                    NX.scale(dve, link, i)
                    if i % 2:
                        ada_dve(i + 4)
                if i:
                    NX.evac_dve(dve, i - 1)
            dve.wait_ge(S("adaT_mm"), 2)
            modulation(2 * KT, 48, ((2, 1, 4 * KT),))
            NC.run_dve(dve, link)
            evac(dve, "u", 8, lambda j: copy(dve, u_sb[:, j, :], bank(j % 4)))
            evac(dve, "dft", 8, lambda j: copy(dve, pq[:, j // 4, j % 4, :], bank(j % 4)))
            dve.wait_ge(S("mid_mm"), 1)
            dve.tensor_copy(middle, bank(6)[:, 0:4]).then_inc(S("mid"), 1)
            for c in range(4):
                cosp, half = bank(2 * (c % 2)), sinp[c % 2]
                dve.wait_ge(S("sinp"), c + 1)
                dve.tensor_tensor(fuT[:, c, 0:HALF], cosp, half, ALU.add).then_inc(S("fu_ev"), 1)
                dve.tensor_tensor(fuT[:, c, HALF + 1:D][:, ::-1], cosp[:, 1:HALF], half[:, 1:HALF], ALU.subtract).then_inc(S("fu_ev"), 1)
            dve.wait_ge(S("fu_mm"), 5)
            dve.tensor_copy(fuT[:, :, HALF], bank(7)[:, 0:4]).then_inc(S("fu_ev"), 1)
            emptied(dve, "dft", 8)
            for i in range(2):
                dve.memset(pads[i], 0.0).then_inc(S("pad_zero"), 1)
                dve.memset(cpads[i], 0.0).then_inc(S("pad_zero"), 1)
            for u in range(8):
                dve.wait_ge(S("qk_pad"), u + 1)
                if u >= 2:
                    dve.wait_ge(S("qk_silu"), u - 1)
                grid = pads[u % 2].rearrange("p (y x) -> p y x", x=PADW)
                acc = accs[u % 2].rearrange("p (y x) -> p y x", x=GRID_W)
                wc = lambda t: wconv[:, u * 9 + t:u * 9 + t + 1]
                tap = lambda t: grid[:, t // 3:t // 3 + GRID_H, t % 3:t % 3 + GRID_W]
                link(dve.tensor_scalar(acc, tap(0), wc(0), None, ALU.mult))
                if u >= 4:
                    ca, cp = caccs[u % 2], cpads[u % 2]
                    link(dve.tensor_scalar(ca, cp[:, 0:CTX], wc(3), None, ALU.mult))
                    for t in (4, 5):
                        link(dve.scalar_tensor_tensor(ca, cp[:, t - 3:t - 3 + CTX], wc(t), ca, ALU.mult, ALU.add))
                for t in range(1, 8):
                    link(dve.scalar_tensor_tensor(acc, tap(t), wc(t), acc, ALU.mult, ALU.add))
                dve.scalar_tensor_tensor(acc, tap(8), wc(8), acc, ALU.mult, ALU.add).then_inc(S("qk_conv"), 1)
            dve.wait_ge(S("fu_out"), 16)
            dve.memset(vex[:, :, :, DH:VW], 1.0).then_inc(S("v_one"), 1)
            link(dve.memset(ones_row, 1.0))
            dve.wait_ge(S("gates"), 1)
            link(dve.tensor_scalar(rM, rM, 0.0, None, ALU.min))
            link(dve.tensor_tensor(rF, rM, rC, ALU.subtract))
            for d in range(2):
                r = slice(0, NH) if d == 0 else slice(BWD, NG)
                sv = (lambda x: x) if d == 0 else (lambda x: x[:, ::-1])
                ends = (CTX - 1, TTOT - 1) if d == 0 else (0, CTX)
                if d == 0:
                    link(dve.memset(rM, 0.0))
                link(dve.tensor_tensor_scan(sv(rM[r, 0:CTX]), sv(rF[r, 0:CTX]), sv(rI[r, 0:CTX]), 0.0, ALU.add, ALU.max))
                link(dve.tensor_tensor_scan(sv(rM[r, CTX:TTOT]), sv(rF[r, CTX:TTOT]), sv(rI[r, CTX:TTOT]),
                                            rM[r, ends[0]:ends[0] + 1], ALU.add, ALU.max))
            link(dve.memset(rC, 0.0))
            for d in range(2):
                r = slice(0, NH) if d == 0 else slice(BWD, NG)
                sv = (lambda x: x) if d == 0 else (lambda x: x[:, ::-1])
                for c in range(NCH):
                    ins = dve.tensor_tensor_scan(sv(rC[r, span(c)]), sv(ones_row[r, :]), sv(rF[r, span(c)]), 0.0, ALU.mult, ALU.add)
                link(ins)
            link(dve.tensor_tensor(rI, rI, rC, ALU.subtract))
            link(dve.tensor_tensor(rR, rC, rM, ALU.subtract))
            link(dve.memset(stat[0:NG, 20:60], 0.0))
            for d in range(2):
                r = slice(0, NH) if d == 0 else slice(BWD, NG)
                e = P - 1 if d == 0 else 0
                link(dve.tensor_copy(stat[r, 20:20 + NCH], rR[r, e:TTOT:P]))
                if d == 0:
                    link(dve.tensor_copy(stat[r, 41:40 + NCH], rM[r, e:TTOT - P:P]))
                else:
                    link(dve.tensor_copy(stat[r, 40:41], rM[r, P:P + 1]))
                    link(dve.tensor_copy(stat[r, 42:42 + TT - 1], rM[r, CTX + P:TTOT:P]))
                    dve.tensor_copy(stat[r, 42 + TT - 1:42 + TT], rM[r, 0:1]).then_inc(S("gate_rows"), 1)
            for c in range(NCH):
                dve.wait_ge(S("cols_mm"), c + 1)
                dve.tensor_copy(colv[:, c, :, :], bank(c % 2)[:, 0:4 * NG].rearrange("p (a g) -> p a g", a=4)).then_inc(S("cols"), 1)
            dve.wait_ge(S("dn_mm"), 1)
            dve.tensor_copy(dnb, bank(2)[:, 0:8 * NCH].rearrange("p (c n) -> p c n", c=8)).then_inc(S("dn"), 1)
            dve.wait_ge(S("cols"), NCH)
            dve.memset(Cst, 0.0).then_inc(S("c_zero"), 1)
            dve.wait_ge(S("dn"), 1)
            dve.wait_ge(S("c_zero"), 1)
            dve.tensor_scalar(colv[:, :, 1, :], colv[:, :, 1, :], KSC, None, ALU.mult).then_inc(S("c_zero"), 1)
            dve.wait_ge(S("c_zero"), 2)
            for i, (d, c, has) in enumerate(steps):
                no = outs_before[i]
                if has:
                    dve.wait_ge(S("scan_s"), no + 1)
                    dve.wait_ge(S("scan_e"), 4 * (no + 1))
                    if no >= 2:
                        dve.wait_ge(S("scan_u"), no - 1)
                    dve.scalar_tensor_tensor(se[:, no % 2, :, :], bank(0).rearrange("p (h n) -> p h n", h=NH), KSC,
                                             ee[:, no % 2, :, :], ALU.mult, ALU.mult).then_inc(S("scan_se"), 1)
                    dve.wait_ge(S("scan_u"), no + 1)
                    for h in range(NH):
                        g = chain_row(d, h)
                        hs = slice((h % 2) * VW, (h % 2 + 1) * VW)
                        link(dve.tensor_scalar(ob[:, h, :], bank(3 + h // 2)[:, hs], colv[:, c, 2, g:g + 1], None, ALU.mult))
                        dve.tensor_tensor(ob[:, h, :], ob[:, h, :], bank(5 + h // 2)[:, hs], ALU.add).then_inc(S("scan_o"), 1)
                    dve.wait_ge(S("scan_o"), 4 * (no + 1))
                    g0 = chain_row(d, 0)
                    link(dve.scalar_tensor_tensor(rec, ob[:, :, DH], -1.0, colv[:, c, 3, g0:g0 + NH], ALU.mult, ALU.max))
                    link(dve.tensor_tensor(rec, rec, ob[:, :, DH], ALU.max))
                    link(dve.reciprocal(rec, rec))
                dve.wait_ge(S("scan_d"), i + 1)
                for h in range(NH):
                    o = bank(7)[:, h * VW:(h + 1) * VW] if h < 3 else bank(2)[:, 0:VW]
                    dve.scalar_tensor_tensor(Cst[:, 4 * d + h, :], Cst[:, 4 * d + h, :], dnb[:, 4 * d + h, c:c + 1], o,
                                             ALU.mult, ALU.add).then_inc(S("scan_c"), 1)
                if has:
                    hv = hsum[:, c - CT, :].rearrange("p (h n) -> p h n", h=NH)
                    first = not any(s[1] == c for s in steps[:i])
                    for h in range(NH):
                        if first:
                            ins = dve.tensor_scalar(hv[:, h, :], ob[:, h, 0:DH], rec[:, h:h + 1], None, ALU.mult)
                        else:
                            ins = dve.scalar_tensor_tensor(hv[:, h, :], ob[:, h, 0:DH], rec[:, h:h + 1], hv[:, h, :], ALU.mult, ALU.add)
                    ins.then_inc(S("scan_out"), 1)
                    dve.wait_ge(S("scan_out"), no + 1)
            dve.wait_ge(S("o_ev"), 8)
            for t in range(TT):
                dve.wait_ge(S("hm_mm"), t + 1)
                dve.tensor_tensor(hmT[:, :, span(t)], bank(4 + t % 2).rearrange("p (h n) -> p h n", h=NH), oT[:, :, span(t)],
                                  ALU.mult).then_inc(S("hm_ev"), 1)
            for j in range(16):
                dve.wait_ge(S("mg_sig"), 2 * (j + 1))
                dve.wait_ge(S("mg_y"), j + 1)
                for i in range(2):
                    dve.tensor_tensor(sgd[:, j % 2, i, :], sg[:, j % 2, i, :], bank(4 * (j % 2) + 2 + i), ALU.mult).then_inc(S("mg_mul"), 1)
                dve.wait_ge(S("mg_mul"), 2 * (j + 1))
                dve.tensor_tensor(mT[:, j // 2, (j % 2) * HALF:(j % 2 + 1) * HALF], sgd[:, j % 2, 0, :], sgd[:, j % 2, 1, :],
                                  ALU.add).then_inc(S("mg_add"), 1)
            dve.wait_ge(S("const2"), 16 * 6)
            for i in range(2):
                dve.tensor_tensor_reduce(out=lamx[:, i, :], in0=lamb[:, 2 * i, :], in1=lamb[:, 2 * i + 1, :], scale=1.0, scalar=0.0,
                                         op0=ALU.mult, op1=ALU.add, accum_out=lsums[:, i:i + 1]).then_inc(S("lam_sum"), 1)
            dve.wait_ge(S("lam_exp"), 1)
            link(dve.tensor_scalar(nlam, lsums[:, 1:2], lsums[:, 0:1], LAM0, ALU.subtract, ALU.subtract))
            link(dve.tensor_scalar(nsink, sinkb, -1.0, None, ALU.mult))
            for i in range(4):
                link(dve.tensor_scalar(gcol[:, 8 + i:9 + i], gcol[:, 2 * i:2 * i + 1], HD ** -0.5, None, ALU.mult))
            link(dve.tensor_scalar(gcol[:, 13:14], gcol[:, 12:13], 1.0 - LAM0, None, ALU.mult))
            dve.wait_ge(S("ga1"), 16)
            for j in range(2 * TT + 2):
                if j < 2 * TT:
                    m, t = j // TT, j % TT
                    ms, part = slice(m * HALF, (m + 1) * HALF), extra[:, (j % 2) * HALF:(j % 2 + 1) * HALF]
                    dve.wait_ge(S("wo_mm"), before("wo_mm") + j + 1)
                    if m == 0 and t % 2 == 0:
                        dve.wait_ge(S(f"x_again{t // 2}"), 16)
                    link(dve.tensor_tensor(part, bank(j % 4), ga1b[:, ms], ALU.mult))
                    dve.tensor_tensor(x1[:, t, ms], part, x1[:, t, ms], ALU.add).then_inc(S("wo_ev"), 1)
                i = j - TT
                if 1 <= i <= TT:
                    N2.scale(dve, link, i - 1)
                if 2 <= i:
                    N2.evac_dve(dve, i - 2)
            dve.wait_ge(S("logits"), TT)
            dve.tensor_reduce(lmax, bank(6)[:, 0:P].rearrange("p (t e) -> p t e", e=NEXP), AX.X, ALU.max, negate=True).then_inc(S("lmax"), 1)
            dve.wait_ge(S("lexp"), TT)
            link(dve.reciprocal(lmax, lsum))
            for t in range(TT):
                ins = dve.tensor_scalar(aff[:, t, :], aff[:, t, :], lmax[:, t:t + 1], None, ALU.mult)
            ins.then_inc(S("aff"), 1)
            dve.wait_ge(S("affT"), 1)
            link(dve.tensor_copy(affT, psum[0:NEXP, HALF:3 * HALF]))
            for r in range(CAP // 8):
                v = vals[:, 8 * r:8 * r + 8]
                link(dve.max(v, affT))
                link(dve.max_index(idx[:, 8 * r:8 * r + 8], v, affT))
                link(dve.match_replace(affT, v, affT, -1.0))
            dve.tensor_copy(idxf, idx).then_inc(S("topk"), 1)
            dve.wait_ge(S("picked"), 1)
            link(dve.tensor_copy(valc, bank(3)[:, 0:NEXP]))
            dve.tensor_copy(idxc, bank(3)[:, NEXP:2 * NEXP]).then_inc(S("route"), 1)
            dve.wait_ge(S("ga2"), 16)

            def x_evac(e):
                dve.wait_ge(S("moe_xtr"), e * 2 + 2)
                for k in range(4, 8):
                    ins = dve.tensor_scalar(xsT[:, k, :], bank(7)[:, span(k - 4)], mod[:, 2 * KT + k:2 * KT + k + 1],
                                            adaT[:, 3 * KT + k:3 * KT + k + 1], ALU.mult, ALU.add)
                ins.then_inc(S("moe_xevD"), 1)

            def hidden_of(e):
                for m in range(2):
                    ms = slice(m * HALF, (m + 1) * HALF)
                    dve.wait_ge(S("moe_sil"), e * 2 + m + 1)
                    dve.wait_ge(S("moe_u"), e * 2 + m + 1)
                    dve.tensor_tensor(hid[:, ms], sgate[:, ms], bank(2 + m), ALU.mult).then_inc(S("moe_hid"), 1)

            def h_evac(e):
                dve.wait_ge(S("moe_htr"), e * 2 + 2)
                dve.tensor_copy(hd[:, HALF:D], bank(7)).then_inc(S("moe_hevD"), 1)

            def outputs(e):
                for m in range(2):
                    ms = slice(m * HALF, (m + 1) * HALF)
                    dve.wait_ge(S("moe_d"), e * 2 + m + 1)
                    dve.scalar_tensor_tensor(yb[:, ms], bank(4 + m), valc[:, bass.ds(e, 1)], ga2b[:, ms],
                                             ALU.mult, ALU.mult).then_inc(S("moe_y"), 1)

            x_evac(0)
            hidden_of(0)
            x_evac(1)
            h_evac(0)

            def turn(e, more):
                dve.wait_ge(S("moe_htr"), e * 2)
                hidden_of(e)
                if not isinstance(e, int) or e >= 2:
                    dve.wait_ge(S("moe_sct"), e * 16 - 16)
                outputs(e - 1)
                if more:
                    x_evac(e + 1)
                h_evac(e)

            turn(1, True)
            with dve.Fori(2, NEXP - 1) as e:
                turn(e, True)
            turn(NEXP - 1, False)
            dve.wait_ge(S("moe_sct"), 16 * NEXP - 16)
            outputs(NEXP - 1)

            def qk_dve(*keys, then_v=None, norm=None, norms=None, aside=None):
                items = rows_of(keys)
                every = items + (rows_of([then_v]) if then_v else [])
                src = lambda t: H2[QK[keys[0]][0]][:, :, span(t)]
                for i, (key, t) in enumerate(items):
                    if norm and i + 1 < TT:
                        norm.evac_dve(dve, i + 1)
                        norm.done(dve, i + 1)
                    next_job(s2, i, every, src)
                    if norm and i + 2 < TT:
                        norms(i + 2)
                    ncol = QK[key][2]
                    nh, q = ncol // HD, 24 * (i % 2)
                    r = qst[:, q + 16:q + 16 + nh]
                    dve.wait_ge(S(key + "_sq"), before(key + "_sq") + t + 1)
                    dve.tensor_reduce(qst[:, q:q + nh], sqz[:, 0:ncol].rearrange("p (h d) -> p h d", d=HD),
                                      AX.X, ALU.add).then_inc(S(key + "_ss"), 1)
                    dve.wait_ge(S(key + "_rt"), before(key + "_rt") + t + 1)
                    link(dve.reciprocal(r, qst[:, q + 8:q + 8 + nh]))
                    if i:
                        pkey, pu = items[i - 1]
                        dve.wait_ge(S(pkey + "_tr"), before(pkey + "_tr") + pu + 1)
                    z, o = bank(i % 3)[:, 0:ncol], zn[:, 0:ncol]
                    if key == "cq":
                        for hh in range(2):
                            ins = dve.tensor_tensor(o.rearrange("p (c h d) -> p h c d", c=4, h=2)[:, hh],
                                                    z.rearrange("p (h c d) -> p h c d", h=2, c=4)[:, hh],
                                                    r[:, 4 * hh:4 * hh + 4].unsqueeze(2).to_broadcast([P, 4, HD]), ALU.mult)
                    else:
                        ins = dve.tensor_tensor(o.rearrange("p (h d) -> p h d", d=HD), z.rearrange("p (h d) -> p h d", d=HD),
                                                r.unsqueeze(2).to_broadcast([P, nh, HD]), ALU.mult)
                    ins.then_inc(S(key + "_zn"), 1)
                    if key == "ck":
                        dve.tensor_copy(v2[:, t, 0:P], bank(i % 3)[:, P:2 * P]).then_inc(S("cv_ev"), 1)
                    if aside:
                        aside(i)
                if then_v:
                    for t in range(TT):
                        next_job(s2, len(items) + t, every, src)
                        if t % 2:
                            dve.wait_ge(S(then_v + "_mm"), before(then_v + "_mm") + t + 1)
                            dve.tensor_copy(v2[:, t, :], bank(7)).then_inc(S(then_v + "_evD"), 1)

            def first_job(layer):
                s2.rows(H2[layer][:, :, span(0)])
                s2.weights()

            def attn_dve(name):
                at = ATT[name]
                nbuf = len(SBUFS[name])

                def scores(g):
                    bias = bias_ready(dve, name, g)
                    for i, (c, h, b, qc, row, kc, k0, nk) in enumerate(at.groups[g]):
                        v = g * at.comps + i
                        dve.wait_ge(S(name + "_qk"), before(name + "_qk") + v + 1)
                        if v >= nbuf:
                            dve.wait_ge(S(name + "_tr"), before(name + "_tr") + (v - nbuf) // at.comps + 1)
                        o = {"A": (TT - 1 - b) * P, "B": 0, "C": (2 - nk) * P, "D": 0}[name]
                        bv = bias[:, 0:nk * P][:, ::-1] if name == "D" else bias[:, o:o + nk * P]
                        init = nsink[:, 2 * c + h:2 * c + h + 1] if name == "C" else 3.0e38
                        dve.tensor_tensor_reduce(out=SBUFS[name][v % nbuf][:, 0:nk * P],
                                                 in0=psum[:, 2 * (v % 2) * HALF:2 * (v % 2) * HALF + nk * P],
                                                 in1=bv, scale=-1.0, scalar=init, op0=ALU.add, op1=ALU.min,
                                                 accum_out=nmx[:, v % 8:v % 8 + 1]).then_inc(S(name + "_s"), 1)

                def weights(g):
                    nk, v = at.groups[g][0][7], 2 * g
                    dve.wait_ge(S("A_e"), before("A_e") + v + 2)
                    link(dve.reciprocal(rinv[:, v % 8:v % 8 + 2], esum[:, v % 8:v % 8 + 2]))
                    e0, e1 = (SBUFS[name][(v + i) % nbuf][:, 0:nk * P] for i in range(2))
                    r1 = rinv[:, v % 8 + 1:v % 8 + 2]
                    link(dve.tensor_scalar(r1, r1, nlam, esum[:, v % 8:v % 8 + 1], ALU.mult, ALU.mult))
                    dve.scalar_tensor_tensor(e0, e1, r1, e0, ALU.mult, ALU.add).then_inc(S("A_w"), 1)

                def empty(g):
                    nk = at.groups[g][0][7]
                    if nk > 4:
                        dve.wait_ge(S(name + "_tr"), before(name + "_tr") + g + 1)
                        dve.tensor_copy(wT[g % 2][:, 4:nk, :], bank(5)[:, 0:(nk - 4) * P].rearrange("p (k n) -> p k n", n=P)).then_inc(S(name + "_wevD"), 1)

                def outputs(g):
                    c, h, b, qc, row, kc, k0, nk = at.groups[g][0]
                    r = g % 8
                    if name != "A":
                        dve.wait_ge(S(name + "_e"), before(name + "_e") + g + 1)
                        if name == "C":
                            dve.wait_ge(S("C_sink"), g + 1)
                            link(dve.tensor_tensor(esum[:, r:r + 1], esum[:, r:r + 1], esk[:, r:r + 1], ALU.add))
                        link(dve.reciprocal(rinv[:, r:r + 1], esum[:, r:r + 1]))
                    dve.wait_ge(S(name + "_pv"), before(name + "_pv") + g + 1)
                    if c >= 2:
                        dve.wait_ge(S(name + "_otr"), before(name + "_otr") + 2 * (c - 1))
                    if name == "A":
                        q = 2 * g % 8
                        ins = dve.tensor_scalar(obuf[c % 2][:, b, :], bank(6)[:, 0:P], rinv[:, q:q + 1], None, ALU.mult)
                    else:
                        ins = dve.tensor_scalar(obuf[c % 2][:, b, h * HD:(h + 1) * HD], bank(6)[:, 0:HD], rinv[:, r:r + 1], None, ALU.mult)
                    ins.then_inc(S(name + "_o"), 1)

                def complete(c):
                    dve.wait_ge(S("A_ort"), c + 1)
                    link(dve.reciprocal(qst[:, 16:24], qst[:, 8:16]))
                    for b in range(TT):
                        ins = dve.tensor_scalar(obuf[c % 2][:, b, :], obuf[c % 2][:, b, :], qst[:, 16 + b:17 + b], None, ALU.mult)
                    ins.then_inc(S("A_on"), 1)

                for a, b, c, full, done in at.steps():
                    if b is not None and name == "A":
                        weights(b)
                    if a is not None:
                        scores(a)
                    if b is not None:
                        empty(b)
                    if c is not None:
                        outputs(c)
                    if name == "A":
                        for chunk in full:
                            complete(chunk)

            def gates_dve(layer):
                g = f"g{layer}"

                def tokens(n, k):
                    if n:
                        dve.wait_ge(S(g + "_mm"), before(g + "_mm") + 8)
                    dve.wait_ge(S(g + "_h"), before(g + "_h") + KT * n + k + 1)
                    dve.tensor_tensor(GLOW[:, k, :], H2[layer][:, k, n * HALF:(n + 1) * HALF], GHIGH[:, k, :].bitcast(F32),
                                      ALU.subtract).then_inc(S(g + "_l"), 1)

                for p in range(PIECES):
                    s2.piece(p)
                    for k in range(PK * p, PK * (p + 1)):
                        tokens(0, k)
                s2.weights()
                for j in range(16):
                    if j == 7:
                        for k in range(KT):
                            tokens(1, k)
                    if j == 14:
                        s2.weights()
                    n = j // 8
                    dve.wait_ge(S(g + "_sg"), before(g + "_sg") + j + 1)
                    o = M2[layer][:, 4 * (j // 4 % 2) + j % 4, n * HALF:(n + 1) * HALF]
                    dve.tensor_tensor(o, o, sgt[j % 2], ALU.mult).then_inc(S(g + "_mul"), 1)
                dve.wait_ge(S(g + "_mul"), before(g + "_mul") + 16)
                s2.rows(M2[layer][:, :, span(0)])

            def out_dve(layer):
                items = rows_of([("out", layer, m) for m in range(2)])
                for j in range(2 * TT + (0 if layer else 2)):
                    m, t = j // TT, j % TT
                    if j < 2 * TT:
                        next_job(s2, j, items, lambda t: M2[layer][:, :, span(t)])
                        ms = slice(m * HALF, (m + 1) * HALF)
                        dve.wait_ge(S(f"wo{layer}_mm"), before(f"wo{layer}_mm") + j + 1)
                        if m == 0 and t % 2 == 0:
                            name = f"res{layer}_in{t // 2}"
                            dve.wait_ge(S(name), before(name) + 16)
                        dve.tensor_tensor(x3[:, t, ms], bank(j % 4), R2[layer][:, t, ms], ALU.add).then_inc(S(f"wo{layer}_ev"), 1)
                    i = j - TT
                    if layer == 0 and 1 <= i <= TT:
                        N4.scale(dve, link, i - 1)
                    if layer == 0 and 2 <= i:
                        N4.evac_dve(dve, i - 2)
                if layer == 0:
                    N4.done(dve, TT - 1)

            def norms(t):
                dve.wait_ge(S("nf_rt"), t + 1)
                link(dve.reciprocal(stat[:, 32 + t:33 + t], stat[:, 16 + t:17 + t]))
                dve.scalar_tensor_tensor(x1[:, t, :], x1[:, t, :], stat[:, 32 + t:33 + t], gfb, ALU.mult, ALU.mult).then_inc(S("xb"), 1)
                N3.scale(dve, link, t)

            dve.wait_ge(S("gf"), 16)
            s2 = Split(dve)
            s2.weights()
            norms(0)
            N3.evac_dve(dve, 0)
            N3.done(dve, 0)
            s2.rows(H2[0][:, :, span(0)])
            norms(1)
            qk_dve("aq", "ak", then_v="av", norm=N3, norms=norms)
            dve.wait_ge(S("res0_out"), before("res0_out") + 16)
            attn_dve("A")

            def forget_dve(i):
                if i == 4:
                    dve.wait_ge(S("forget_ln"), 1)
                    link(dve.tensor_scalar(frow[0], frow[0], 0.0, None, ALU.min))
                if i == 5:
                    link(dve.tensor_tensor(frow[1], frow[1], frow[0], ALU.subtract))
                if i == 6:
                    link(dve.memset(frow[2], 1.0))
                if i == 7:
                    dve.tensor_tensor_scan(frow[0], frow[2], frow[1], 0.0, ALU.mult, ALU.add).then_inc(S("forget"), 1)
                if i == 2 * TT - 1:
                    dve.wait_ge(S("ncum_out"), 16)

            first_job(0)
            qk_dve("bq", "bk", then_v="bv", aside=forget_dve)
            attn_dve("B")
            gates_dve(0)
            out_dve(0)
            dve.wait_ge(S("res1_out"), before("res1_out") + 16)
            first_job(1)
            qk_dve("cq", "ck")
            attn_dve("C")
            first_job(1)
            qk_dve("dq", "dk", then_v="dv")
            attn_dve("D")
            gates_dve(1)
            out_dve(1)
    return


SCRATCH = {"fu": (P, 4, D), "ada": (6 * D,), "acc": (SEQ, D), "xn": (SEQ, D), "xb": (SEQ, D), "x3": (SEQ, D), "ncum": (8, SEQ)}


def host_layout(i):
    n = np.arange(SEQ)
    ang = 2 * np.pi * ((n[:, None] * n[None, :]) % SEQ) / SEQ
    norm = 1.0 / math.sqrt(SEQ * P)
    m = np.arange(P)
    angc = 2 * np.pi * ((m[:, None] * m[None, :]) % P) / P
    w_in = i["w_in"][0]
    colT = lambda v: np.ascontiguousarray(v.reshape(-1, P).T)
    g = w_in[:, 2560:2576].reshape(D, 4, NH)
    wg = np.zeros((D, FROW + NG), np.float32)
    bg = np.zeros((NG, 2), np.float32)
    for k in range(2):
        wg[:, FROW * k:FROW * k + NH], wg[:, FROW * k + BWD:FROW * k + NG] = g[:, k], g[:, 2 + k]
        bg[0:NH, k], bg[BWD:NG, k] = i["b_gates"][0, k], i["b_gates"][0, 2 + k]
    sel = np.zeros((NG, 8, P), np.float32)
    for c in range(8):
        sel[c if c < NH else BWD + c - NH, c] = 1
    lower, upper = m[:, None] <= m[None, :], m[:, None] >= m[None, :]
    masks = np.stack([np.where(q, 0, NEG) for q in (lower, upper)])
    col = np.arange(SEQ)
    dist = np.abs(m[:, None] - (col[None, :] - (SEQ - P)))
    hide = (col[None, :] - (SEQ - P)) // HD > m[:, None] // HD
    slope = lambda n: 2.0 ** (-8.0 * np.arange(1, n + 1) / n)
    strip_a = np.stack([np.where(hide, NEG, -q * dist) for q in slope(4)]).astype(np.float32)
    col = np.arange(2 * P)
    dist = np.abs(m[:, None] - (col[None, :] - P))
    step = m[:, None] // HD + 2 - col[None, :] // HD
    strip_c = np.stack([np.where((step < 0) | (step > 2), NEG, -q * dist) for q in slope(8)]).astype(np.float32)
    rel = np.ascontiguousarray(np.pad(i["d_rel_bias_2"][0], ((0, 0), (64, 384)), mode="edge"))
    return {
        "x": i["x"][0], "ctx": i["ctx"][0], "w_ada": i["w_ada"][0], "w_in": w_in,
        "w_fourier": i["w_fourier"][0], "w_mlstm": i["w_mlstm"][0], "w_out": i["w_out"][0],
        "cT": np.ascontiguousarray(np.stack([i["c"][0], i["c_ctx"]]).reshape(2, KT, P).transpose(2, 1, 0)).reshape(P, -1),
        "b_adaT": colT(i["b_ada"][0]),
        "gT": np.concatenate([colT(v) for v in (i["g_norm1"][0], i["g_norm2"][0], i["even_ln_g_2"][0],
                                                i["odd_ln_g_2"][0], i["g_final"])], 1),
        "w_convT": np.ascontiguousarray(i["w_conv"][0].reshape(9, 8, P).transpose(2, 1, 0)).reshape(P, -1),
        "w_mgate": np.ascontiguousarray(wg.reshape(KT, P, -1).transpose(1, 0, 2)).reshape(P, -1),
        "w_routerT": np.ascontiguousarray(i["w_router"][0].reshape(KT, P, NEXP).transpose(1, 0, 2)).reshape(P, -1),
        "w_gate": i["w_gate_e"][0], "w_up": i["w_up_e"][0], "w_down": i["w_down_e"][0], "g_final": i["g_final"],
        "even_w_in": i["even_w_in_2"][0], "even_w_out": i["even_w_out_2"][0],
        "odd_w_in": i["odd_w_in_2"][0], "odd_w_out": i["odd_w_out_2"][0],
        "lams": np.concatenate([i[f"a_lambda_{n}_2"][0] for n in ("q1", "k1", "q2", "k2")]),
        "sinks": i["c_sinks_2"][0],
        "qk_gains": np.stack([np.tile(i[f"{n}_norm_g_2"][0], 2) for n in ("a_q", "a_k", "b_q", "b_k", "c_q", "c_k", "d_q", "d_k")], 1),
        "sub_gain": i["a_subln_g_2"][0].reshape(P, 1),
        "w_forget": np.ascontiguousarray(i["even_w_in_2"][0][:, 4096:4104].reshape(KT, P, 8).transpose(1, 0, 2)).reshape(P, -1),
        "b_forget": i["b_forget_bias_2"][0].reshape(8, 1),
        "strip_a": strip_a, "strip_c": strip_c, "rel": rel,
        "b_gate": bg, "sel": sel.reshape(NG, -1),
        "ident": np.eye(P, dtype=np.float32),
        "masks": np.concatenate([np.tile(q, (1, NH)) for q in masks], 1).astype(np.float32),
        "dftc": np.concatenate([np.cos(angc), -np.sin(angc), norm * (1.0 - 2.0 * (m[:, None] % 2))], 1).astype(np.float32),
        "dft_cos": (np.cos(ang) * norm)[:, 0:HALF].astype(np.float32), "dft_sin": (np.sin(ang) * norm)[:, 0:HALF].astype(np.float32),
    }


def kernel(**inputs):
    import concourse.bacc as bacc
    from concourse.bass_utils import run_bass_kernel_spmd

    arrays = host_layout({n: np.asarray(v) for n, v in inputs.items()})
    nc = bacc.Bacc("TRN2", target_bir_lowering=False, num_devices=1)
    a = {n: nc.dram_tensor("in_" + n, v.shape, mybir.dt.from_np(v.dtype), kind="ExternalInput").ap() for n, v in arrays.items()}
    out = nc.dram_tensor("out", (SEQ, D), F32, kind="ExternalOutput").ap()
    scratch = {n: nc.dram_tensor("scratch_" + n, v, F32, kind="Internal").ap() for n, v in SCRATCH.items()}
    build(nc, a, out, scratch)
    r = run_bass_kernel_spmd(nc, [{"in_" + n: v for n, v in arrays.items()}], core_ids=[0])
    return r.results[0]["out"].reshape(1, SEQ, D)
```
